# Optimizing a Trainium2 kernel written in Bass

```python
import jax, jax.numpy as jnp
from jax import lax
import numpy as np

D_MODEL = 1024
BATCH = 1
SEQ = 256
DEPTH = 1
DEC_BATCH = 8
DEC_SEQ = 8
PAST_LEN = 1024
PAGE_SIZE = 128

D_HEAD = 64
MOBA_HEADS = 8
MOBA_BLOCK = 256
MOBA_TOPK = 3
NSA_HEADS = 8
NSA_KV_HEADS = 2
NSA_GROUP = NSA_HEADS // NSA_KV_HEADS
CMP_LEN = 32
CMP_STRIDE = 16
CMP_HIDDEN = 128
SLC_BLOCK = 64
SLC_TOPN = 16
WINDOW = 512
N_GROUPS = 4
EXPERTS_PER_GROUP = 8
N_EXPERTS = N_GROUPS * EXPERTS_PER_GROUP
D_EXPERT = 256
TOPK_IN_GROUP = 2
ROPE_THETA = 10000.0
EPS = 1e-6
Q_CHUNK = 128
TOKEN_BLOCK = 1024
NEG_INF = -1e30
BIG = 1e30
TINY = 1e-30
MOBA_WIDTH = MOBA_HEADS * D_HEAD
NSA_WIDTH = NSA_HEADS * D_HEAD
NSA_KV_WIDTH = NSA_KV_HEADS * D_HEAD
IN_SIZES = (MOBA_WIDTH,) * 3 + (NSA_WIDTH,) + (NSA_KV_WIDTH,) * 6 + (3 * NSA_HEADS, 2 * D_MODEL)
IN_COLS = sum(IN_SIZES)

kernel_name = 'hybrid_moba_nsa_hmoe_decode_step'

def rms_norm(x, g):
    xf = x.astype(jnp.float32)
    y = xf * lax.rsqrt(jnp.mean(xf * xf, axis=-1, keepdims=True) + EPS)
    return (y * g.astype(jnp.float32)).astype(x.dtype)

def modulate(h, shift, scale):
    return h * (1.0 + scale[:, None, :]) + shift[:, None, :]

def rope(x, pos):
    half = D_HEAD // 2
    inv = ROPE_THETA ** (-jnp.arange(half, dtype=jnp.float32) / half)
    ang = pos.astype(jnp.float32)[:, None] * inv[None, :]
    cos = jnp.cos(ang)[None, :, None, :]
    sin = jnp.sin(ang)[None, :, None, :]
    xf = x.astype(jnp.float32)
    x1, x2 = xf[..., :half], xf[..., half:]
    return jnp.concatenate([x1 * cos - x2 * sin, x2 * cos + x1 * sin], axis=-1).astype(x.dtype)

def masked_softmax(s, mask):
    s = jnp.where(mask, s, NEG_INF)
    m = jnp.max(s, axis=-1, keepdims=True)
    p = jnp.where(mask, jnp.exp(s - m), 0.0)
    return p / jnp.maximum(jnp.sum(p, axis=-1, keepdims=True), TINY)

def map_query_chunks(fn, q, pos):
    B, T = q.shape[0], q.shape[1]
    if T <= Q_CHUNK or T % Q_CHUNK != 0:
        return fn(q, pos)
    n = T // Q_CHUNK
    qs = jnp.swapaxes(q.reshape((B, n, Q_CHUNK) + q.shape[2:]), 0, 1)
    out = lax.map(lambda a: fn(a[0], a[1]), (qs, pos.reshape(n, Q_CHUNK)))
    return jnp.swapaxes(out, 0, 1).reshape((B, T) + out.shape[3:])

def pad_to_blocks(x, blk):
    L = x.shape[1]
    n = -(-L // blk)
    x = jnp.pad(x, ((0, 0), (0, n * blk - L)) + ((0, 0),) * (x.ndim - 2))
    return x.reshape((x.shape[0], n, blk) + x.shape[2:]), n

def gather_pages(cache, page_table):
    pages = cache[page_table]
    return pages.reshape((pages.shape[0], pages.shape[1] * pages.shape[2]) + pages.shape[3:])

def moba_attention(q, k, v, q_pos):
    B = k.shape[0]
    kb, nblk = pad_to_blocks(k, MOBA_BLOCK)
    vb, _ = pad_to_blocks(v, MOBA_BLOCK)
    kb = kb.transpose(0, 3, 1, 2, 4)
    vb = vb.transpose(0, 3, 1, 2, 4)
    k_mean = jnp.mean(kb.astype(jnp.float32), axis=3)
    n_sel = min(MOBA_TOPK, nblk)
    b_ix = jnp.arange(B)[:, None, None, None]
    h_ix = jnp.arange(MOBA_HEADS)[None, :, None, None]
    blk_ids = jnp.arange(nblk)
    offs = jnp.arange(MOBA_BLOCK)
    scale = D_HEAD ** -0.5

    def chunk(qc, pc):
        C = qc.shape[1]
        q_blk = pc // MOBA_BLOCK
        gate = jnp.einsum('bchd,bhnd->bhcn', qc.astype(jnp.float32), k_mean)
        past = blk_ids[None, :] < q_blk[:, None]
        _, top_i = lax.top_k(jnp.where(past, gate, NEG_INF), n_sel)
        own = jnp.broadcast_to(q_blk[:, None], (B, MOBA_HEADS, C, 1)).astype(top_i.dtype)
        idx = jnp.concatenate([top_i, own], axis=-1)
        valid = jnp.concatenate([top_i < q_blk[:, None], jnp.ones(own.shape, dtype=bool)], axis=-1)
        kg = kb[b_ix, h_ix, idx]
        vg = vb[b_ix, h_ix, idx]
        k_pos = idx[..., None] * MOBA_BLOCK + offs
        mask = valid[..., None] & (k_pos <= pc[:, None, None])
        s = jnp.einsum('bchd,bhcskd->bhcsk', qc, kg).astype(jnp.float32) * scale
        p = masked_softmax(s.reshape(B, MOBA_HEADS, C, -1), mask.reshape(B, MOBA_HEADS, C, -1))
        o = jnp.einsum('bhcsk,bhcskd->bchd', p.reshape(s.shape).astype(vg.dtype), vg)
        return o.astype(qc.dtype)

    return map_query_chunks(chunk, q, q_pos)

def compress(k, pe, w1, w2):
    B, L = k.shape[0], k.shape[1]
    nc = (L - CMP_LEN) // CMP_STRIDE + 1
    idx = jnp.arange(nc)[:, None] * CMP_STRIDE + jnp.arange(CMP_LEN)[None, :]
    blocks = k[:, idx] + pe[None, None, :, None, :]
    flat = blocks.transpose(0, 1, 3, 2, 4).reshape(B, nc, NSA_KV_HEADS, CMP_LEN * D_HEAD)
    return jax.nn.gelu(flat @ w1) @ w2

def nsa_attention(q, kc, vc, ks, vs, kw, vw, wp0, q_pos, pe_k, wk1, wk2, pe_v, wv1, wv2):
    B = kc.shape[0]
    k_cmp = compress(kc, pe_k, wk1, wk2)
    v_cmp = compress(vc, pe_v, wv1, wv2)
    nc = k_cmp.shape[1]
    cmp_start = jnp.arange(nc) * CMP_STRIDE
    cmp_end = cmp_start + CMP_LEN - 1
    ksb, nslc = pad_to_blocks(ks, SLC_BLOCK)
    vsb, _ = pad_to_blocks(vs, SLC_BLOCK)
    ksb = ksb.transpose(0, 3, 1, 2, 4)
    vsb = vsb.transpose(0, 3, 1, 2, 4)
    slc_start = jnp.arange(nslc) * SLC_BLOCK
    overlap = ((cmp_start[:, None] < slc_start[None, :] + SLC_BLOCK)
               & (cmp_start[:, None] + CMP_LEN > slc_start[None, :])).astype(jnp.float32)
    n_top = min(SLC_TOPN, nslc)
    kw_pad = jnp.pad(kw, ((0, 0), (WINDOW, 0), (0, 0), (0, 0)))
    vw_pad = jnp.pad(vw, ((0, 0), (WINDOW, 0), (0, 0), (0, 0)))
    b_ix = jnp.arange(B)[:, None, None, None]
    g_ix = jnp.arange(NSA_KV_HEADS)[None, :, None, None]
    offs = jnp.arange(SLC_BLOCK)
    scale = D_HEAD ** -0.5

    def chunk(qc, pc):
        C = qc.shape[1]
        qg = qc.reshape(B, C, NSA_KV_HEADS, NSA_GROUP, D_HEAD)
        s_c = jnp.einsum('bcgrd,bngd->bgrcn', qg, k_cmp).astype(jnp.float32) * scale
        p_c = masked_softmax(s_c, cmp_end[None, :] <= pc[:, None])
        o_c = jnp.einsum('bgrcn,bngd->bcgrd', p_c.astype(v_cmp.dtype), v_cmp)
        imp = jnp.einsum('bgrcn,nj->bgcj', p_c, overlap)
        q_blk = pc // SLC_BLOCK
        j = jnp.arange(nslc)[None, :]
        imp = jnp.where(j == q_blk[:, None], BIG, jnp.where(j < q_blk[:, None], imp, NEG_INF))
        _, top_i = lax.top_k(imp, n_top)
        kg = ksb[b_ix, g_ix, top_i]
        vg = vsb[b_ix, g_ix, top_i]
        k_pos = top_i[..., None] * SLC_BLOCK + offs
        mask_s = (top_i <= q_blk[:, None])[..., None] & (k_pos <= pc[:, None, None])
        s_s = jnp.einsum('bcgrd,bgcskd->bgrcsk', qg, kg).astype(jnp.float32) * scale
        p_s = masked_softmax(s_s.reshape(B, NSA_KV_HEADS, NSA_GROUP, C, -1),
                             mask_s.reshape(B, NSA_KV_HEADS, 1, C, -1)).reshape(s_s.shape)
        o_s = jnp.einsum('bgrcsk,bgcskd->bcgrd', p_s.astype(vg.dtype), vg)
        start = pc[0] - wp0
        kwc = lax.dynamic_slice_in_dim(kw_pad, start, WINDOW + C, axis=1)
        vwc = lax.dynamic_slice_in_dim(vw_pad, start, WINDOW + C, axis=1)
        w_pos = pc[0] - WINDOW + jnp.arange(WINDOW + C)
        dist = pc[:, None] - w_pos[None, :]
        mask_w = (dist >= 0) & (dist <= WINDOW) & (w_pos >= wp0)[None, :]
        s_w = jnp.einsum('bcgrd,bkgd->bgrck', qg, kwc).astype(jnp.float32) * scale
        p_w = masked_softmax(s_w, mask_w)
        o_w = jnp.einsum('bgrck,bkgd->bcgrd', p_w.astype(vwc.dtype), vwc)
        o = jnp.stack([o_c, o_s, o_w], axis=-2)
        return o.reshape(B, C, NSA_HEADS, 3, D_HEAD).astype(qc.dtype)

    return map_query_chunks(chunk, q, q_pos)

def hmoe(h, w_grp, w_exp, w_ein, w_eout):
    B, T, D = h.shape
    N = B * T

    def route_mix(t):
        p_grp = jax.nn.softmax((t @ w_grp).astype(jnp.float32), axis=-1)
        g_sel = jnp.argmax(p_grp, axis=-1)
        g_w = jnp.max(p_grp, axis=-1)
        le = (t @ w_exp).astype(jnp.float32).reshape(-1, N_GROUPS, EXPERTS_PER_GROUP)
        le_g = jnp.take_along_axis(le, g_sel[:, None, None], axis=1)[:, 0]
        top_v, top_i = lax.top_k(jax.nn.softmax(le_g, axis=-1), TOPK_IN_GROUP)
        top_v = top_v / jnp.sum(top_v, axis=-1, keepdims=True)
        within = jnp.sum(jax.nn.one_hot(top_i, EXPERTS_PER_GROUP, dtype=jnp.float32) * top_v[..., None], axis=1)
        combine = (g_w[:, None, None] * jax.nn.one_hot(g_sel, N_GROUPS, dtype=jnp.float32)[:, :, None]
                   * within[:, None, :]).reshape(-1, N_EXPERTS)
        hid = jnp.einsum('nd,edf->nef', t, w_ein)
        a, b = jnp.split(hid, 2, axis=-1)
        act = jax.nn.silu(a) * b * combine[..., None].astype(hid.dtype)
        return jnp.einsum('nef,efd->nd', act, w_eout)

    t = h.reshape(N, D)
    if N > TOKEN_BLOCK and N % TOKEN_BLOCK == 0:
        out = lax.map(route_mix, t.reshape(N // TOKEN_BLOCK, TOKEN_BLOCK, D)).reshape(N, D)
    else:
        out = route_mix(t)
    return out.reshape(B, T, D).astype(h.dtype)

def split_cols(proj):
    parts = []
    off = 0
    for n in IN_SIZES:
        parts.append(proj[..., off:off + n])
        off += n
    return parts

def layer(x, c, pos, past, lw):
    B, T = x.shape[0], x.shape[1]
    mod = jax.nn.silu(c) @ lw['w_ada'] + lw['b_ada']
    sh1, sc1, g1, sh2, sc2, g2 = jnp.split(mod, 6, axis=-1)
    h = modulate(rms_norm(x, lw['norm_mix_g']), sh1, sc1)
    a_q, a_k, a_v, b_q, b_kc, b_vc, b_ks, b_vs, b_kw, b_vw, b_gate, merge = split_cols(h @ lw['w_in'])
    a_q = rope(a_q.reshape(B, T, MOBA_HEADS, D_HEAD), pos)
    a_k = rope(a_k.reshape(B, T, MOBA_HEADS, D_HEAD), pos)
    a_v = a_v.reshape(B, T, MOBA_HEADS, D_HEAD)
    b_q = rope(b_q.reshape(B, T, NSA_HEADS, D_HEAD), pos)
    b_kc = rope(b_kc.reshape(B, T, NSA_KV_HEADS, D_HEAD), pos)
    b_vc = b_vc.reshape(B, T, NSA_KV_HEADS, D_HEAD)
    b_ks = rope(b_ks.reshape(B, T, NSA_KV_HEADS, D_HEAD), pos)
    b_vs = b_vs.reshape(B, T, NSA_KV_HEADS, D_HEAD)
    b_kw = rope(b_kw.reshape(B, T, NSA_KV_HEADS, D_HEAD), pos)
    b_vw = b_vw.reshape(B, T, NSA_KV_HEADS, D_HEAD)
    wb = min(WINDOW, PAST_LEN)
    if past is None:
        k_a, v_a, k_c, v_c, k_s, v_s = a_k, a_v, b_kc, b_vc, b_ks, b_vs
        k_w, v_w, wp0 = b_kw, b_vw, 0
    else:
        pk_a, pv_a, pk_c, pv_c, pk_s, pv_s, buf_k, buf_v = past
        k_a = jnp.concatenate([pk_a, a_k], axis=1)
        v_a = jnp.concatenate([pv_a, a_v], axis=1)
        k_c = jnp.concatenate([pk_c, b_kc], axis=1)
        v_c = jnp.concatenate([pv_c, b_vc], axis=1)
        k_s = jnp.concatenate([pk_s, b_ks], axis=1)
        v_s = jnp.concatenate([pv_s, b_vs], axis=1)
        k_w = jnp.concatenate([buf_k, b_kw], axis=1)
        v_w = jnp.concatenate([buf_v, b_vw], axis=1)
        wp0 = pk_a.shape[1] - buf_k.shape[1]
    pad_w = max(0, wb - k_w.shape[1])
    new_wk = jnp.pad(k_w, ((0, 0), (pad_w, 0), (0, 0), (0, 0)))[:, -wb:]
    new_wv = jnp.pad(v_w, ((0, 0), (pad_w, 0), (0, 0), (0, 0)))[:, -wb:]
    o_a = moba_attention(a_q, k_a, v_a, pos).reshape(B, T, MOBA_WIDTH) @ lw['w_br_a']
    br = nsa_attention(b_q, k_c, v_c, k_s, v_s, k_w, v_w, wp0, pos,
                       lw['pe_cmp_k'], lw['w_cmp_k1'], lw['w_cmp_k2'],
                       lw['pe_cmp_v'], lw['w_cmp_v1'], lw['w_cmp_v2'])
    gates = jax.nn.sigmoid(b_gate.reshape(B, T, NSA_HEADS, 3))
    o_b = jnp.sum(gates[..., None] * br, axis=3).reshape(B, T, NSA_WIDTH) @ lw['w_br_b']
    m_a, m_b = jnp.split(jax.nn.sigmoid(merge), 2, axis=-1)
    x = x + g1[:, None, :] * ((m_a * o_a + m_b * o_b) @ lw['w_out'])
    h2 = modulate(rms_norm(x, lw['norm_ffn_g']), sh2, sc2)
    x = x + g2[:, None, :] * hmoe(h2, lw['w_router_grp'], lw['w_router_exp'], lw['w_expert_in'], lw['w_expert_out'])
    return x, (a_k, a_v, b_kc, b_vc, b_ks, b_vs, new_wk, new_wv)

def setup_inputs(seed: int = 0) -> dict:
    key = jax.random.key(seed)
    ks = jax.random.split(key, 32)
    f32 = jnp.float32

    def nrm(k, shape, scale):
        return jax.random.normal(k, shape, f32) * scale

    n_pages = PAST_LEN // PAGE_SIZE
    n_phys = (DEC_BATCH * n_pages * 5) // 4
    wb = min(WINDOW, PAST_LEN)
    page_table = jax.random.permutation(ks[0], n_phys)[:DEC_BATCH * n_pages].reshape(DEC_BATCH, n_pages).astype(jnp.int32)
    return {
        'x_prompt': nrm(ks[1], (BATCH, SEQ, D_MODEL), 1.0),
        'x_sample': nrm(ks[2], (DEC_BATCH, DEC_SEQ, D_MODEL), 1.0),
        'c_prompt': nrm(ks[3], (BATCH, D_MODEL), 1.0),
        'c_sample': nrm(ks[4], (DEC_BATCH, D_MODEL), 1.0),
        'cache_moba_k': nrm(ks[5], (DEPTH, n_phys, PAGE_SIZE, MOBA_HEADS, D_HEAD), 1.0),
        'cache_moba_v': nrm(ks[6], (DEPTH, n_phys, PAGE_SIZE, MOBA_HEADS, D_HEAD), 1.0),
        'cache_nsa_cmp_k': nrm(ks[7], (DEPTH, n_phys, PAGE_SIZE, NSA_KV_HEADS, D_HEAD), 1.0),
        'cache_nsa_cmp_v': nrm(ks[8], (DEPTH, n_phys, PAGE_SIZE, NSA_KV_HEADS, D_HEAD), 1.0),
        'cache_nsa_slc_k': nrm(ks[9], (DEPTH, n_phys, PAGE_SIZE, NSA_KV_HEADS, D_HEAD), 1.0),
        'cache_nsa_slc_v': nrm(ks[10], (DEPTH, n_phys, PAGE_SIZE, NSA_KV_HEADS, D_HEAD), 1.0),
        'state_nsa_win_k': nrm(ks[11], (DEPTH, DEC_BATCH, wb, NSA_KV_HEADS, D_HEAD), 1.0),
        'state_nsa_win_v': nrm(ks[12], (DEPTH, DEC_BATCH, wb, NSA_KV_HEADS, D_HEAD), 1.0),
        'page_table': page_table,
        'w_ada': nrm(ks[13], (DEPTH, D_MODEL, 6 * D_MODEL), D_MODEL ** -0.5),
        'b_ada': nrm(ks[14], (DEPTH, 6 * D_MODEL), 0.01),
        'norm_mix_g': 1.0 + nrm(ks[15], (DEPTH, D_MODEL), 0.02),
        'w_in': nrm(ks[16], (DEPTH, D_MODEL, IN_COLS), D_MODEL ** -0.5),
        'pe_cmp_k': nrm(ks[17], (DEPTH, CMP_LEN, D_HEAD), 0.1),
        'w_cmp_k1': nrm(ks[18], (DEPTH, CMP_LEN * D_HEAD, CMP_HIDDEN), (CMP_LEN * D_HEAD) ** -0.5),
        'w_cmp_k2': nrm(ks[19], (DEPTH, CMP_HIDDEN, D_HEAD), CMP_HIDDEN ** -0.5),
        'pe_cmp_v': nrm(ks[20], (DEPTH, CMP_LEN, D_HEAD), 0.1),
        'w_cmp_v1': nrm(ks[21], (DEPTH, CMP_LEN * D_HEAD, CMP_HIDDEN), (CMP_LEN * D_HEAD) ** -0.5),
        'w_cmp_v2': nrm(ks[22], (DEPTH, CMP_HIDDEN, D_HEAD), CMP_HIDDEN ** -0.5),
        'w_br_a': nrm(ks[23], (DEPTH, MOBA_WIDTH, D_MODEL), MOBA_WIDTH ** -0.5),
        'w_br_b': nrm(ks[24], (DEPTH, NSA_WIDTH, D_MODEL), NSA_WIDTH ** -0.5),
        'w_out': nrm(ks[25], (DEPTH, D_MODEL, D_MODEL), D_MODEL ** -0.5),
        'norm_ffn_g': 1.0 + nrm(ks[26], (DEPTH, D_MODEL), 0.02),
        'w_router_grp': nrm(ks[27], (DEPTH, D_MODEL, N_GROUPS), D_MODEL ** -0.5),
        'w_router_exp': nrm(ks[28], (DEPTH, D_MODEL, N_EXPERTS), D_MODEL ** -0.5),
        'w_expert_in': nrm(ks[29], (DEPTH, N_EXPERTS, D_MODEL, 2 * D_EXPERT), D_MODEL ** -0.5),
        'w_expert_out': nrm(ks[30], (DEPTH, N_EXPERTS, D_EXPERT, D_MODEL), D_EXPERT ** -0.5),
        'norm_final_g': 1.0 + nrm(ks[31], (D_MODEL,), 0.02),
    }

def reference(x_prompt, x_sample, c_prompt, c_sample, cache_moba_k, cache_moba_v,
              cache_nsa_cmp_k, cache_nsa_cmp_v, cache_nsa_slc_k, cache_nsa_slc_v,
              state_nsa_win_k, state_nsa_win_v, page_table, w_ada, b_ada, norm_mix_g, w_in,
              pe_cmp_k, w_cmp_k1, w_cmp_k2, pe_cmp_v, w_cmp_v1, w_cmp_v2, w_br_a, w_br_b, w_out,
              norm_ffn_g, w_router_grp, w_router_exp, w_expert_in, w_expert_out, norm_final_g):
    t_p = x_prompt.shape[1]
    t_s = x_sample.shape[1]
    past_len = page_table.shape[1] * cache_moba_k.shape[2]
    pos_p = jnp.arange(t_p, dtype=jnp.int32)
    pos_s = past_len + jnp.arange(t_s, dtype=jnp.int32)
    xp, xs = x_prompt, x_sample
    st_p, st_s = [], []
    for l in range(DEPTH):
        lw = {'w_ada': w_ada[l], 'b_ada': b_ada[l], 'norm_mix_g': norm_mix_g[l], 'w_in': w_in[l],
              'pe_cmp_k': pe_cmp_k[l], 'w_cmp_k1': w_cmp_k1[l], 'w_cmp_k2': w_cmp_k2[l],
              'pe_cmp_v': pe_cmp_v[l], 'w_cmp_v1': w_cmp_v1[l], 'w_cmp_v2': w_cmp_v2[l],
              'w_br_a': w_br_a[l], 'w_br_b': w_br_b[l], 'w_out': w_out[l], 'norm_ffn_g': norm_ffn_g[l],
              'w_router_grp': w_router_grp[l], 'w_router_exp': w_router_exp[l],
              'w_expert_in': w_expert_in[l], 'w_expert_out': w_expert_out[l]}
        xp, new_p = layer(xp, c_prompt, pos_p, None, lw)
        past = (gather_pages(cache_moba_k[l], page_table), gather_pages(cache_moba_v[l], page_table),
                gather_pages(cache_nsa_cmp_k[l], page_table), gather_pages(cache_nsa_cmp_v[l], page_table),
                gather_pages(cache_nsa_slc_k[l], page_table), gather_pages(cache_nsa_slc_v[l], page_table),
                state_nsa_win_k[l], state_nsa_win_v[l])
        xs, new_s = layer(xs, c_sample, pos_s, past, lw)
        st_p.append(new_p)
        st_s.append(new_s)
    sp = [jnp.stack(a, axis=0) for a in zip(*st_p)]
    ss = [jnp.stack(a, axis=0) for a in zip(*st_s)]
    y_prompt = rms_norm(xp, norm_final_g)
    y_sample = rms_norm(xs, norm_final_g)
    return (y_prompt, y_sample, sp[0], sp[1], sp[2], sp[3], sp[4], sp[5], sp[6], sp[7],
            ss[0], ss[1], ss[2], ss[3], ss[4], ss[5], ss[6], ss[7])


_drawn_inputs = setup_inputs


def setup_inputs(seed=0):
    import zlib

    import numpy as np

    out = dict(_drawn_inputs(seed))
    spreads = {}
    factors = {'cache_nsa_cmp_k': 4.007, 'pe_cmp_k': 8.0, 'norm_final_g': 2.886}
    for name, (base, spread) in spreads.items():
        noise = np.random.default_rng([zlib.crc32(name.encode()), seed]).standard_normal(out[name].shape)
        drawn = base * np.exp(spread * noise) if base else spread * noise
        out[name] = __import__('jax').numpy.asarray(drawn.astype(out[name].dtype))
    for name, factor in factors.items():
        out[name] = (out[name] * factor).astype(out[name].dtype)
    return out
```

```python
from contextlib import ExitStack

import concourse.bass as bass
from concourse import mybir

F32 = mybir.dt.float32
I32 = mybir.dt.int32
ALU = mybir.AluOpType
ACT = mybir.ActivationFunctionType
AX = mybir.AxisListType.X

P = 128
D = 1024
KD = D // P
NP_, NB, NQ = 256, 8, 8
NS = NB * NQ
N = NP_ + NS
NC = 1 + NB
PAGES = 8
PAGE = 128
NPHYS = 80
H = 8
DH = 64
NCMP = 63
NCMPP = 15
E = 32
EPS = 1e-6
TINY = 1e-30
NEG = -1e30
SCALE = DH ** -0.5
WIN = 512
TOK = [(0, 128), (128, 128), (256, 64)]
GATES = 3 * H
ADA_TILES = 12
T_TILES = 8
ROT = 15
SLOT = KD * 512
RT = 80

C_ID, C_TRI, C_R, C_NEW = 0, 128, 512, 640
C_WIN = C_NEW + 4 * NS
C_CADD = C_WIN + 8
C_C01 = C_CADD + 2 * NCMPP
C_IDX = C_C01 + 2 * NCMPP
C_ONE = C_IDX + 16
C_PERM = C_ONE + 128
C_COS = C_PERM + 128
C_SIN = C_COS + N
C_ALL = C_SIN + N
V_B, V_G = 0, 48
V_W2K = V_G + 3 * KD
V_W2V = V_W2K + DH
V_PE = V_W2V + DH
V_WR = V_PE + 32
V_C = V_WR + KD * 36
V_ALL = V_C + KD * NC


def build(nc, vec, x_t, pages, w_ada, w_in, w1, w1d, cmp_pages, k_pages, v_pages, win, w_br, w_out,
          w_moe, consts, win_state,
          o_y, o_kt, o_small, o_va, o_vs, o_zero, o_win, scratch):
    with ExitStack() as ctx:
        def sem(name):
            return ctx.enter_context(nc.semaphore(name))

        TOTAL = 53000
        arena = ctx.enter_context(nc.sbuf_tensor("arena", [P, TOTAL], F32))
        page_row = ctx.enter_context(nc.sbuf_tensor("page_row", [1, NB * PAGES], I32))
        banks = [ctx.enter_context(nc.psum_tensor(f"bank{i}", [P, 512], F32)) for i in range(8)]

        def at(off, *dims):
            size = 1
            for d in dims:
                size *= d
            assert off + size <= TOTAL, (off, size)
            ap = arena[:, off:off + size]
            if len(dims) == 2:
                return ap.rearrange("p (a b) -> p a b", b=dims[1])
            if len(dims) == 3:
                return ap.rearrange("p (a b c) -> p a b c", b=dims[1], c=dims[2])
            if len(dims) == 4:
                return ap.rearrange("p (a b c d) -> p a b c d", b=dims[1], c=dims[2], d=dims[3])
            return ap

        place = [0]

        def keep(*dims):
            size = 1
            for d in dims:
                size *= d
            place[0] += size
            return at(place[0] - size, *dims)

        cst = keep(C_ALL)
        vecs = keep(V_ALL)
        mod = keep(48, NC)
        scl = keep(2, KD, NC)
        xT = keep(KD, N)
        mT = keep(16, N)
        oTa = keep(4, N)
        oTb = keep(4, N)
        rstd = keep(N)
        assert place[0] <= 15000, place[0]
        PJ = place[0]
        qA, kA, qB = keep(4, N), keep(4, N), keep(4, N)
        kvc = keep(4, N)
        vA = keep(3, 512)
        vS = keep(3, 256)
        gate = keep(3, GATES)
        gateS = keep(4, 3)
        kcm = keep(NB, NCMP)
        vcm = keep(NB, P)
        kcmp, vcmp = keep(NCMPP), keep(P)
        A = place[0]
        sq = at(A, KD, N)
        hT = at(A + 2560, KD, N)
        ring = [at(A + 5120 + SLOT * k, KD, 512) for k in range(3)]
        qs = at(A + 5120 + 3 * SLOT, 3, N)
        turn = at(A + 5120 + 3 * SLOT + 3 * N, 2, 2, N)
        W1 = A + 5120
        w1_sb = at(W1, 2, 16, P)
        w1d_sb = at(W1 + 4096, 2, 32, P)
        XCO = W1 + 3 * SLOT + 7 * N
        xc = at(XCO, 32, 256)
        hA, hB, hS = at(A, 4, 2, 64), at(A + 512, 4, 2, 64), at(A + 1024, 8, 63)
        gl = at(A + 1536, 2, 4, 2, 63)
        glp = at(A + 2600, 2, 2, NCMPP)
        peb = at(A + 2700, 2)
        UNIT = PAGES * 640 + WIN
        kU = [at(A + UNIT * b, UNIT) for b in range(2)]
        vU = [at(A + UNIT * (2 + b), UNIT) for b in range(2)]
        B = A + 4 * UNIT
        sM, sS, sW = at(B, 1024 + NS), at(B + 1088, 1024 + NS), at(B + 2176, WIN + NS)
        sC = at(B + 2752, 72)
        sP = [at(B + 420 * k, 420) for k in range(3)]
        ptP = at(B + 1300, 3, 384)
        ptC = at(B + 2452, 256)
        pcn = at(B + 2824, 66)
        st = at(B + 2890, 64)
        pt = at(B + 2960, 6, 512)
        qz = at(B + 6032, 2, 4, 64)
        qzb = at(B + 6544, 2, 64)
        pcg = at(B + 6672, 64)
        wbr_sb = at(PJ, 8, D)
        wo_sb = at(PJ + 8192, KD, D)
        M0 = PJ + 16384
        slots = [at(M0 + 6144 * k, 6144) for k in range(2)]
        cbc = at(M0 + 12288, E, N)
        sq2 = at(PJ, KD, N)
        rt = PJ + 2560
        moe_in = mT[:, 8:16, :]
        yR = at(PJ + 3800, 3, D)

        ident = cst[:, C_ID:C_ID + 128]
        ones = cst[:, C_ONE:C_ONE + 128]
        cT = vecs[:, V_C:V_C + KD * NC].rearrange("p (k c) -> p k c", c=NC)
        gains = vecs[:, V_G:V_G + 3 * KD].rearrange("p (j k) -> p j k", k=KD)
        w2k, w2v = vecs[:, V_W2K:V_W2K + DH], vecs[:, V_W2V:V_W2V + DH]
        pe = vecs[:, V_PE:V_PE + 32].rearrange("p (v t) -> p v t", t=16)
        w_rt = vecs[:, V_WR:V_WR + KD * 36].rearrange("p (k n) -> p k n", n=36)
        idx = cst[:, C_IDX:C_IDX + 16]

        s_in = sem("inputs_loaded")
        s_w = [sem(f"weight_tile_loaded{k}") for k in range(3)]
        s_w1 = sem("cmp_weights_loaded")
        s_xc = sem("cmp_pages_loaded")
        s_k = [sem(f"keys_loaded{b}") for b in range(2)]
        s_v = [sem(f"values_loaded{b}") for b in range(2)]
        s_wbr, s_wo = sem("branch_weights_loaded"), sem("out_weights_loaded")
        s_e = [sem(f"expert_loaded{k}") for k in range(2)]
        s_gd, s_gs = sem("gates_in_dram"), sem("gates_by_row")
        s_out = sem("outputs_written")
        s_silu, s_sq, s_ss = sem("cond_silu"), sem("squares"), sem("square_sums")
        s_ada, s_mod, s_h = sem("ada_tile_done"), sem("mod_written"), sem("h_ready")
        s_proj, s_pev = sem("proj_chunk_done"), sem("proj_evacuated")
        s_rot, s_rope, s_t1 = sem("rotated"), sem("rope_done"), sem("rope_cos_part")
        s_row, s_rowA, s_rowV = sem("row_proj_done"), sem("row_small_evac"), sem("row_v_evac")
        s_pb, s_pbv = sem("pe_bias_sum"), sem("pe_bias_ready")
        s_cp, s_cpg, s_cp2, s_cpe = sem("cmp_prompt_hid"), sem("cmp_prompt_gelu"), sem("cmp_prompt_out"), sem("cmp_prompt_ready")
        s_cAB, s_cA, s_cB = sem("cmp_hid"), sem("cmp_first_half_out"), sem("cmp_second_half_out")
        s_cS, s_cg, s_c2, s_kcm = sem("cmp_hid_sum"), sem("cmp_gelu"), sem("cmp_out"), sem("cmp_ready")
        s_sc, s_sev, s_nm, s_exp = sem("p_scores"), sem("p_scores_out"), sem("p_max"), sem("p_exp")
        s_r, s_nrm, s_tr = sem("p_recip"), sem("p_normed"), sem("p_turned")
        s_ptA, s_ptD, s_pv, s_oev = sem("p_probs_moba_out"), sem("p_probs_nsa_out"), sem("p_pv"), sem("p_o_out")
        z_qz, z_kd, z_small, z_sev = sem("q_blocks"), [sem(f"keys_used{b}") for b in range(2)], sem("s_scores"), sem("s_scores_out")
        z_cm, z_ce, z_pcn, z_imp, z_gsr = sem("cmp_max"), sem("cmp_exp"), sem("cmp_probs"), sem("cmp_group_sums"), sem("cmp_group_read")
        z_nm, z_ex, z_rr, z_np, z_nd = sem("s_max"), sem("s_exp"), sem("s_recip"), sem("s_normed_pool"), sem("s_normed_dve")
        z_tr, z_tA, z_tD = sem("s_turned"), sem("s_turned_out_act"), sem("s_turned_out_dve")
        z_vd, z_oev = [sem(f"values_used{b}") for b in range(2)], sem("s_o_out")
        s_br, s_mg, s_op, s_x1 = sem("branch_proj"), sem("merged"), sem("out_proj"), sem("x1_chunk")
        s_sq2, s_ss2, s_h2 = sem("squares2"), sem("square_sums2"), sem("moe_in_ready")
        s_lg, s_lc, s_le, s_l8, s_l8e = sem("logits"), sem("logit_diffs"), sem("group_exp"), sem("expert_diffs"), sem("expert_exp")
        s_cb, s_cbt, s_cbr, s_bc, s_bce = sem("combine"), sem("combine_turned"), sem("combine_rows"), sem("combine_spread"), sem("combine_kept")
        s_hid, s_sil, s_gb, s_act, s_eo = sem("expert_hid"), sem("silu_done"), sem("gated_half"), sem("expert_act"), sem("expert_used")
        s_ya, s_yr, s_yt, s_x2, s_sq3, s_ss3, s_fin = (sem("moe_sum"), sem("moe_rows"), sem("moe_turned"), sem("x2_chunk"),
                                                       sem("squares3"), sem("square_sums3"), sem("final_ready"))
        s_ch, s_cha, s_chp = sem("vector_chain"), sem("scalar_chain"), sem("pool_chain")
        s_z, s_y = sem("zeros_ready"), sem("y_written")
        s_ms, s_rms = sem("mean_square"), sem("root_mean_square")

        block = ctx.enter_context(nc.Block())

        @block.sync
        def _(sp):
            sp.dma_start(vecs, vec).then_inc(s_in, 16)
            sp.dma_start(cst, consts).then_inc(s_in, 16)
            sp.dma_start(xT, x_t).then_inc(s_in, 16)
            sp.dma_start(page_row[:, :], pages).then_inc(s_in, 16)

            def page_of(b, p):
                return sp.value_load(page_row[0:1, b * PAGES + p:b * PAGES + p + 1], min_val=0, max_val=NPHYS - 1)

            def cmp_half(half):
                for j in range(32):
                    pg = page_of(4 * half + j // PAGES, j % PAGES)
                    sp.dma_start(xc[:, j, :], cmp_pages[bass.ds(pg, 1), :, :].rearrange("o p n -> (o p) n")).then_inc(s_xc, 16)

            def unit(b, dst, src, w, s):
                for p in range(PAGES):
                    pg = page_of(b, p)
                    sp.dma_start(dst[:, p * 640:(p + 1) * 640],
                                 src[bass.ds(pg, 1), :, :].rearrange("o p n -> (o p) n")).then_inc(s, 16)
                sp.dma_start(dst[:, PAGES * 640:UNIT], win[w, b]).then_inc(s, 16)

            for n in range(ADA_TILES + 10):
                if n >= 3 and n - 3 < ADA_TILES:
                    sp.wait_ge(s_ada, n - 2)
                elif n >= 3:
                    sp.wait_ge(s_proj, 4 * (n - 2 - ADA_TILES))
                if n < ADA_TILES:
                    sp.dma_start(ring[n % 3], w_ada[n]).then_inc(s_w[n % 3], 16)
                else:
                    sp.dma_start(ring[n % 3], w_in[n - ADA_TILES]).then_inc(s_w[n % 3], 16)
                if n == ADA_TILES:
                    sp.wait_ge(s_in, 64)
                    cmp_half(0)
            sp.wait_ge(s_row, 6)
            sp.dma_start(w1_sb, w1).then_inc(s_w1, 16)
            for v in range(2):
                sp.dma_start(w1d_sb[:, v], w1d[v]).then_inc(s_w1, 16)
            sp.wait_ge(s_cAB, 4)
            cmp_half(1)
            sp.wait_ge(s_kcm, 4)
            sp.wait_ge(s_cpe, 2)
            for i in range(4):
                for b in range(2):
                    if i:
                        sp.wait_ge(z_kd[b], i)
                    unit(2 * i + b, kU[b], k_pages, 0, s_k[b])
                for b in range(2):
                    if i:
                        sp.wait_ge(z_vd[b], i)
                    unit(2 * i + b, vU[b], v_pages, 1, s_v[b])
            for b in range(2):
                sp.wait_ge(z_vd[b], 4)
            sp.dma_start(wbr_sb, w_br).then_inc(s_wbr, 16)
            sp.dma_start(wo_sb, w_out).then_inc(s_wo, 16)
            for k in range(2):
                sp.dma_start(slots[k], w_moe[k]).then_inc(s_e[k], 16)
            with sp.Fori(1, E // 2) as i:
                for k in range(2):
                    sp.wait_ge(s_eo, i * 2 + (k - 1))
                    sp.dma_start(slots[k], w_moe[bass.ds(i * 2 + k, 1), :, :].rearrange("o p n -> (o p) n")).then_inc(s_e[k], 16)
            sp.wait_ge(s_fin, 1)
            sp.dma_start(o_y, xT).then_inc(s_y, 16)
            sp.wait_ge(s_y, 16)
            sp.wait_ge(s_out, 16 * 9)

        @block.tensor
        def _(te):
            mm = te.matmul
            te.wait_ge(s_in, 64)
            te.wait_ge(s_sq, 1)
            for k in range(KD):
                m = mm(banks[7][:, 0:N], ones, sq[:, k, :], start=(k == 0), stop=(k == KD - 1))
            m.then_inc(s_ss, 1)
            te.wait_ge(s_silu, 1)
            for n in range(ADA_TILES):
                te.wait_ge(s_w[n % 3], 16 * (n // 3 + 1))
                if n >= 3:
                    te.wait_ge(s_mod, n - 2)
                for c in range(4):
                    for k in range(KD):
                        m = mm(banks[n % 3][:, NC * c:NC * (c + 1)], ring[n % 3][:, k, P * c:P * (c + 1)],
                               cT[:, k, :], start=(k == 0), stop=(k == KD - 1))
                m.then_inc(s_ada, 1)
            te.wait_ge(s_h, 1)
            te.wait_ge(s_mod, ADA_TILES)

            def rotate(c):
                te.wait_ge(s_pev, c + 1)
                if c >= 2:
                    te.wait_ge(s_rope, c - 1)
                mm(banks[4 + c % 2][:, 0:N], cst[:, C_PERM:C_PERM + P], qs[:, c % 3, :],
                   start=True, stop=True).then_inc(s_rot, 1)

            for c in range(4 * T_TILES):
                n = ADA_TILES + c // 4
                te.wait_ge(s_w[n % 3], 16 * (n // 3 + 1))
                if c >= 4:
                    te.wait_ge(s_pev, c - 3)
                for k in range(KD):
                    m = mm(banks[c % 4][:, 0:N], ring[n % 3][:, k, P * (c % 4):P * (c % 4 + 1)], hT[:, k, :],
                           start=(k == 0), stop=(k == KD - 1))
                m.then_inc(s_proj, 1)
                if 1 <= c <= ROT:
                    rotate(c - 1)
            te.wait_ge(s_rope, ROT)
            te.wait_ge(s_pev, 4 * T_TILES)
            for j, width in enumerate((512, 280)):
                n = ADA_TILES + T_TILES + j
                te.wait_ge(s_w[n % 3], 16 * (n // 3 + 1))
                for t, (t0, tn) in enumerate(TOK):
                    bank = banks[4 + t] if j == 0 else banks[t]
                    for k in range(KD):
                        m = mm(bank[0:tn, 0:width], hT[:, k, t0:t0 + tn], ring[n % 3][:, k, 0:width],
                               start=(k == 0), stop=(k == KD - 1))
                    m.then_inc(s_row, 1)

            te.wait_ge(s_w1, 48)
            for v in range(2):
                for t in range(16):
                    m = mm(banks[7][:, v:v + 1], w1_sb[:, v, t, :], pe[:, v, t:t + 1], start=(t == 0), stop=(t == 15))
            m.then_inc(s_pb, 1)
            te.wait_ge(s_rowV, 3)
            for v in range(2):
                for g in range(2):
                    for t in range(32):
                        m = mm(banks[6 - g][:, v * NCMPP:(v + 1) * NCMPP],
                               w1d_sb[DH * g:DH * (g + 1), v, t, :],
                               kvc[DH * g:DH * (g + 1), 3 * v, t:t + 16 * (NCMPP - 1) + 1:16],
                               start=(t == 0), stop=(t == 31))
            m.then_inc(s_cp, 1)

            def cmp_hid(half):
                te.wait_ge(s_xc, 32 * 16 * (half + 1))
                if half == 0:
                    te.wait_ge(s_rowA, 6)
                for v in range(2):
                    for part in range(2):
                        if half:
                            te.wait_ge(s_cA if part == 0 else s_cB, v + 1)
                        for t in range(8):
                            c = P * v + 16 * t
                            m = mm(banks[2 * v + part][:, :].rearrange("p (j n) -> p j n", n=16),
                                   w1_sb[:, v, 8 * part + t, :], xc[:, :, c:c + 16],
                                   start=(t == 0), stop=(t == 7))
                        m.then_inc(s_cAB, 1)

            def cmp_out(half):
                te.wait_ge(s_cg, 2 * half + 1)
                if half:
                    te.wait_ge(s_kcm, 2)
                for g in range(2):
                    m = mm(banks[4][DH * g:DH * (g + 1), 0:4 * NCMP].rearrange("p (b n) -> p b n", n=NCMP),
                           w2k, gl[:, 0, :, g, :], start=True, stop=True)
                m.then_inc(s_c2, 1)
                te.wait_ge(s_cg, 2 * half + 2)
                for b in range(4):
                    for g in range(2):
                        m = mm(banks[5][0:NCMP, P * b + DH * g:P * b + DH * (g + 1)], gl[:, 1, b, g, :], w2v,
                               start=True, stop=True)
                m.then_inc(s_c2, 1)

            cmp_hid(0)
            te.wait_ge(s_cpg, 4)
            te.wait_ge(s_pbv, 1)
            for g in range(2):
                m = mm(banks[7][DH * g:DH * (g + 1), 0:NCMPP], w2k, glp[:, 0, g, :], start=True, stop=True)
            m.then_inc(s_cp2, 1)
            for g in range(2):
                m = mm(banks[6][0:NCMPP, DH * g:DH * (g + 1)], glp[:, 1, g, :], w2v, start=True, stop=True)
            m.then_inc(s_cp2, 1)
            cmp_out(0)
            cmp_hid(1)
            cmp_out(1)

            def p_scores(h):
                g, r, hp, o = h // 4, h % 4, h // 2, DH * (h % 2)
                for kind in range(3):
                    if h:
                        te.wait_ge(s_sev, 3 * (h - 1) + kind + 1)
                    if kind == 0:
                        q, k = qA[o:o + DH, hp, :], kA[o:o + DH, hp, :]
                    else:
                        q, k = qB[DH * g:DH * (g + 1), r, :], kvc[DH * g:DH * (g + 1), kind, :]
                    mm(banks[kind][:, 0:128], q[:, 0:128], k[:, 0:128], start=True, stop=True)
                    m = mm(banks[kind][:, 128:384], q[:, 128:256], k[:, 0:256], start=True, stop=True)
                    if kind == 2:
                        for c in range(2):
                            m = mm(banks[kind][:, 384 + NCMPP * c:384 + NCMPP * (c + 1)], q[:, 128 * c:128 * (c + 1)],
                                   kcmp[DH * g:DH * (g + 1), :], start=True, stop=True)
                    m.then_inc(s_sc, 1)

            def p_turn(h):
                te.wait_ge(s_nrm, h + 1)
                for kind in range(3):
                    if h:
                        te.wait_ge(*((s_ptA, h) if kind == 0 else (s_ptD, 2 * (h - 1) + kind)))
                    if kind < 2:
                        te.transpose(banks[3 + kind][0:NCMPP, 384:512],
                                     sP[2][:, 384 + NCMPP * kind:384 + NCMPP * (kind + 1)], ident)
                    for j in range(3):
                        m = te.transpose(banks[3 + kind][:, P * j:P * (j + 1)], sP[kind][:, P * j:P * (j + 1)], ident)
                    m.then_inc(s_tr, 1)

            def p_values(h):
                g, o = h // 4, DH * (h % 2)
                if h:
                    te.wait_ge(s_oev, 2 * (h - 1) + 1)
                te.wait_ge(s_ptA, h + 1)
                mm(banks[6][o:o + DH, 0:256], vA[:, 0, DH * h:DH * (h + 1)], ptP[:, 0, 0:256], start=True, stop=False)
                mm(banks[6][o:o + DH, 128:256], vA[:, 1, DH * h:DH * (h + 1)], ptP[:, 0, 256:384],
                   start=False, stop=True).then_inc(s_pv, 1)
                if h:
                    te.wait_ge(s_oev, 2 * h)
                te.wait_ge(s_ptD, 2 * h + 2)
                out = banks[7][DH * g:DH * (g + 1), :]
                mm(out[:, 0:256], vcmp[0:NCMPP, DH * g:DH * (g + 1)], ptC[0:NCMPP, :], start=True, stop=False)
                for kind in (1, 2):
                    c = P * (kind - 1) + DH * g
                    mm(out[:, 0:256], vS[:, 0, c:c + DH], ptP[:, kind, 0:256], start=False, stop=False)
                    m = mm(out[:, 128:256], vS[:, 1, c:c + DH], ptP[:, kind, 256:384], start=False, stop=(kind == 2))
                m.then_inc(s_pv, 1)

            te.wait_ge(s_cpe, 2)
            te.wait_ge(s_kcm, 4)
            p_scores(0)
            for h in range(H):
                if h + 1 < H:
                    p_scores(h + 1)
                p_turn(h)
                p_values(h)

            def smp_scores(i):
                te.wait_ge(z_qz, i + 1)
                if i:
                    te.wait_ge(z_sev, i)
                for b in range(2):
                    rows = slice(64 * b, 64 * b + 64)
                    te.wait_ge(s_k[b], 144 * (i + 1))
                    pg = kU[b][:, 0:PAGES * 640].rearrange("p (j n) -> p j n", n=640)
                    for half in range(2):
                        for hp in range(4):
                            mm(banks[half][rows, :].rearrange("p (j n) -> p j n", n=P), qz[:, b, hp, :],
                               pg[:, 4 * half:4 * half + 4, P * hp:P * (hp + 1)], start=(hp == 0), stop=(hp == 3))
                        mm(banks[2 + half][rows, :].rearrange("p (j n) -> p j n", n=P), qzb[:, b, :],
                           pg[:, 4 * half:4 * half + 4, 512:640], start=True, stop=True)
                    mm(banks[4][rows, :], qzb[:, b, :], kU[b][:, PAGES * 640:UNIT], start=True, stop=True)\
                        .then_inc(z_kd[b], 1)
                for b in range(2):
                    rows = slice(64 * b, 64 * b + 64)
                    for hp in range(4):
                        mm(banks[5][rows, 0:64], qz[:, b, hp, :], kA[:, hp, NP_:N], start=(hp == 0), stop=(hp == 3))
                    mm(banks[5][rows, 64:128], qzb[:, b, :], kvc[:, 1, NP_:N], start=True, stop=True)
                    mm(banks[5][rows, 128:192], qzb[:, b, :], kvc[:, 2, NP_:N], start=True, stop=True)
                    m = mm(banks[5][rows, 192:192 + NCMP], qzb[:, b, :], kcm[:, 2 * i + b, :], start=True, stop=True)
                m.then_inc(z_small, 1)

            def smp_group(i):
                te.wait_ge(z_pcn, i + 1)
                mm(banks[5][:, 256:321], cst[:, C_R:C_R + P], pcn[:, 0:65], start=True, stop=True).then_inc(z_imp, 1)

            def smp_turn(i):
                te.wait_ge(z_np, 2 * i + 2)
                te.wait_ge(z_nd, i + 1)
                for j in range(6):
                    if 6 * i + j:
                        prev = 6 * i + j - 1
                        te.wait_ge(z_tA if prev % 2 == 0 else z_tD, prev // 2 + 1)
                    for c in range(4):
                        if j < 5:
                            src = (sM, sM, sS, sS, sW)[j][:, 512 * (j % 2 if j < 4 else 0) + P * c:][:, 0:P]
                            m = te.transpose(banks[6][:, P * c:P * (c + 1)], src, ident)
                        else:
                            src = (sM[:, 1024:1088], sS[:, 1024:1088], sW[:, 512:576], pcg)[c]
                            m = te.transpose(banks[6][0:64, P * c:P * (c + 1)], src, ident)
                    m.then_inc(z_tr, 1)

            def smp_values(i):
                te.wait_ge(z_tA, 3 * i + 3)
                te.wait_ge(z_tD, 3 * i + 3)
                if i:
                    te.wait_ge(z_oev, i)
                for b in range(2):
                    te.wait_ge(s_v[b], 144 * (i + 1))
                    for hp in range(4):
                        out = banks[7][:, P * b + 16 * hp:P * b + 16 * hp + 16]
                        c = 64 * b + 16 * hp
                        for p in range(PAGES):
                            mm(out, vU[b][:, 640 * p + P * hp:640 * p + P * (hp + 1)],
                               pt[:, p // 4, P * (p % 4) + c:P * (p % 4) + c + 16], start=(p == 0), stop=False)
                        mm(out, vA[0:64, 2, P * hp:P * (hp + 1)], pt[0:64, 5, c:c + 16], start=False, stop=True)
                    out = banks[7][:, P * b + 64:P * b + 128]
                    for p in range(PAGES):
                        mm(out, vU[b][:, 640 * p + 512:640 * p + 640],
                           pt[:, 2 + p // 4, P * (p % 4) + 64 * b:P * (p % 4) + 64 * b + 64], start=(p == 0), stop=False)
                    for p in range(4):
                        mm(out, vU[b][:, PAGES * 640 + P * p:PAGES * 640 + P * (p + 1)],
                           pt[:, 4, P * p + 64 * b:P * p + 64 * b + 64], start=False, stop=False)
                    mm(out, vS[0:64, 2, 0:128], pt[0:64, 5, P + 64 * b:P + 64 * b + 64], start=False, stop=False)
                    mm(out, vS[0:64, 2, 128:256], pt[0:64, 5, 2 * P + 64 * b:2 * P + 64 * b + 64], start=False, stop=False)
                    mm(out, vcm[0:NCMP, 2 * i + b, :], pt[0:NCMP, 5, 3 * P + 64 * b:3 * P + 64 * b + 64],
                       start=False, stop=True).then_inc(z_vd[b], 1)

            te.wait_ge(s_ptD, 2 * H)
            te.wait_ge(s_oev, 2 * H)
            smp_scores(0)
            smp_group(0)
            for i in range(4):
                if i + 1 < 4:
                    smp_scores(i + 1)
                smp_turn(i)
                smp_values(i)
                if i + 1 < 4:
                    smp_group(i + 1)

            te.wait_ge(z_oev, 4)
            te.wait_ge(s_wbr, 16)
            for c in range(KD):
                for a, src in ((0, oTa), (1, oTb)):
                    if c >= 2:
                        te.wait_ge(s_mg, c - 1)
                    for k in range(4):
                        m = mm(banks[2 * (c % 2) + a][:, 0:N], wbr_sb[:, 4 * a + k, P * c:P * (c + 1)], src[:, k, :],
                               start=(k == 0), stop=(k == 3))
                m.then_inc(s_br, 1)
            te.wait_ge(s_mg, KD)
            te.wait_ge(s_wo, 16)
            for c in range(KD):
                if c >= 2:
                    te.wait_ge(s_x1, c - 1)
                for k in range(KD):
                    m = mm(banks[4 + c % 2][:, 0:N], wo_sb[:, k, P * c:P * (c + 1)], mT[:, k, :],
                           start=(k == 0), stop=(k == KD - 1))
                m.then_inc(s_op, 1)
            te.wait_ge(s_sq2, 1)
            for k in range(KD):
                m = mm(banks[7][:, 0:N], ones, sq2[:, k, :], start=(k == 0), stop=(k == KD - 1))
            m.then_inc(s_ss2, 1)

            te.wait_ge(s_h2, 1)
            for t in range(4):
                for k in range(KD):
                    m = mm(banks[0][0:RT, 36 * t:36 * (t + 1)], moe_in[:, k, RT * t:RT * (t + 1)], w_rt[:, k, :],
                           start=(k == 0), stop=(k == KD - 1))
            m.then_inc(s_lg, 1)
            te.wait_ge(s_cb, 1)
            for t in range(4):
                m = te.transpose(banks[1][0:E, RT * t:RT * (t + 1)], at(rt + 800, 4, E)[0:RT, t, :], ident[0:RT, 0:RT])
            m.then_inc(s_cbt, 1)
            te.wait_ge(s_cbr, 1)
            for e in range(E):
                if e >= 2:
                    te.wait_ge(s_bce, e - 1)
                mm(banks[2 + e % 2][:, 0:N], ident[0:E, e:e + 1].to_broadcast([E, P]), at(rt + 930, N)[0:E, :],
                   start=True, stop=True).then_inc(s_bc, 1)

            te.wait_ge(s_bce, E)

            def hidden(k, step, first):
                w = slots[k][:, 0:4096].rearrange("p (k n) -> p k n", n=512)
                j = step[1]
                for a in range(2):
                    if not first:
                        te.wait_ge(s_sil if a == 0 else s_gb, step[0])
                    for c in range(KD):
                        m = mm(banks[6 + a][:, 0:N], w[:, c, 256 * a + P * j:256 * a + P * (j + 1)], moe_in[:, c, :],
                               start=(c == 0), stop=(c == KD - 1))
                    m.then_inc(s_hid, 1)

            def output(k, done, j, act, start, stop):
                w = slots[k][:, 4096:6144].rearrange("p (j n) -> p j n", n=D)
                te.wait_ge(s_act, done)
                for t, (t0, tn) in enumerate(TOK):
                    for half in range(2):
                        m = mm(banks[2 * t + half][0:tn, :], act[:, t0:t0 + tn], w[:, j, 512 * half:512 * (half + 1)],
                               start=start, stop=stop)
                return m

            acts = at(rt + 8000 - 2560 + 0, 2, N)
            te.wait_ge(s_e[0], 16)
            hidden(0, (0, 0), True)
            hidden(0, (1, 1), False)
            output(0, 1, 0, acts[:, 0, :], True, False)
            te.wait_ge(s_e[1], 16)
            hidden(1, (2, 0), False)
            output(0, 2, 1, acts[:, 1, :], False, False).then_inc(s_eo, 1)
            hidden(1, (3, 1), False)
            output(1, 3, 0, acts[:, 0, :], False, False)
            with te.Fori(1, E // 2) as i:
                te.wait_ge(s_e[0], i * 16 + 16)
                hidden(0, (i * 4, 0), False)
                output(1, i * 4, 1, acts[:, 1, :], False, False).then_inc(s_eo, 1)
                hidden(0, (i * 4 + 1, 1), False)
                output(0, i * 4 + 1, 0, acts[:, 0, :], False, False)
                te.wait_ge(s_e[1], i * 16 + 16)
                hidden(1, (i * 4 + 2, 0), False)
                output(0, i * 4 + 2, 1, acts[:, 1, :], False, False).then_inc(s_eo, 1)
                hidden(1, (i * 4 + 3, 1), False)
                output(1, i * 4 + 3, 0, acts[:, 0, :], False, False)
            output(1, 2 * E, 1, acts[:, 1, :], False, True).then_inc(s_ya, 1)
            te.wait_ge(s_sil, 2 * E)
            te.wait_ge(s_yr, 6)
            for c in range(KD):
                if c >= 2:
                    te.wait_ge(s_x2, c - 1)
                for t, (t0, tn) in enumerate(TOK):
                    m = te.transpose(banks[6 + c % 2][:, t0:t0 + tn], yR[0:tn, t, P * c:P * (c + 1)], ident[0:tn, 0:tn])
                m.then_inc(s_yt, 1)
            te.wait_ge(s_sq3, 1)
            for k in range(KD):
                m = mm(banks[0][:, 0:N], ones, sq2[:, k, :], start=(k == 0), stop=(k == KD - 1))
            m.then_inc(s_ss3, 1)

        @block.scalar
        def _(sc):
            act = sc.activation

            def rms(n):
                sc.wait_ge(s_ms, n)
                act(rstd, rstd, ACT.Sqrt).then_inc(s_rms, 1)

            sc.wait_ge(s_in, 64)
            act(cT, cT, ACT.Silu).then_inc(s_silu, 1)
            act(sq, xT, ACT.Square).then_inc(s_sq, 1)
            rms(1)
            for c in range(4 * T_TILES):
                sc.wait_ge(s_proj, c + 1)
                if c < ROT:
                    if c >= 3:
                        sc.wait_ge(s_rope, c - 2)
                    act(qs[:, c % 3, :], banks[c % 4][:, 0:N], ACT.Copy).then_inc(s_pev, 1)
                elif c == ROT:
                    act(kvc[:, 3, :], banks[c % 4][:, 0:N], ACT.Copy).then_inc(s_pev, 1)
                else:
                    act(mT[:, c - 16, :], banks[c % 4][:, 0:N], ACT.Sigmoid).then_inc(s_pev, 1)
            for t, (t0, tn) in enumerate(TOK):
                sc.wait_ge(s_row, 4 + t)
                act(vS[0:tn, t, :], banks[t][0:tn, 0:256], ACT.Copy).then_inc(s_rowA, 1)
                act(gate[0:tn, t, :], banks[t][0:tn, 256:280], ACT.Sigmoid).then_inc(s_rowA, 1)
            sc.wait_ge(s_cp, 1)
            sc.wait_ge(s_pbv, 1)
            for v in range(2):
                for g in range(2):
                    act(glp[:, v, g, :], banks[6 - g][:, v * NCMPP:(v + 1) * NCMPP], ACT.Gelu_apprx_tanh,
                        bias=peb[:, v:v + 1]).then_inc(s_cpg, 1)
            for half in range(2):
                for v in range(2):
                    n = 2 * half + v
                    sc.wait_ge(s_cAB, 4 * half + 2 * v + 1)
                    if n:
                        sc.wait_ge(s_cS, n)
                    src = banks[2 * v][:, :].rearrange("p (b q g n) -> p b q g n", b=4, q=8, g=2)
                    for g in range(2):
                        m = act(hA[:, :, g, :].rearrange("p b (q n) -> p b q n", n=8), src[:, :, :, g, :], ACT.Copy)
                    m.then_inc(s_cA, 1)
                    sc.wait_ge(s_cS, n + 1)
                    if half:
                        sc.wait_ge(s_c2, v + 1)
                    act(gl[:, v].rearrange("p b g n -> p (b g n)"), hS.rearrange("p a n -> p (a n)"),
                        ACT.Gelu_apprx_tanh, bias=peb[:, v:v + 1]).then_inc(s_cg, 1)

            def p_exp(h):
                sc.wait_ge(s_nm, h + 1)
                for j in range(6):
                    seg = sP[j // 2][:, 0:128] if j % 2 == 0 else sP[j // 2][:, 128:384]
                    act(seg, seg, ACT.Exp, bias=st[:, 8 + j:9 + j], scale=SCALE, accum_out=st[:, 16 + j:17 + j])
                for c in range(2):
                    seg = sP[2][:, 384 + NCMPP * c:384 + NCMPP * (c + 1)]
                    m = act(seg, seg, ACT.Exp, bias=st[:, 14 + c:15 + c], scale=SCALE)
                m.then_inc(s_exp, 1)

            def p_out(h):
                g, r, hp, o = h // 4, h % 4, h // 2, DH * (h % 2)
                sc.wait_ge(s_tr, 3 * h + 1)
                if h:
                    sc.wait_ge(s_pv, 2 * h)
                act(ptC[0:NCMPP, 0:128], banks[3][0:NCMPP, 384:512], ACT.Copy)
                act(ptP[:, 0, :], banks[3][:, 0:384], ACT.Copy).then_inc(s_ptA, 1)
                sc.wait_ge(s_pv, 2 * h + 1)
                act(oTa[o:o + DH, hp, 0:NP_], banks[6][o:o + DH, 0:NP_], ACT.Copy).then_inc(s_oev, 1)
                sc.wait_ge(s_pv, 2 * h + 2)
                act(oTb[DH * g:DH * (g + 1), r, 0:NP_], banks[7][DH * g:DH * (g + 1), 0:NP_], ACT.Copy).then_inc(s_oev, 1)

            for h in range(H):
                p_exp(h)
                p_out(h)

            def smp_cmp_exp(i):
                sc.wait_ge(z_cm, i + 1)
                act(sC[:, 0:NCMP], sC[:, 0:NCMP], ACT.Exp, bias=st[:, 33:34], scale=SCALE,
                    accum_out=st[:, 34:35]).then_inc(z_ce, 1)

            def smp_exp(i):
                for j, (s, w) in enumerate(((sM, 1088), (sS, 1088), (sW, 576))):
                    sc.wait_ge(z_nm, 3 * i + j + 1)
                    act(s[:, 0:w], s[:, 0:w], ACT.Exp, bias=st[:, 40 + j:41 + j], scale=SCALE,
                        accum_out=st[:, 44 + j:45 + j]).then_inc(z_ex, 1)

            def smp_turned(i):
                for j in (0, 2, 4):
                    sc.wait_ge(z_tr, 6 * i + j + 1)
                    if i and j == 0:
                        sc.wait_ge(z_vd[1], i)
                    act(pt[:, j, :], banks[6][:, :], ACT.Copy).then_inc(z_tA, 1)

            def smp_out(i):
                sc.wait_ge(z_vd[1], i + 1)
                src = banks[7][:, 0:256].rearrange("p (b x n) -> p b x n", b=2, n=16)
                new = NP_ + 2 * NQ * i
                for u in range(2):
                    rows = slice(DH * u, DH * (u + 1))
                    act(oTa[rows, :, new:new + 16].rearrange("p h (b q) -> p b h q", b=2),
                        src[rows, :, 0:4, 8 * u:8 * u + 8], ACT.Copy)
                    m = act(oTb[rows, :, new:new + 16].rearrange("p h (b q) -> p b h q", b=2),
                            banks[7][rows, 0:256].rearrange("p (b x n) -> p b x n", b=2, n=8)[:, :, 8 + 4 * u:12 + 4 * u, :],
                            ACT.Copy)
                m.then_inc(z_oev, 1)

            smp_cmp_exp(0)
            for i in range(4):
                smp_exp(i)
                smp_turned(i)
                smp_out(i)
                if i + 1 < 4:
                    smp_cmp_exp(i + 1)

            sc.wait_ge(s_x1, KD)
            act(sq2, xT, ACT.Square).then_inc(s_sq2, 1)
            rms(2)
            sc.wait_ge(s_lc, 1)
            g4 = at(rt + 160, 4, 4)
            act(g4[0:RT], g4[0:RT], ACT.Exp).then_inc(s_le, 1)
            sc.wait_ge(s_l8, 1)
            e8 = at(rt + 400, 4, 8)
            act(e8[0:RT], e8[0:RT], ACT.Exp).then_inc(s_l8e, 1)
            for e in range(1, E, 2):
                sc.wait_ge(s_bc, e + 1)
                sc.wait_ge(s_bce, e)
                act(cbc[:, e, :], banks[2 + e % 2][:, 0:N], ACT.Copy).then_inc(s_bce, 1)
            sil = at(rt + 8640 - 2560, 2, N)

            def silu(s, j, first):
                sc.wait_ge(s_hid, s * 2 + 1)
                if not first:
                    sc.wait_ge(s_act, s - 1)
                act(sil[:, j, :], banks[6][:, 0:N], ACT.Silu).then_inc(s_sil, 1)

            silu(0, 0, True)
            silu(1, 1, True)
            with sc.Fori(1, E) as i:
                silu(i * 2, 0, False)
                silu(i * 2 + 1, 1, False)
            sc.wait_ge(s_ya, 1)
            for b in (1, 3, 5):
                t, (t0, tn) = b // 2, TOK[b // 2]
                sc.wait_ge(s_yr, b)
                act(yR[0:tn, t, 512:1024], banks[b][0:tn, :], ACT.Copy).then_inc(s_yr, 1)
            sc.wait_ge(s_x2, KD)
            act(sq2, xT, ACT.Square).then_inc(s_sq3, 1)
            rms(3)

        @block.vector
        def _(ve):
            chain = [0]

            def link(ins):
                chain[0] += 1
                ins.then_inc(s_ch, 1)
                ve.wait_ge(s_ch, chain[0])

            def modulated(dst, src, s, shift):
                for k in range(KD):
                    link(ve.tensor_scalar(dst[:, k, 0:NP_], src[:, k, 0:NP_], s[:, k, 0:1], shift[:, k, 0:1], ALU.mult, ALU.add))
                a = src[:, :, NP_:N].rearrange("p k (b q) -> p k b q", q=NQ)
                o = dst[:, :, NP_:N].rearrange("p k (b q) -> p k b q", q=NQ)
                wide = [P, KD, NB, NQ]
                link(ve.tensor_tensor(o, a, s[:, :, 1:NC].unsqueeze(3).to_broadcast(wide), ALU.mult))
                return ve.tensor_tensor(o, o, shift[:, :, 1:NC].unsqueeze(3).to_broadcast(wide), ALU.add)

            def root(total, n):
                ve.tensor_scalar(rstd, total, 1.0 / D, EPS, ALU.mult, ALU.add).then_inc(s_ms, 1)
                ve.wait_ge(s_rms, n)
                link(ve.reciprocal(rstd, rstd))

            def normed(dst):
                return ve.tensor_tensor(dst, xT, rstd.unsqueeze(1).to_broadcast([P, KD, N]), ALU.mult)

            ve.wait_ge(s_in, 64)
            ve.wait_ge(s_ss, 1)
            root(banks[7][:, 0:N], 1)
            link(normed(sq))
            for n in range(ADA_TILES):
                ve.wait_ge(s_ada, n + 1)
                ve.tensor_tensor(mod[:, 4 * n:4 * n + 4, :], banks[n % 3][:, 0:4 * NC].rearrange("p (c n) -> p c n", n=NC),
                                 vecs[:, 4 * n:4 * n + 4].unsqueeze(2).to_broadcast([P, 4, NC]), ALU.add).then_inc(s_mod, 1)
            ve.wait_ge(s_mod, ADA_TILES)
            for j in range(2):
                link(ve.scalar_tensor_tensor(scl[:, j], mod[:, 8 + 24 * j:16 + 24 * j, :], 1.0,
                                             gains[:, j].unsqueeze(2).to_broadcast([P, KD, NC]), ALU.add, ALU.mult))
            modulated(hT, sq, scl[:, 0], mod[:, 0:8, :]).then_inc(s_h, 1)
            dst = [qA[:, c] for c in range(4)] + [kA[:, c] for c in range(4)] + [qB[:, c] for c in range(4)] + [kvc[:, c] for c in range(3)]
            for c in range(ROT):
                ve.wait_ge(s_pev, c + 1)
                ve.wait_ge(s_rot, c + 1)
                ve.tensor_tensor(turn[:, c % 2, 0, :], qs[:, c % 3, :], cst[:, C_COS:C_COS + N], ALU.mult)
                link(ve.tensor_tensor(turn[:, c % 2, 1, :], banks[4 + c % 2][:, 0:N], cst[:, C_SIN:C_SIN + N], ALU.mult))
                ve.tensor_tensor(dst[c], turn[:, c % 2, 0, :], turn[:, c % 2, 1, :], ALU.add).then_inc(s_rope, 1)
            for t, (t0, tn) in enumerate(TOK):
                ve.wait_ge(s_row, t + 1)
                ve.tensor_copy(vA[0:tn, t, :], banks[4 + t][0:tn, :]).then_inc(s_rowV, 1)
            ve.wait_ge(s_pb, 1)
            ve.tensor_copy(peb, banks[7][:, 0:2]).then_inc(s_pbv, 1)
            ve.wait_ge(s_cp2, 1)
            ve.tensor_copy(kcmp, banks[7][:, 0:NCMPP]).then_inc(s_cpe, 1)
            ve.wait_ge(s_cp2, 2)
            ve.tensor_copy(vcmp[0:NCMPP, :], banks[6][0:NCMPP, 0:P]).then_inc(s_cpe, 1)
            for half in range(2):
                for v in range(2):
                    n = 2 * half + v
                    ve.wait_ge(s_cAB, 4 * half + 2 * v + 2)
                    if n:
                        ve.wait_ge(s_cS, n)
                    src = banks[2 * v + 1][:, :].rearrange("p (b q g n) -> p b q g n", b=4, q=8, g=2)
                    for g in range(2):
                        m = ve.tensor_copy(hB[:, :, g, :].rearrange("p b (q n) -> p b q n", n=8), src[:, :, :, g, :])
                    m.then_inc(s_cB, 1)
                    ve.wait_ge(s_cB, n + 1)
                    ve.wait_ge(s_cA, n + 1)
                    if n:
                        ve.wait_ge(s_cg, n)
                    ve.tensor_tensor(hS, hA.rearrange("p b g n -> p (b g) n")[:, :, 0:63],
                                     hB.rearrange("p b g n -> p (b g) n")[:, :, 1:64], ALU.add).then_inc(s_cS, 1)
                ve.wait_ge(s_c2, 2 * half + 1)
                ve.tensor_copy(kcm[:, 4 * half:4 * half + 4, :],
                               banks[4][:, 0:4 * NCMP].rearrange("p (b n) -> p b n", n=NCMP)).then_inc(s_kcm, 1)
                ve.wait_ge(s_c2, 2 * half + 2)
                ve.tensor_copy(vcm[0:NCMP, 4 * half:4 * half + 4, :],
                               banks[5][0:NCMP, :].rearrange("p (b n) -> p b n", n=P)).then_inc(s_kcm, 1)

            ve.wait_ge(s_rowA, 6)

            def p_max(h):
                for kind in range(3):
                    ve.wait_ge(s_sc, 3 * h + kind + 1)
                    if h:
                        ve.wait_ge(s_tr, 3 * h)
                    if kind == 2:
                        ve.tensor_tensor(sP[2][:, 384:414], banks[2][:, 384:414], cst[:, C_CADD:C_CADD + 30], ALU.add)
                    ve.tensor_tensor(sP[kind][:, 0:384], banks[kind][:, 0:384], cst[:, C_TRI:C_TRI + 384], ALU.add)\
                        .then_inc(s_sev, 1)
                    ve.wait_ge(s_sev, 3 * h + kind + 1)
                    ve.tensor_reduce(st[:, 2 * kind:2 * kind + 1], sP[kind][:, 0:128], AX, ALU.max)
                    m = ve.tensor_reduce(st[:, 2 * kind + 1:2 * kind + 2], sP[kind][:, 128:384], AX, ALU.max)
                link(ve.tensor_reduce(st[:, 6:8], sP[2][:, 384:414].rearrange("p (c n) -> p c n", n=NCMPP), AX, ALU.max))
                ve.tensor_scalar(st[:, 8:16], st[:, 0:8], -SCALE, None, ALU.mult).then_inc(s_nm, 1)

            def p_recip(h):
                ve.wait_ge(s_exp, h + 1)
                link(ve.tensor_tensor(sP[2][:, 384:414], sP[2][:, 384:414], cst[:, C_C01:C_C01 + 30], ALU.mult))
                link(ve.tensor_reduce(st[:, 22:24], sP[2][:, 384:414].rearrange("p (c n) -> p c n", n=NCMPP), AX, ALU.add))
                link(ve.tensor_scalar(st[:, 16:24], st[:, 16:24], TINY, None, ALU.max))
                link(ve.reciprocal(st[:, 24:32], st[:, 16:24]))
                w = st[:, 26:32].rearrange("p (j t) -> p j t", t=2)
                ve.tensor_tensor(w, w, gate[:, 0:2, 3 * h:3 * h + 3].rearrange("p t j -> p j t"), ALU.mult).then_inc(s_r, 1)

            def p_turned(h):
                for kind in (1, 2):
                    ve.wait_ge(s_tr, 3 * h + kind + 1)
                    if h:
                        ve.wait_ge(s_pv, 2 * h)
                    if kind == 1:
                        ve.tensor_copy(ptC[0:NCMPP, 128:256], banks[4][0:NCMPP, 384:512])
                    ve.tensor_copy(ptP[:, kind, :], banks[3 + kind][:, 0:384]).then_inc(s_ptD, 1)

            for h in range(H):
                p_max(h)
                p_recip(h)
                p_turned(h)

            ve.wait_ge(s_tr, 3 * H)
            ve.wait_ge(s_pv, 2 * H)
            link(ve.memset(qz, 0.0))
            link(ve.memset(qzb, 0.0))
            link(ve.memset(pcn, 0.0))
            link(ve.memset(pcg, 0.0))
            ve.wait_ge(s_gs, 16 * 16)

            def smp_blocks(i):
                if i:
                    ve.wait_ge(z_small, i)
                new = NP_ + 2 * NQ * i
                for hp in range(4):
                    for u in range(2):
                        rows = slice(DH * u, DH * (u + 1))
                        ve.tensor_copy(qz[rows, :, hp, 16 * hp + 8 * u:16 * hp + 8 * u + 8],
                                       qA[rows, hp, new:new + 16].rearrange("p (b q) -> p b q", b=2))
                for g in range(2):
                    for b in range(2):
                        rows = slice(DH * g, DH * (g + 1))
                        m = ve.tensor_copy(qzb[rows, b, 32 * g:32 * g + 32].rearrange("p (r q) -> p r q", q=NQ),
                                           qB[rows, :, new + 8 * b:new + 8 * b + 8])
                m.then_inc(z_qz, 1)

            def dropped(src, n):
                d, e, pen = st[:, 50:51], at(B + 6740, 16)[:, 0:n], at(B + 6756, 16)[:, 0:n]
                link(ve.tensor_reduce(d, src, AX, ALU.min))
                link(ve.scalar_tensor_tensor(e, src, d, idx[:, 0:n], ALU.is_equal, ALU.mult))
                link(ve.tensor_reduce(st[:, 51:52], e, AX, ALU.max))
                link(ve.tensor_scalar(pen, idx[:, 0:n], st[:, 51:52], NEG, ALU.is_equal, ALU.mult))
                return pen

            def smp_max(i):
                ve.wait_ge(z_small, i + 1)
                new = cst[:, C_NEW + NS * i:C_NEW + NS * (i + 1)]
                link(ve.tensor_copy(sC[:, 0:NCMP], banks[5][:, 192:192 + NCMP]))
                link(ve.tensor_reduce(st[:, 32:33], sC[:, 0:NCMP], AX, ALU.max))
                ve.tensor_scalar(st[:, 33:34], st[:, 32:33], -SCALE, None, ALU.mult).then_inc(z_cm, 1)
                ve.tensor_tensor(sM[:, 1024:1088], banks[5][:, 0:64], new, ALU.add)
                ve.tensor_tensor(sS[:, 1024:1088], banks[5][:, 64:128], new, ALU.add)
                ve.tensor_tensor(sW[:, 512:576], banks[5][:, 128:192], new, ALU.add)
                ve.tensor_tensor(sW[:, 0:8], banks[4][:, 0:8], cst[:, C_WIN:C_WIN + 8], ALU.add)
                link(ve.tensor_copy(sW[:, 8:512], banks[4][:, 8:512]))
                g4 = st[:, 52:56]
                for half in range(2):
                    link(ve.tensor_reduce(g4[:, 2 * half:2 * half + 2], banks[half][:, :].rearrange("p (j n) -> p j n", n=256),
                                          AX, ALU.add))
                pen = dropped(g4, 4)
                for half in range(2):
                    link(ve.tensor_tensor(sM[:, 512 * half:512 * (half + 1)].rearrange("p (j n) -> p j n", n=256),
                                          banks[half][:, :].rearrange("p (j n) -> p j n", n=256),
                                          pen[:, 2 * half:2 * half + 2].unsqueeze(2).to_broadcast([P, 2, 256]), ALU.add))
                link(ve.tensor_reduce(st[:, 36:37], sM, AX, ALU.max))
                ve.tensor_scalar(st[:, 40:41], st[:, 36:37], -SCALE, None, ALU.mult).then_inc(z_nm, 1)
                ve.wait_ge(z_ce, i + 1)
                link(ve.tensor_scalar(st[:, 34:35], st[:, 34:35], TINY, None, ALU.max))
                link(ve.reciprocal(st[:, 35:36], st[:, 34:35]))
                ve.tensor_scalar(pcn[:, 1:1 + NCMP], sC[:, 0:NCMP], st[:, 35:36], None, ALU.mult).then_inc(z_pcn, 1)
                link(ve.tensor_reduce(st[:, 38:39], sW, AX, ALU.max))
                ve.wait_ge(z_imp, i + 1)
                imp = at(B + 6772, 16)
                grp = at(B + 6788, 66)
                link(ve.tensor_copy(grp[:, 0:65], banks[5][:, 256:321]))
                link(ve.tensor_reduce(imp, grp[:, 0:64].rearrange("p (j n) -> p j n", n=4), AX, ALU.add))
                link(ve.tensor_tensor(imp, imp, grp[:, 4:65:4], ALU.add))
                pen = dropped(imp, 16)
                for half in range(2):
                    m = ve.tensor_tensor(sS[:, 512 * half:512 * (half + 1)].rearrange("p (j n) -> p j n", n=64),
                                         banks[2 + half][:, :].rearrange("p (j n) -> p j n", n=64),
                                         pen[:, 8 * half:8 * half + 8].unsqueeze(2).to_broadcast([P, 8, 64]), ALU.add)
                m.then_inc(z_sev, 1)
                ve.wait_ge(z_sev, i + 1)
                link(ve.tensor_reduce(st[:, 37:38], sS, AX, ALU.max))
                ve.tensor_scalar(st[:, 41:42], st[:, 37:38], -SCALE, None, ALU.mult).then_inc(z_nm, 1)
                ve.tensor_scalar(st[:, 42:43], st[:, 38:39], -SCALE, None, ALU.mult).then_inc(z_nm, 1)

            def smp_recip(i):
                ve.wait_ge(z_ex, 3 * i + 3)
                link(ve.tensor_scalar(st[:, 44:47], st[:, 44:47], TINY, None, ALU.max))
                link(ve.reciprocal(st[:, 56:59], st[:, 44:47]))
                ve.tensor_tensor(st[:, 57:59], st[:, 57:59], gateS[:, i, 0:2], ALU.mult).then_inc(z_rr, 1)
                ve.wait_ge(z_rr, i + 1)
                ve.tensor_scalar(pcg[:, 0:NCMP], pcn[:, 1:1 + NCMP], gateS[:, i, 2:3], None, ALU.mult)
                ve.tensor_scalar(sW, sW, st[:, 58:59], None, ALU.mult).then_inc(z_nd, 1)

            def smp_turned(i):
                for j in (1, 3, 5):
                    ve.wait_ge(z_tr, 6 * i + j + 1)
                    if i and j == 1:
                        ve.wait_ge(z_vd[1], i)
                    if j < 5:
                        ve.tensor_copy(pt[:, j, :], banks[6][:, :]).then_inc(z_tD, 1)
                    else:
                        ve.tensor_copy(pt[0:64, j, :], banks[6][0:64, :]).then_inc(z_tD, 1)

            smp_blocks(0)
            for i in range(4):
                smp_max(i)
                if i + 1 < 4:
                    smp_blocks(i + 1)
                smp_recip(i)
                smp_turned(i)

            for c in range(KD):
                ve.wait_ge(s_br, c + 1)
                ve.tensor_tensor(mT[:, c, :], mT[:, c, :], banks[2 * (c % 2)][:, 0:N], ALU.mult)
                link(ve.tensor_tensor(mT[:, 8 + c, :], mT[:, 8 + c, :], banks[2 * (c % 2) + 1][:, 0:N], ALU.mult))
                ve.tensor_tensor(mT[:, c, :], mT[:, c, :], mT[:, 8 + c, :], ALU.add).then_inc(s_mg, 1)
            tmp = at(PJ, NS)

            def residual(c, bank, g0, s):
                if c:
                    ve.wait_ge(s, c)
                ve.scalar_tensor_tensor(xT[:, c, 0:NP_], bank[:, 0:NP_], mod[:, g0 + c, 0:1], xT[:, c, 0:NP_], ALU.mult, ALU.add)
                link(ve.tensor_tensor(tmp.rearrange("p (b q) -> p b q", q=NQ), bank[:, NP_:N].rearrange("p (b q) -> p b q", q=NQ),
                                      mod[:, g0 + c, 1:NC].unsqueeze(2).to_broadcast([P, NB, NQ]), ALU.mult))
                ve.tensor_tensor(xT[:, c, NP_:N], xT[:, c, NP_:N], tmp, ALU.add).then_inc(s, 1)

            for c in range(KD):
                ve.wait_ge(s_op, c + 1)
                residual(c, banks[4 + c % 2], 16, s_x1)
            ve.wait_ge(s_ss2, 1)
            root(banks[7][:, 0:N], 2)
            link(normed(moe_in))
            modulated(moe_in, moe_in, scl[:, 1], mod[:, 24:32, :]).then_inc(s_h2, 1)

            ve.wait_ge(s_lg, 1)
            R = slice(0, RT)
            lg = at(rt, 4, 36)
            g4 = at(rt + 160, 4, 4)
            e8 = at(rt + 400, 4, 8)
            oh = at(rt + 180, 4, 4)
            m1 = at(rt + 200, 4)
            gw = at(rt + 204, 4)
            v2 = at(rt + 208, 4)
            big = at(rt + 240, 4, 8, 4)
            oh1, oh2, e2 = at(rt + 440, 4, 8), at(rt + 480, 4, 8), at(rt + 520, 4, 8)
            comb = at(rt + 800, 4, E)

            def wide(ap, n):
                return ap[R].unsqueeze(2).to_broadcast([RT, 4, n])

            def first_best(dst, src, best, n):
                down = idx[R, 0:n].unsqueeze(1).to_broadcast([RT, 4, n])
                link(ve.tensor_tensor(dst[R], src[R], wide(best, n), ALU.is_equal))
                link(ve.tensor_tensor(e2[R, :, 0:n], dst[R], down, ALU.mult))
                link(ve.scalar_tensor_tensor(dst[R], dst[R], 64.0, e2[R, :, 0:n], ALU.mult, ALU.subtract))
                link(ve.tensor_reduce(m1[R], dst[R], AX, ALU.max))
                link(ve.tensor_tensor(dst[R], dst[R], wide(m1, n), ALU.is_equal))

            link(ve.tensor_copy(lg[R], banks[0][R, 0:144].rearrange("p (t n) -> p t n", n=36)))
            link(ve.tensor_reduce(m1[R], lg[R, :, 0:4], AX, ALU.max))
            ve.tensor_tensor(g4[R], lg[R, :, 0:4], wide(m1, 4), ALU.subtract).then_inc(s_lc, 1)
            ve.wait_ge(s_le, 1)
            link(ve.tensor_reduce(gw[R], g4[R], AX, ALU.add))
            link(ve.reciprocal(gw[R], gw[R]))
            link(ve.tensor_reduce(v2[R], g4[R], AX, ALU.max))
            first_best(oh, g4, v2, 4)
            for t in range(4):
                m = ve.tensor_tensor(big[R, t], lg[R, t, 4:36].rearrange("p (g e) -> p e g", e=8),
                                     oh[R, t].unsqueeze(1).to_broadcast([RT, 8, 4]), ALU.mult)
            link(m)
            link(ve.tensor_reduce(e8[R], big[R], AX, ALU.add))
            link(ve.tensor_reduce(m1[R], e8[R], AX, ALU.max))
            ve.tensor_tensor(e8[R], e8[R], wide(m1, 8), ALU.subtract).then_inc(s_l8, 1)
            ve.wait_ge(s_l8e, 1)
            link(ve.tensor_reduce(v2[R], e8[R], AX, ALU.max))
            first_best(oh1, e8, v2, 8)
            rest = at(rt + 560, 4, 8)
            link(ve.scalar_tensor_tensor(rest[R], oh1[R], -4.0, e8[R], ALU.mult, ALU.add))
            link(ve.tensor_reduce(v2[R], rest[R], AX, ALU.max))
            first_best(oh2, rest, v2, 8)
            tot, w1_, w2_ = at(rt + 212, 4), at(rt + 216, 4), at(rt + 220, 4)
            link(ve.tensor_tensor(oh2[R], oh2[R], wide(v2, 8), ALU.mult))
            link(ve.tensor_scalar(tot[R], v2[R], 1.0, None, ALU.add))
            link(ve.reciprocal(tot[R], tot[R]))
            link(ve.tensor_tensor(oh1[R], oh1[R], oh2[R], ALU.add))
            link(ve.tensor_tensor(tot[R], tot[R], gw[R], ALU.mult))
            link(ve.tensor_tensor(oh1[R], oh1[R], wide(tot, 8), ALU.mult))
            for t in range(4):
                m = ve.tensor_tensor(comb[R, t].rearrange("p (g e) -> p g e", e=8), oh1[R, t].unsqueeze(1).to_broadcast([RT, 4, 8]),
                                     oh[R, t].unsqueeze(2).to_broadcast([RT, 4, 8]), ALU.mult)
            m.then_inc(s_cb, 1)
            ve.wait_ge(s_cbt, 1)
            ve.tensor_copy(at(rt + 930, N)[0:E, :], banks[1][0:E, 0:N]).then_inc(s_cbr, 1)
            for e in range(0, E, 2):
                ve.wait_ge(s_bc, e + 1)
                if e:
                    ve.wait_ge(s_bce, e)
                ve.tensor_copy(cbc[:, e, :], banks[2 + e % 2][:, 0:N]).then_inc(s_bce, 1)

            acts = at(rt + 8000 - 2560, 2, N)
            sil = at(rt + 8640 - 2560, 2, N)
            half = at(rt + 9280 - 2560, 2, N)

            def gated(s, j, e, first):
                ve.wait_ge(s_hid, s * 2 + 2)
                ve.tensor_tensor(half[:, j, :], banks[7][:, 0:N], cbc[:, e, :].rearrange("p o n -> p (o n)"), ALU.mult).then_inc(s_gb, 1)
                ve.wait_ge(s_gb, s + 1)
                ve.wait_ge(s_sil, s + 1)
                ve.tensor_tensor(acts[:, j, :], sil[:, j, :], half[:, j, :], ALU.mult).then_inc(s_act, 1)

            ve.wait_ge(s_bce, E)
            gated(0, 0, slice(0, 1), True)
            gated(1, 1, slice(0, 1), True)
            with ve.Fori(1, E) as i:
                gated(i * 2, 0, bass.ds(i, 1), False)
                gated(i * 2 + 1, 1, bass.ds(i, 1), False)
            ve.wait_ge(s_ya, 1)
            for b in (0, 2, 4):
                t, (t0, tn) = b // 2, TOK[b // 2]
                if b:
                    ve.wait_ge(s_yr, b)
                ve.tensor_copy(yR[0:tn, t, 0:512], banks[b][0:tn, :]).then_inc(s_yr, 1)
            for c in range(KD):
                ve.wait_ge(s_yt, c + 1)
                residual(c, banks[6 + c % 2], 40, s_x2)
            ve.wait_ge(s_ss3, 1)
            root(banks[0][:, 0:N], 3)
            link(normed(xT))
            ve.tensor_tensor(xT, xT, gains[:, 2].unsqueeze(2).to_broadcast([P, KD, N]), ALU.mult).then_inc(s_fin, 1)

        @block.gpsimd
        def _(po):
            zeros = at(B + 6900, 256)
            po.memset(zeros, 0.0).then_inc(s_z, 1)
            po.dma_start(o_win[0], win_state[0]).then_inc(s_out, 16)
            po.dma_start(o_win[1], win_state[1]).then_inc(s_out, 16)
            po.wait_ge(s_z, 1)
            po.dma_start(o_zero, zeros).then_inc(s_out, 16)
            po.wait_ge(s_rope, ROT)
            po.dma_start(o_kt, kA).then_inc(s_out, 16)
            po.wait_ge(s_pev, ROT + 1)
            po.dma_start(o_small, kvc).then_inc(s_out, 16)
            po.wait_ge(s_rowV, 3)
            po.dma_start(o_va[:, 0:2, :], vA[:, 0:2, :]).then_inc(s_out, 16)
            po.dma_start(o_va[0:64, 2, :], vA[0:64, 2, :]).then_inc(s_out, 16)
            po.wait_ge(s_rowA, 6)
            po.dma_start(o_vs[:, 0:2, :], vS[:, 0:2, :]).then_inc(s_out, 16)
            po.dma_start(o_vs[0:64, 2, :], vS[0:64, 2, :]).then_inc(s_out, 16)
            po.dma_start(scratch, gate[0:NS, 2, :]).then_inc(s_gd, 16)
            po.wait_ge(s_gd, 16)
            by_head = scratch.rearrange("(i b q) (h j) -> b h q i j", b=2, q=NQ, j=3)
            for b in range(2):
                for h in range(H):
                    row = 64 * b + 8 * h
                    po.dma_start(gateS[row:row + 8, :, :], by_head[b, h]).then_inc(s_gs, 16)

            for h in range(H):
                po.wait_ge(s_r, h + 1)
                for j in range(6):
                    seg = sP[j // 2][:, 0:128] if j % 2 == 0 else sP[j // 2][:, 128:384]
                    po.tensor_scalar(seg, seg, st[:, 24 + j:25 + j], None, ALU.mult)
                for c in range(2):
                    seg = sP[2][:, 384 + NCMPP * c:384 + NCMPP * (c + 1)]
                    m = po.tensor_scalar(seg, seg, st[:, 30 + c:31 + c], None, ALU.mult)
                m.then_inc(s_nrm, 1)
            for i in range(4):
                po.wait_ge(z_rr, i + 1)
                for j, s in enumerate((sM, sS)):
                    po.tensor_scalar(s, s, st[:, 56 + j:57 + j], None, ALU.mult).then_inc(z_np, 1)


def constants():
    import numpy as np
    c = np.zeros((P, C_ALL), np.float32)
    r = np.arange(P)
    c[:, C_ID:C_ID + P] = np.eye(P)
    tri = np.where(r[None, :] <= r[:, None], 0.0, NEG)
    c[:, C_TRI:C_TRI + P] = tri
    c[:, C_TRI + 256:C_TRI + 384] = tri
    b2, g, q = r // 64, (r % 64) // 32, r % 8
    c[:, C_R:C_R + P] = (b2[:, None] == b2) & (g[:, None] == g) & (q[:, None] == q)
    for i in range(4):
        tok = np.arange(NS)
        ok = (tok[None, :] // NQ == (2 * i + b2)[:, None]) & (tok[None, :] % NQ <= q[:, None])
        c[:, C_NEW + NS * i:C_NEW + NS * (i + 1)] = np.where(ok, 0.0, NEG)
    c[:, C_WIN:C_WIN + 8] = np.where(np.arange(8)[None, :] >= q[:, None], 0.0, NEG)
    for t in range(2):
        ok = (np.arange(NCMPP) * 16 + 31)[None, :] <= (r + P * t)[:, None]
        c[:, C_CADD + NCMPP * t:C_CADD + NCMPP * (t + 1)] = np.where(ok, 0.0, NEG)
        c[:, C_C01 + NCMPP * t:C_C01 + NCMPP * (t + 1)] = ok
    c[:, C_IDX:C_IDX + 16] = np.arange(1, 17)
    c[:, C_ONE:C_ONE + P] = 1.0
    c[(r // 64) * 64 + (r % 64 + 32) % 64, C_PERM + r] = 1.0
    pos = np.concatenate([np.arange(NP_), np.tile(1024 + np.arange(NQ), NB)]).astype(np.float32)
    inv = np.float32(10000.0) ** (-np.arange(32, dtype=np.float32) / np.float32(32))
    ang = (inv[r % 32][:, None] * pos[None, :]).astype(np.float32)
    c[:, C_COS:C_COS + N] = np.cos(ang)
    c[:, C_SIN:C_SIN + N] = np.sin(ang) * np.where(r % 64 < 32, -1.0, 1.0)[:, None]
    return c


def kernel(**inputs):
    import numpy as np
    import concourse.bacc as _bacc
    from concourse.bass_utils import run_bass_kernel_spmd as _run

    a = {k: np.asarray(v) for k, v in inputs.items()}
    c_ = np.ascontiguousarray

    def kp(w):
        return w.reshape(-1, P, w.shape[-1]).transpose(1, 0, 2)

    cond = np.concatenate([a["c_prompt"], a["c_sample"]]).T
    xt = np.concatenate([a["x_prompt"].reshape(-1, D), a["x_sample"].reshape(-1, D)]).T
    w1 = [a["w_cmp_k1"][0], a["w_cmp_v1"][0]]
    vec = np.concatenate([
        a["b_ada"][0].reshape(48, P).T,
        np.stack([a["norm_mix_g"][0], a["norm_ffn_g"][0], a["norm_final_g"]]).reshape(3 * KD, P).T,
        a["w_cmp_k2"][0], a["w_cmp_v2"][0],
        a["pe_cmp_k"][0].reshape(16, P).T, a["pe_cmp_v"][0].reshape(16, P).T,
        kp(np.concatenate([a["w_router_grp"][0], a["w_router_exp"][0]], axis=1)).reshape(P, -1),
        kp(cond).reshape(P, -1)], axis=1)
    w = a["w_in"][0]
    q_b = w[:, 1536:2048].reshape(D, 2, 4, DH).transpose(0, 2, 1, 3).reshape(D, 512)
    gates = w[:, 2816:2840].reshape(D, H, 3)[:, :, [1, 2, 0]].reshape(D, GATES)
    turned = np.concatenate([w[:, 0:1024], q_b, w[:, 2048:2176], w[:, 2304:2432], w[:, 2560:2688],
                             w[:, 2176:2304], w[:, 2840:4888]], axis=1)
    rows = np.concatenate([w[:, 1024:1536], w[:, 2432:2560], w[:, 2688:2816], gates,
                           np.zeros((D, 232), w.dtype)], axis=1)
    w_in = kp(np.concatenate([turned, rows], axis=1)).reshape(P, KD, 10, 512).transpose(2, 0, 1, 3)

    def pages_t(x):
        x = x[0].reshape(NPHYS, PAGE, -1, P)
        return x.transpose(0, 3, 2, 1).reshape(NPHYS, P, -1)

    def pages_c(x):
        x = x[0].reshape(NPHYS, 8, 8, 2, 2, DH)
        return x.transpose(0, 3, 5, 2, 4, 1).reshape(NPHYS, P, P)

    ins = {
        "vec": vec, "x_t": kp(xt), "pages": a["page_table"].reshape(1, -1).astype(np.int32),
        "w_ada": kp(a["w_ada"][0]).reshape(P, KD, ADA_TILES, 512).transpose(2, 0, 1, 3),
        "w_in": w_in,
        "w1": np.stack([kp(x) for x in w1], axis=1),
        "w1d": np.stack([np.concatenate([x.reshape(32, DH, P).transpose(1, 0, 2)] * 2, axis=0) for x in w1]),
        "cmp_pages": np.concatenate([pages_c(a["cache_nsa_cmp_k"]), pages_c(a["cache_nsa_cmp_v"])], axis=2),
        "k_pages": np.concatenate([pages_t(a["cache_moba_k"]), pages_t(a["cache_nsa_slc_k"])], axis=2),
        "v_pages": np.concatenate([a["cache_moba_v"][0].reshape(NPHYS, PAGE, 512),
                                   a["cache_nsa_slc_v"][0].reshape(NPHYS, PAGE, P)], axis=2),
        "win": np.stack([a["state_nsa_win_k"][0].reshape(NB, WIN, P).transpose(0, 2, 1),
                         a["state_nsa_win_v"][0].reshape(NB, 4, P, P).transpose(0, 2, 1, 3).reshape(NB, P, WIN)]),
        "w_br": kp(np.concatenate([a["w_br_a"][0],
                                   a["w_br_b"][0].reshape(2, 4, DH, D).transpose(1, 0, 2, 3).reshape(512, D)])),
        "w_out": kp(a["w_out"][0]),
        "w_moe": np.concatenate([a["w_expert_in"][0].reshape(E, KD, P, 512).transpose(0, 2, 1, 3).reshape(E, P, -1),
                                 a["w_expert_out"][0].reshape(E, 2, P, D).transpose(0, 2, 1, 3).reshape(E, P, -1)], axis=2),
        "consts": constants(),
        "win_state": np.stack([a["state_nsa_win_k"][0].reshape(NB, WIN, P)[:, NQ:],
                               a["state_nsa_win_v"][0].reshape(NB, WIN, P)[:, NQ:]]).reshape(2, -1, 1008),
    }
    outs = {"y": (P, KD, N), "kt": (P, 4, N), "small": (P, 4, N), "va": (P, 3, 512), "vs": (P, 3, 256),
            "zero": (P, 256), "win_new": (2, 512, 1008)}
    nc = _bacc.Bacc("TRN2", target_bir_lowering=False, num_devices=1)
    args, arrays = [], {}
    for name, x in ins.items():
        arrays[f"in_{name}"] = c_(x)
        args.append(nc.dram_tensor(f"in_{name}", x.shape, mybir.dt.from_np(x.dtype), kind="ExternalInput").ap())
    for name, shape in outs.items():
        args.append(nc.dram_tensor(f"out_{name}", shape, F32, kind="ExternalOutput").ap())
    args.append(nc.dram_tensor("gates_scratch", (NS, GATES), F32, kind="Internal").ap())
    build(nc, *args)
    got = _run(nc, [arrays], core_ids=[0]).results[0]
    y = got["out_y"].transpose(2, 1, 0).reshape(N, D)
    kt = got["out_kt"].transpose(2, 1, 0).reshape(N, 512)
    kc, ks, kw, vc = (got["out_small"][:, j, :].T for j in range(4))
    va = got["out_va"].transpose(1, 0, 2).reshape(3 * P, 512)[:N]
    vsw = got["out_vs"].transpose(1, 0, 2).reshape(3 * P, 256)[:N]
    vs, vw = vsw[:, 0:128], vsw[:, 128:256]
    zero = got["out_zero"].reshape(256, 128)
    old = got["out_win_new"].reshape(2, NB, WIN - NQ, P)

    def p_(x):
        return c_(x[:NP_].reshape(1, 1, NP_, -1, DH))

    def s_(x):
        return c_(x[NP_:].reshape(1, NB, NQ, -1, DH))

    def pw(x):
        return c_(np.concatenate([zero, x[:NP_]]).reshape(1, 1, WIN, 2, DH))

    def sw(j, x):
        return c_(np.concatenate([old[j], x[NP_:].reshape(NB, NQ, P)], axis=1).reshape(1, NB, WIN, 2, DH))

    return (c_(y[:NP_].reshape(1, NP_, D)), c_(y[NP_:].reshape(NB, NQ, D)),
            p_(kt), p_(va), p_(kc), p_(vc), p_(ks), p_(vs), pw(kw), pw(vw),
            s_(kt), s_(va), s_(kc), s_(vc), s_(ks), s_(vs), sw(0, kw), sw(1, vw))
```

```python
from contextlib import ExitStack

import concourse.bass as bass
from concourse import mybir

F32 = mybir.dt.float32
I32 = mybir.dt.int32
ALU = mybir.AluOpType
ACT = mybir.ActivationFunctionType
AX = mybir.AxisListType.X

P = 128
D = 1024
KD = D // P
NP_, NB, NQ = 256, 8, 8
NS = NB * NQ
N = NP_ + NS
NC = 1 + NB
PAGES = 8
PAGE = 128
NPHYS = 80
H = 8
DH = 64
NCMP = 63
NCMPP = 15
E = 32
EPS = 1e-6
TINY = 1e-30
NEG = -1e30
SCALE = DH ** -0.5
WIN = 512
TOK = [(0, 128), (128, 128), (256, 64)]
GATES = 3 * H
ADA_TILES = 12
T_TILES = 8
ROT = 15
SLOT = KD * 512
RT = 80
CAP = 64
EXTRA = 10
PAIRS = E // 2

C_ID, C_TRI, C_R, C_NEW = 0, 128, 512, 640
C_WIN = C_NEW + 4 * NS
C_CADD = C_WIN + 8
C_C01 = C_CADD + 2 * NCMPP
C_IDX = C_C01 + 2 * NCMPP
C_ONE = C_IDX + 16
C_PERM = C_ONE + 128
C_COS = C_PERM + 128
C_SIN = C_COS + N
C_LT = C_SIN + N
C_E = C_LT + 128
C_K = C_E + E
C_SEL = C_K + EXTRA
C_ALL = C_SEL + NC
V_B, V_G = 0, 48
V_W2K = V_G + 3 * KD
V_W2V = V_W2K + DH
V_PE = V_W2V + DH
V_WR = V_PE + 32
V_C = V_WR + KD * 36
V_ALL = V_C + KD * NC


def build(nc, vec, x_t, pages, w_ada, w_in, w1, cmp_pages, k_pages, v_pages, win, w_br, w_out,
          w_ein, w_eout, consts, win_state,
          o_y, o_kt, o_small, o_va, o_vs, o_zero, o_win, scratch, x_rows, y_rows):
    with ExitStack() as ctx:
        def sem(name):
            return ctx.enter_context(nc.semaphore(name))

        TOTAL = 53000
        arena = ctx.enter_context(nc.sbuf_tensor("arena", [P, TOTAL], F32))
        index = ctx.enter_context(nc.sbuf_tensor("expert_rows", [RT, 8], I32))
        extra = ctx.enter_context(nc.sbuf_tensor("extra_tiles", [1, 1 + EXTRA], I32))
        page_row = ctx.enter_context(nc.sbuf_tensor("page_row", [1, NB * PAGES], I32))
        banks = [ctx.enter_context(nc.psum_tensor(f"bank{i}", [P, 512], F32)) for i in range(8)]

        def at(off, *dims):
            size = 1
            for d in dims:
                size *= d
            assert off + size <= TOTAL, (off, size)
            ap = arena[:, off:off + size]
            if len(dims) == 2:
                return ap.rearrange("p (a b) -> p a b", b=dims[1])
            if len(dims) == 3:
                return ap.rearrange("p (a b c) -> p a b c", b=dims[1], c=dims[2])
            if len(dims) == 4:
                return ap.rearrange("p (a b c d) -> p a b c d", b=dims[1], c=dims[2], d=dims[3])
            return ap

        place = [0]

        def keep(*dims):
            size = 1
            for d in dims:
                size *= d
            place[0] += size
            return at(place[0] - size, *dims)

        cst = keep(C_ALL)
        vecs = keep(V_ALL)
        mod = keep(48, NC)
        scl = keep(2, KD, NC)
        xT = keep(KD, N)
        mT = keep(16, N)
        OT = place[0]
        oTa = keep(4, N)
        oTb = keep(4, N)
        rstd = keep(N)
        sample_part = keep(NS)
        assert place[0] <= 15000, place[0]
        PJ = place[0]
        qA, kA, qB = keep(4, N), keep(4, N), keep(4, N)
        kvc = keep(4, N)
        vA = keep(3, 512)
        vS = keep(3, 256)
        gate = keep(3, GATES)
        gateS = keep(4, 3)
        kcm = keep(NB, NCMP)
        vcm = keep(NB, P)
        kcmp, vcmp = keep(NCMPP), keep(P)
        A = place[0]
        sq = at(A, KD, N)
        hT = at(A + 2560, KD, N)
        ring = [at(A + 5120 + SLOT * k, KD, 512) for k in range(3)]
        qs = at(A + 5120 + 3 * SLOT, 3, N)
        turn = at(A + 5120 + 3 * SLOT + 3 * N, 2, 2, N)
        condS = at(A + 5120 + 3 * SLOT, KD, 64)
        adaR = [at(A + 5120 + 3 * SLOT + 3 * N + 512 * k, 512) for k in range(2)]
        kx = at(A + 5120 + 3 * SLOT + 3 * N, 2, 2, P)
        w1_sb = [at(A, 16, P), at(OT, 16, P)]
        XCO = A + 5120 + 3 * SLOT + 7 * N
        xc = [at(XCO, 32, 256), at(A + 5376, 32, 256)]
        HC = A + 2560
        hA, hB, hS = at(HC, 4, 2, 64), at(HC + 512, 4, 2, 64), at(HC + 1024, 8, 63)
        gl = at(HC + 1536, 2, 4, 2, 63)
        glp = at(HC + 2544, 2, 2, NCMPP)
        peb = at(HC + 2604, 2)
        UNIT = PAGES * 640 + WIN
        kU = [at(A + UNIT * b, UNIT) for b in range(2)]
        vU = [at(A + UNIT * (2 + b), UNIT) for b in range(2)]
        B = A + 4 * UNIT
        sM, sS, sW = at(B, 1024 + NS), at(B + 1088, 1024 + NS), at(B + 2176, WIN + NS)
        sC = at(B + 2752, 72)
        sPs = [[at(B + 3000 * d + 420 * k, 420) for k in range(3)] for d in range(2)]
        ptP = at(B + 1300, 3, 384)
        ptC = at(B + 2452, 256)
        pcn = at(B + 2824, 66)
        st = at(B + 2890, 64)
        sts = [st, at(B + 4300, 64)]
        pt = at(B + 2960, 6, 512)
        qz = at(B + 6032, 2, 4, 64)
        qzb = at(B + 6544, 2, 64)
        pcg = at(B + 6672, 64)
        wbr_sb = at(A, 8, D)
        wo_sb = at(PJ, KD, D)
        assert PJ + 8192 <= A and A + 8192 <= A + 2 * UNIT
        moe_in = mT[:, 8:16, :]
        sq2 = at(PJ, KD, N)
        hR = at(PJ, 4, D)
        rt = PJ + 4096
        X = rt + 1760
        xeS = [at(X + D * k, D) for k in range(2)]
        xeT = [at(X + 2048 + D * k, KD, P) for k in range(2)]
        silS, actS = at(X + 4096, 2, 256), at(X + 4608, 2, 256)
        actT = at(X + 5120, 2, 2, P)
        yeS = [at(X + 5632 + D * k, D) for k in range(2)]
        M0 = TOTAL - 24576
        assert X + 7680 <= M0
        wo2 = [at(M0 + 4096 * k, 2, 2, D) for k in range(2)]
        wi2 = [at(M0 + 8192 * (k + 1), 2, KD, 512) for k in range(2)]
        yG = [at(M0 + 8192 + 4096 * r, 4, D) for r in range(2)]

        ident = cst[:, C_ID:C_ID + 128]
        ones = cst[:, C_ONE:C_ONE + 128]
        cT = vecs[:, V_C:V_C + KD * NC].rearrange("p (k c) -> p k c", c=NC)
        gains = vecs[:, V_G:V_G + 3 * KD].rearrange("p (j k) -> p j k", k=KD)
        w2k, w2v = vecs[:, V_W2K:V_W2K + DH], vecs[:, V_W2V:V_W2V + DH]
        pe = vecs[:, V_PE:V_PE + 32].rearrange("p (v t) -> p v t", t=16)
        w_rt = vecs[:, V_WR:V_WR + KD * 36].rearrange("p (k n) -> p k n", n=36)
        idx = cst[:, C_IDX:C_IDX + 16]

        s_in = sem("inputs_loaded")
        s_w = [sem(f"weight_tile_loaded{k}") for k in range(3)]
        s_w1 = sem("cmp_weights_loaded")
        s_xc = sem("cmp_pages_loaded")
        s_k = [sem(f"keys_loaded{b}") for b in range(2)]
        s_v = [sem(f"values_loaded{b}") for b in range(2)]
        s_wbr, s_wo = sem("branch_weights_loaded"), sem("out_weights_loaded")
        s_wi = [sem(f"expert_in_loaded{k}") for k in range(2)]
        s_wo2 = [sem(f"expert_out_loaded{k}") for k in range(2)]
        s_xl = [sem(f"expert_rows_loaded{k}") for k in range(2)]
        s_st = [sem(f"expert_rows_stored{k}") for k in range(2)]
        s_xe, s_zf, s_yg = sem("rows_scattered"), sem("rows_zeroed"), sem("rows_gathered")
        s_gd, s_gs = sem("gates_in_dram"), sem("gates_by_row")
        s_out = sem("outputs_written")
        s_silu, s_sq, s_ss = sem("cond_silu"), sem("squares"), sem("square_sums")
        s_cz, s_adr = sem("cond_padding"), sem("ada_rows_out")
        s_adt = sem("ada_tile_turned")
        s_kx, s_kxe = sem("prompt_pairs"), sem("prompt_pairs_out")
        s_ada, s_mod, s_h = sem("ada_tile_done"), sem("mod_written"), sem("h_ready")
        s_proj, s_pev = sem("proj_chunk_done"), sem("proj_evacuated")
        s_rot, s_rope, s_t1 = sem("rotated"), sem("rope_done"), sem("rope_cos_part")
        s_row, s_rowA, s_rowV = sem("row_proj_done"), sem("row_small_evac"), sem("row_v_evac")
        s_pb, s_pbv = sem("pe_bias_sum"), sem("pe_bias_ready")
        s_cp, s_cpg, s_cp2, s_cpe = sem("cmp_prompt_hid"), sem("cmp_prompt_gelu"), sem("cmp_prompt_out"), sem("cmp_prompt_ready")
        s_cAB, s_cA, s_cB = sem("cmp_hid"), sem("cmp_first_half_out"), sem("cmp_second_half_out")
        s_cS, s_cg, s_c2, s_kcm = sem("cmp_hid_sum"), sem("cmp_gelu"), sem("cmp_out"), sem("cmp_ready")
        s_sc, s_sev, s_nm, s_exp = sem("p_scores"), sem("p_scores_out"), sem("p_max"), sem("p_exp")
        s_nrm, s_tr = sem("p_normed"), sem("p_turned")
        s_ptA, s_ptD, s_pv, s_oev = sem("p_probs_moba_out"), sem("p_probs_nsa_out"), sem("p_pv"), sem("p_o_out")
        z_main, z_wev = sem("s_page_scores"), sem("s_window_out")
        z_qz, z_kd, z_small, z_sev = sem("q_blocks"), [sem(f"keys_used{b}") for b in range(2)], sem("s_scores"), sem("s_scores_out")
        z_cm, z_ce, z_pcn, z_imp, z_gsr = sem("cmp_max"), sem("cmp_exp"), sem("cmp_probs"), sem("cmp_group_sums"), sem("cmp_group_read")
        z_nm, z_ex, z_rr, z_np, z_nd = sem("s_max"), sem("s_exp"), sem("s_recip"), sem("s_normed_act"), sem("s_normed_dve")
        z_tr, z_tA, z_tD = sem("s_turned"), sem("s_turned_out_act"), sem("s_turned_out_dve")
        z_vd, z_oev = [sem(f"values_used{b}") for b in range(2)], sem("s_o_out")
        s_br, s_mg, s_op, s_x1 = sem("branch_proj"), sem("merged"), sem("out_proj"), sem("x1_chunk")
        s_sq2, s_ss2, s_h2 = sem("squares2"), sem("square_sums2"), sem("moe_in_ready")
        s_lg, s_lc, s_le, s_l8, s_l8e = sem("logits"), sem("logit_diffs"), sem("group_exp"), sem("expert_diffs"), sem("expert_exp")
        s_m, s_pos, s_idx, s_flag = sem("chosen"), sem("positions"), sem("indices_ready"), sem("extra_tiles_ready")
        s_ht, s_hr = sem("h_rows_turned"), sem("h_rows_ready")
        s_xt, s_xtA, s_xtD = sem("pair_rows_turned"), sem("pair_rows_out_act"), sem("pair_rows_out_dve")
        s_hd, s_sil, s_ac, s_at, s_atE = (sem("pair_hidden"), sem("pair_silu"), sem("pair_act"), sem("pair_act_turned"),
                                          sem("pair_act_out"))
        s_od, s_yA, s_yD = sem("pair_out"), sem("pair_out_act"), sem("pair_out_dve")
        s_dn, s_g1, s_yr = sem("outputs_stored"), sem("first_outputs_weighed"), sem("outputs_mixed")
        s_yt, s_x2, s_sq3, s_ss3, s_fin = (sem("moe_turned"), sem("x2_chunk"), sem("squares3"), sem("square_sums3"),
                                           sem("final_ready"))
        x_w = [sem(f"extra_weights_loaded{k}") for k in range(2)]
        s_ch, s_cha, s_chp = sem("vector_chain"), sem("scalar_chain"), sem("pool_chain")
        s_z, s_y = sem("zeros_ready"), sem("y_written")
        s_ms, s_rms = sem("mean_square"), sem("root_mean_square")

        block = ctx.enter_context(nc.Block())

        @block.sync
        def _(sp):
            sp.dma_start(vecs, vec).then_inc(s_in, 16)
            sp.dma_start(cst, consts).then_inc(s_in, 16)
            sp.dma_start(xT, x_t).then_inc(s_in, 16)
            sp.dma_start(page_row[:, :], pages).then_inc(s_in, 16)

            def page_of(b, p):
                return sp.value_load(page_row[0:1, b * PAGES + p:b * PAGES + p + 1], min_val=0, max_val=NPHYS - 1)

            def cmp_half(half):
                for j in range(32):
                    pg = page_of(4 * half + j // PAGES, j % PAGES)
                    sp.dma_start(xc[half][:, j, :],
                                 cmp_pages[bass.ds(pg, 1), :, :].rearrange("o p n -> (o p) n")).then_inc(s_xc, 16)

            def unit(b, dst, src, w, s):
                for p in range(PAGES):
                    pg = page_of(b, p)
                    sp.dma_start(dst[:, p * 640:(p + 1) * 640],
                                 src[bass.ds(pg, 1), :, :].rearrange("o p n -> (o p) n")).then_inc(s, 16)
                sp.dma_start(dst[:, PAGES * 640:UNIT], win[w, b]).then_inc(s, 16)

            for n in range(ADA_TILES + 10):
                if n >= 3 and n - 3 < ADA_TILES:
                    sp.wait_ge(s_ada, n - 2)
                elif n >= 3:
                    sp.wait_ge(s_proj, 4 * (n - 2 - ADA_TILES))
                if n < ADA_TILES:
                    sp.dma_start(ring[n % 3], w_ada[n]).then_inc(s_w[n % 3], 16)
                else:
                    sp.dma_start(ring[n % 3], w_in[n - ADA_TILES]).then_inc(s_w[n % 3], 16)
                if n == ADA_TILES + 4:
                    sp.wait_ge(s_h, 1)
                    for v in range(2):
                        sp.dma_start(w1_sb[v], w1[:, v]).then_inc(s_w1, 16)
                if n == ADA_TILES + 5:
                    sp.wait_ge(s_in, 64)
                    cmp_half(0)
            sp.wait_ge(s_row, 6)
            cmp_half(1)
            sp.wait_ge(s_kcm, 4)
            sp.wait_ge(s_cpe, 2)
            for i in range(4):
                for b in range(2):
                    if i:
                        sp.wait_ge(z_kd[b], i)
                    unit(2 * i + b, kU[b], k_pages, 0, s_k[b])
                for b in range(2):
                    if i:
                        sp.wait_ge(z_vd[b], i)
                    unit(2 * i + b, vU[b], v_pages, 1, s_v[b])
            for b in range(2):
                sp.wait_ge(z_kd[b], 4)
            sp.dma_start(wbr_sb, w_br).then_inc(s_wbr, 16)
            for b in range(2):
                sp.wait_ge(z_vd[b], 4)
            sp.dma_start(wo_sb, w_out).then_inc(s_wo, 16)

            def pair_in(p, q):
                sp.dma_start(wi2[q].rearrange("p e k n -> p e (k n)"),
                             w_ein[bass.ds(p * 2, 2), :, :].rearrange("e p n -> p e n")).then_inc(s_wi[q], 16)

            def pair_out(p, q):
                sp.dma_start(wo2[q].rearrange("p e k n -> p e (k n)"),
                             w_eout[bass.ds(p * 2, 2), :, :].rearrange("e p n -> p e n")).then_inc(s_wo2[q], 16)

            def pair_rows(p, q):
                sp.dma_start(xeS[q], x_rows[bass.ds(p * P, P), :]).then_inc(s_xl[q], 16)

            for q in range(2):
                pair_in(q, q)
            sp.wait_ge(s_br, KD)
            for q in range(2):
                pair_out(q, q)
            sp.wait_ge(s_xe, 16 * 8)
            for q in range(2):
                pair_rows(q, q)
            with sp.Fori(1, PAIRS // 2) as i:
                for q in range(2):
                    p = i * 2 + q
                    sp.wait_ge(s_xt, p - 1)
                    pair_rows(p, q)
                    sp.wait_ge(s_hd, p - 1)
                    pair_in(p, q)
                    sp.wait_ge(s_od, (p - 1) * 2)
                    pair_out(p, q)
            sp.wait_ge(s_flag, 1)
            n_extra = sp.value_load(extra[0:1, 0:1], min_val=0, max_val=EXTRA)
            for x in range(EXTRA // 2):
                p, q = PAIRS + x, x % 2
                with sp.If(n_extra > 2 * x):
                    sp.wait_ge(s_xt, p - 1)
                    pair_rows(p, q)
                    sp.wait_ge(s_od, (p - 1) * 2)
                    for u in range(2):
                        e = sp.value_load(extra[0:1, 1 + 2 * x + u:2 + 2 * x + u], min_val=0, max_val=E - 1)
                        sp.dma_start(wi2[q][:, u].rearrange("p k n -> p (k n)"),
                                     w_ein[bass.ds(e, 1), :, :].rearrange("o p n -> (o p) n")).then_inc(x_w[q], 16)
                        sp.dma_start(wo2[q][:, u].rearrange("p k n -> p (k n)"),
                                     w_eout[bass.ds(e, 1), :, :].rearrange("o p n -> (o p) n")).then_inc(x_w[q], 16)
            sp.wait_ge(s_fin, 1)
            sp.dma_start(o_y, xT).then_inc(s_y, 16)
            sp.wait_ge(s_y, 16)
            sp.wait_ge(s_out, 16 * 8)

        @block.tensor
        def _(te):
            mm = te.matmul
            te.wait_ge(s_in, 64)
            te.wait_ge(s_sq, 1)
            for k in range(KD):
                m = mm(banks[7][:, 0:N], ones, sq[:, k, :], start=(k == 0), stop=(k == KD - 1))
            m.then_inc(s_ss, 1)
            te.wait_ge(s_silu, 1)

            def turn_ada(n):
                te.wait_ge(s_adr, n + 1)
                if n >= 2:
                    te.wait_ge(s_mod, n - 1)
                for c in range(4):
                    m = mm(banks[2 + n % 2][:, NC * c:NC * (c + 1)], adaR[n % 2][:, P * c:P * (c + 1)],
                           cst[:, C_SEL:C_SEL + NC], start=True, stop=True)
                m.then_inc(s_adt, 1)

            for n in range(ADA_TILES):
                te.wait_ge(s_w[n % 3], 16 * (n // 3 + 1))
                if n >= 2:
                    te.wait_ge(s_adr, n - 1)
                for k in range(0, KD, 2):
                    for j in range(2):
                        m = mm(banks[n % 2][64 * j:64 * (j + 1), :], condS[:, k + j, :], ring[n % 3][:, k + j, :],
                               start=(k == 0), stop=(k == KD - 2))
                m.then_inc(s_ada, 1)
                if n:
                    turn_ada(n - 1)
            turn_ada(ADA_TILES - 1)
            te.wait_ge(s_h, 1)
            te.wait_ge(s_mod, ADA_TILES)

            def rotate(c):
                te.wait_ge(s_pev, c + 1)
                if c >= 2:
                    te.wait_ge(s_rope, c - 1)
                mm(banks[4 + c % 2][:, 0:N], cst[:, C_PERM:C_PERM + P], qs[:, c % 3, :],
                   start=True, stop=True).then_inc(s_rot, 1)

            for c in range(4 * T_TILES):
                n = ADA_TILES + c // 4
                te.wait_ge(s_w[n % 3], 16 * (n // 3 + 1))
                if c >= 4:
                    te.wait_ge(s_pev, c - 3)
                for k in range(KD):
                    m = mm(banks[c % 4][:, 0:N], ring[n % 3][:, k, P * (c % 4):P * (c % 4 + 1)], hT[:, k, :],
                           start=(k == 0), stop=(k == KD - 1))
                m.then_inc(s_proj, 1)
                if 1 <= c <= ROT:
                    rotate(c - 1)
            te.wait_ge(s_rope, ROT)
            te.wait_ge(s_pev, 4 * T_TILES)
            for j, width in enumerate((512, 280)):
                n = ADA_TILES + T_TILES + j
                te.wait_ge(s_w[n % 3], 16 * (n // 3 + 1))
                for t, (t0, tn) in enumerate(TOK):
                    bank = banks[4 + t] if j == 0 else banks[t]
                    for k in range(KD):
                        m = mm(bank[0:tn, 0:width], hT[:, k, t0:t0 + tn], ring[n % 3][:, k, 0:width],
                               start=(k == 0), stop=(k == KD - 1))
                    m.then_inc(s_row, 1)

            for v in range(2):
                for g in range(2):
                    for t2 in range(2):
                        m = mm(banks[3][DH * t2:DH * (t2 + 1), P * (2 * v + g):P * (2 * v + g + 1)],
                               ident[:, DH * g:DH * (g + 1)], kvc[:, 3 * v, t2:NP_:2], start=True, stop=True)
            m.then_inc(s_kx, 1)
            te.wait_ge(s_w1, 32)
            for v in range(2):
                for t in range(16):
                    m = mm(banks[7][:, v:v + 1], w1_sb[v][:, t, :], pe[:, v, t:t + 1], start=(t == 0), stop=(t == 15))
            m.then_inc(s_pb, 1)
            te.wait_ge(s_kxe, 1)
            te.wait_ge(s_pbv, 1)
            for v in range(2):
                for t in range(16):
                    m = mm(banks[7][:, 32 * (v + 1):32 * (v + 1) + 2 * NCMPP].rearrange("p (g n) -> p g n", g=2),
                           w1_sb[v][:, t, :], kx[:, v, :, t:t + 8 * (NCMPP - 1) + 1:8], start=(t == 0), stop=(t == 15))
            m.then_inc(s_cp, 1)

            def cmp_hid(half):
                te.wait_ge(s_xc, 32 * 16 * (half + 1))
                if half == 0:
                    te.wait_ge(s_rowA, 6)
                for v in range(2):
                    for part in range(2):
                        if half:
                            te.wait_ge(s_cA if part == 0 else s_cB, v + 1)
                        for t in range(8):
                            c = P * v + 16 * t
                            m = mm(banks[2 * v + part][:, :].rearrange("p (j n) -> p j n", n=16),
                                   w1_sb[v][:, 8 * part + t, :], xc[half][:, :, c:c + 16],
                                   start=(t == 0), stop=(t == 7))
                        m.then_inc(s_cAB, 1)

            def cmp_out(half):
                te.wait_ge(s_cg, 2 * half + 1)
                if half:
                    te.wait_ge(s_kcm, 2)
                for g in range(2):
                    m = mm(banks[4][DH * g:DH * (g + 1), 0:4 * NCMP].rearrange("p (b n) -> p b n", n=NCMP),
                           w2k, gl[:, 0, :, g, :], start=True, stop=True)
                m.then_inc(s_c2, 1)
                te.wait_ge(s_cg, 2 * half + 2)
                for b in range(4):
                    for g in range(2):
                        m = mm(banks[5][0:NCMP, P * b + DH * g:P * b + DH * (g + 1)], gl[:, 1, b, g, :], w2v,
                               start=True, stop=True)
                m.then_inc(s_c2, 1)

            cmp_hid(0)
            te.wait_ge(s_cpg, 2)
            te.wait_ge(s_pbv, 1)
            for g in range(2):
                m = mm(banks[7][DH * g:DH * (g + 1), 0:NCMPP], w2k, glp[:, 0, g, :], start=True, stop=True)
            m.then_inc(s_cp2, 1)
            for g in range(2):
                m = mm(banks[6][0:NCMPP, DH * g:DH * (g + 1)], glp[:, 1, g, :], w2v, start=True, stop=True)
            m.then_inc(s_cp2, 1)
            cmp_out(0)
            cmp_hid(1)
            cmp_out(1)

            def p_scores(h):
                g, r, hp, o = h // 4, h % 4, h // 2, DH * (h % 2)
                for kind in range(3):
                    if h:
                        te.wait_ge(s_sev, 3 * (h - 1) + kind + 1)
                    if kind == 0:
                        q, k = qA[o:o + DH, hp, :], kA[o:o + DH, hp, :]
                    else:
                        q, k = qB[DH * g:DH * (g + 1), r, :], kvc[DH * g:DH * (g + 1), kind, :]
                    mm(banks[kind][:, 0:128], q[:, 0:128], k[:, 0:128], start=True, stop=True)
                    m = mm(banks[kind][:, 128:384], q[:, 128:256], k[:, 0:256], start=True, stop=True)
                    if kind == 2:
                        for c in range(2):
                            m = mm(banks[kind][:, 384 + NCMPP * c:384 + NCMPP * (c + 1)], q[:, 128 * c:128 * (c + 1)],
                                   kcmp[DH * g:DH * (g + 1), :], start=True, stop=True)
                    m.then_inc(s_sc, 1)

            def p_turn(h):
                sP = sPs[h % 2]
                for kind in range(3):
                    te.wait_ge(s_nrm, 3 * h + kind + 1)
                    if h:
                        te.wait_ge(*((s_ptA, h) if kind == 0 else (s_ptD, 2 * (h - 1) + kind)))
                    if kind < 2:
                        te.transpose(banks[3 + kind][0:NCMPP, 384:512],
                                     sP[2][:, 384 + NCMPP * kind:384 + NCMPP * (kind + 1)], ident)
                    for j in range(3):
                        m = te.transpose(banks[3 + kind][:, P * j:P * (j + 1)], sP[kind][:, P * j:P * (j + 1)], ident)
                    m.then_inc(s_tr, 1)

            def p_values(h):
                g, o = h // 4, DH * (h % 2)
                if h:
                    te.wait_ge(s_oev, 2 * (h - 1) + 1)
                te.wait_ge(s_ptA, h + 1)
                mm(banks[6][o:o + DH, 0:256], vA[:, 0, DH * h:DH * (h + 1)], ptP[:, 0, 0:256], start=True, stop=False)
                mm(banks[6][o:o + DH, 128:256], vA[:, 1, DH * h:DH * (h + 1)], ptP[:, 0, 256:384],
                   start=False, stop=True).then_inc(s_pv, 1)
                if h:
                    te.wait_ge(s_oev, 2 * h)
                te.wait_ge(s_ptD, 2 * h + 2)
                out = banks[7][DH * g:DH * (g + 1), :]
                mm(out[:, 0:256], vcmp[0:NCMPP, DH * g:DH * (g + 1)], ptC[0:NCMPP, :], start=True, stop=False)
                for kind in (1, 2):
                    c = P * (kind - 1) + DH * g
                    mm(out[:, 0:256], vS[:, 0, c:c + DH], ptP[:, kind, 0:256], start=False, stop=False)
                    m = mm(out[:, 128:256], vS[:, 1, c:c + DH], ptP[:, kind, 256:384], start=False, stop=(kind == 2))
                m.then_inc(s_pv, 1)

            te.wait_ge(s_cpe, 2)
            te.wait_ge(s_kcm, 4)
            p_scores(0)
            p_scores(1)
            for h in range(H):
                p_turn(h)
                if h + 2 < H:
                    p_scores(h + 2)
                p_values(h)

            def smp_scores(i):
                te.wait_ge(z_qz, i + 1)
                if i:
                    te.wait_ge(z_sev, i)
                for b in range(2):
                    te.wait_ge(s_k[b], 144 * (i + 1))
                pg = [kU[b][:, 0:PAGES * 640].rearrange("p (j n) -> p j n", n=640) for b in range(2)]
                for half in range(2):
                    for hp in range(4):
                        for b in range(2):
                            mm(banks[half][64 * b:64 * b + 64, :].rearrange("p (j n) -> p j n", n=P), qz[:, b, hp, :],
                               pg[b][:, 4 * half:4 * half + 4, P * hp:P * (hp + 1)], start=(hp == 0), stop=(hp == 3))
                    for b in range(2):
                        m = mm(banks[2 + half][64 * b:64 * b + 64, :].rearrange("p (j n) -> p j n", n=P), qzb[:, b, :],
                               pg[b][:, 4 * half:4 * half + 4, 512:640], start=True, stop=True)
                m.then_inc(z_main, 1)

            def smp_small(i):
                if i:
                    te.wait_ge(z_wev, i)
                    te.wait_ge(z_tD, 3 * i)
                for b in range(2):
                    mm(banks[4][64 * b:64 * b + 64, :], qzb[:, b, :], kU[b][:, PAGES * 640:UNIT], start=True, stop=True)\
                        .then_inc(z_kd[b], 1)
                for b in range(2):
                    rows = slice(64 * b, 64 * b + 64)
                    for hp in range(4):
                        mm(banks[5][rows, 0:64], qz[:, b, hp, :], kA[:, hp, NP_:N], start=(hp == 0), stop=(hp == 3))
                    mm(banks[5][rows, 64:128], qzb[:, b, :], kvc[:, 1, NP_:N], start=True, stop=True)
                    mm(banks[5][rows, 128:192], qzb[:, b, :], kvc[:, 2, NP_:N], start=True, stop=True)
                    m = mm(banks[5][rows, 192:192 + NCMP], qzb[:, b, :], kcm[:, 2 * i + b, :], start=True, stop=True)
                m.then_inc(z_small, 1)

            def smp_group(i):
                te.wait_ge(z_pcn, i + 1)
                mm(banks[5][:, 256:321], cst[:, C_R:C_R + P], pcn[:, 0:65], start=True, stop=True).then_inc(z_imp, 1)

            def smp_turn(i):
                for j, (s, n) in enumerate(((z_nd, 2 * i + 1), (z_nd, 2 * i + 1), (z_np, i + 1), (z_np, i + 1),
                                            (z_nd, 2 * i + 2), (z_nd, 2 * i + 2))):
                    te.wait_ge(s, n)
                    bank = banks[6 if j % 2 == 0 else 4]
                    if j >= 2 or i:
                        te.wait_ge(z_tA if j % 2 == 0 else z_tD, 3 * i + j // 2)
                    if j == 1:
                        te.wait_ge(z_wev, i + 1)
                    for c in range(4):
                        if j < 5:
                            src = (sM, sM, sS, sS, sW)[j][:, 512 * (j % 2 if j < 4 else 0) + P * c:][:, 0:P]
                            m = te.transpose(bank[:, P * c:P * (c + 1)], src, ident)
                        else:
                            src = (sM[:, 1024:1088], sS[:, 1024:1088], sW[:, 512:576], pcg)[c]
                            m = te.transpose(bank[0:64, P * c:P * (c + 1)], src, ident)
                    m.then_inc(z_tr, 1)

            def smp_values(i, b):
                if b == 0:
                    te.wait_ge(z_tA, 3 * i + 3)
                    te.wait_ge(z_tD, 3 * i + 3)
                    if i:
                        te.wait_ge(z_oev, i)
                te.wait_ge(s_v[b], 144 * (i + 1))
                for hp in range(4):
                    out = banks[7][:, P * b + 16 * hp:P * b + 16 * hp + 16]
                    c = 64 * b + 16 * hp
                    for p in range(PAGES):
                        mm(out, vU[b][:, 640 * p + P * hp:640 * p + P * (hp + 1)],
                           pt[:, p // 4, P * (p % 4) + c:P * (p % 4) + c + 16], start=(p == 0), stop=False)
                    mm(out, vA[0:64, 2, P * hp:P * (hp + 1)], pt[0:64, 5, c:c + 16], start=False, stop=True)
                out = banks[7][:, P * b + 64:P * b + 128]
                for p in range(PAGES):
                    mm(out, vU[b][:, 640 * p + 512:640 * p + 640],
                       pt[:, 2 + p // 4, P * (p % 4) + 64 * b:P * (p % 4) + 64 * b + 64], start=(p == 0), stop=False)
                for p in range(4):
                    mm(out, vU[b][:, PAGES * 640 + P * p:PAGES * 640 + P * (p + 1)],
                       pt[:, 4, P * p + 64 * b:P * p + 64 * b + 64], start=False, stop=False)
                mm(out, vS[0:64, 2, 0:128], pt[0:64, 5, P + 64 * b:P + 64 * b + 64], start=False, stop=False)
                mm(out, vS[0:64, 2, 128:256], pt[0:64, 5, 2 * P + 64 * b:2 * P + 64 * b + 64], start=False, stop=False)
                mm(out, vcm[0:NCMP, 2 * i + b, :], pt[0:NCMP, 5, 3 * P + 64 * b:3 * P + 64 * b + 64],
                   start=False, stop=True).then_inc(z_vd[b], 1)

            te.wait_ge(s_ptD, 2 * H)
            te.wait_ge(s_oev, 2 * H)
            smp_scores(0)
            smp_small(0)
            smp_group(0)
            for i in range(4):
                if i + 1 < 4:
                    smp_scores(i + 1)
                smp_turn(i)
                if i + 1 < 4:
                    smp_small(i + 1)
                smp_values(i, 0)
                if i + 1 < 4:
                    smp_group(i + 1)
                smp_values(i, 1)

            te.wait_ge(z_oev, 4)
            te.wait_ge(s_wbr, 16)
            for c in range(KD):
                for a, src in ((0, oTa), (1, oTb)):
                    if c >= 2:
                        te.wait_ge(s_mg, c - 1)
                    for k in range(4):
                        m = mm(banks[2 * (c % 2) + a][:, 0:N], wbr_sb[:, 4 * a + k, P * c:P * (c + 1)], src[:, k, :],
                               start=(k == 0), stop=(k == 3))
                m.then_inc(s_br, 1)
            te.wait_ge(s_mg, KD)
            te.wait_ge(s_wo, 16)
            for c in range(KD):
                if c >= 2:
                    te.wait_ge(s_x1, c - 1)
                for k in range(KD):
                    m = mm(banks[4 + c % 2][:, 0:N], wo_sb[:, k, P * c:P * (c + 1)], mT[:, k, :],
                           start=(k == 0), stop=(k == KD - 1))
                m.then_inc(s_op, 1)
            te.wait_ge(s_sq2, 1)
            for k in range(KD):
                m = mm(banks[7][:, 0:N], ones, sq2[:, k, :], start=(k == 0), stop=(k == KD - 1))
            m.then_inc(s_ss2, 1)

            te.wait_ge(s_h2, 1)
            for t in range(4):
                for k in range(KD):
                    m = mm(banks[0][0:RT, 36 * t:36 * (t + 1)], moe_in[:, k, RT * t:RT * (t + 1)], w_rt[:, k, :],
                           start=(k == 0), stop=(k == KD - 1))
            m.then_inc(s_lg, 1)
            for n in range(8):
                if n >= 4:
                    te.wait_ge(s_hr, n - 3)
                for c in range(4):
                    m = te.transpose(banks[2 + n % 4][0:RT, P * c:P * (c + 1)],
                                     moe_in[:, 4 * (n % 2) + c, RT * (n // 2):RT * (n // 2 + 1)], ident)
                m.then_inc(s_ht, 1)
            te.wait_ge(s_m, 1)
            chosen = at(rt + 900, 4, E)
            for t in range(4):
                for u in range(t + 1):
                    lhs = cst[0:RT, C_LT:C_LT + RT] if u == t else ones[0:RT, 0:RT]
                    m = mm(banks[1][0:RT, E * t:E * (t + 1)], lhs, chosen[0:RT, u, :], start=(u == 0), stop=(u == t))
            for u in range(4):
                m = mm(banks[1][0:RT, 4 * E:5 * E], ones[0:RT, 0:RT], chosen[0:RT, u, :], start=(u == 0), stop=(u == 3))
            m.then_inc(s_pos, 1)

            def turn_rows(p, q, first=False):
                te.wait_ge(s_xl[q], (p - q) * 8 + 16)
                if not first:
                    te.wait_ge(s_xtA, p)
                    te.wait_ge(s_xtD, p)
                for k in range(KD):
                    m = te.transpose(banks[k // 4][:, P * (k % 4):P * (k % 4 + 1)], xeS[q][:, P * k:P * (k + 1)], ident)
                m.then_inc(s_xt, 1)

            def hidden(p, q, loaded=None):
                te.wait_ge(*(loaded or (s_wi[q], (p - q) * 8 + 16)))
                te.wait_ge(s_xtA, p + 1)
                te.wait_ge(s_xtD, p + 1)
                for k in range(KD):
                    for e in range(2):
                        m = mm(banks[2 + q][CAP * e:CAP * (e + 1), :], xeT[q][:, k, CAP * e:CAP * (e + 1)],
                               wi2[q][:, e, k, :], start=(k == 0), stop=(k == KD - 1))
                m.then_inc(s_hd, 1)

            def turn_act(p, q):
                te.wait_ge(s_ac, p + 1)
                for j in range(2):
                    m = te.transpose(banks[4 + q][:, P * j:P * (j + 1)], actS[:, q, P * j:P * (j + 1)], ident)
                m.then_inc(s_at, 1)

            def pair_output(p, q, first=False, loaded=None):
                te.wait_ge(*(loaded or (s_wo2[q], (p - q) * 8 + 16)))
                te.wait_ge(s_atE, p + 1)
                for half in range(2):
                    if not first:
                        te.wait_ge(s_yA if half == 0 else s_yD, p)
                    for j in range(2):
                        for e in range(2):
                            m = mm(banks[6 + half][CAP * e:CAP * (e + 1), :], actT[:, q, j, CAP * e:CAP * (e + 1)],
                                   wo2[q][:, e, j, 512 * half:512 * (half + 1)], start=(j == 0), stop=(j == 1))
                    m.then_inc(s_od, 1)

            te.wait_ge(s_hr, 8)
            te.wait_ge(s_flag, 1)
            turn_rows(0, 0, True)
            hidden(0, 0)
            turn_rows(1, 1)
            turn_act(0, 0)
            hidden(1, 1)
            turn_rows(2, 0)
            pair_output(0, 0, True)
            turn_act(1, 1)
            with te.Fori(1, PAIRS // 2 - 1) as i:
                for q in range(2):
                    p = i * 2 + q
                    hidden(p, q)
                    turn_rows(p + 1, 1 - q)
                    pair_output(p - 1, 1 - q)
                    turn_act(p, q)
            p = PAIRS - 2
            hidden(p, 0)
            turn_rows(p + 1, 1)
            pair_output(p - 1, 1)
            turn_act(p, 0)
            hidden(p + 1, 1)
            pair_output(p, 0)
            turn_act(p + 1, 1)
            pair_output(p + 1, 1)

            n_extra = te.value_load(extra[0:1, 0:1], min_val=0, max_val=EXTRA)
            for x in range(EXTRA // 2):
                p, q = PAIRS + x, x % 2
                with te.If(n_extra > 2 * x):
                    loaded = (x_w[q], 64 * (x // 2 + 1))
                    turn_rows(p, q)
                    hidden(p, q, loaded)
                    turn_act(p, q)
                    pair_output(p, q, False, loaded)
            te.wait_ge(s_dn, 1)
            te.wait_ge(s_yr, 4)
            for c in range(KD):
                if c >= 2:
                    te.wait_ge(s_x2, c - 1)
                for t in range(4):
                    m = te.transpose(banks[6 + c % 2][:, RT * t:RT * (t + 1)], yG[0][0:RT, t, P * c:P * (c + 1)],
                                     ident[0:RT, 0:RT])
                m.then_inc(s_yt, 1)
            te.wait_ge(s_sq3, 1)
            for k in range(KD):
                m = mm(banks[0][:, 0:N], ones, sq2[:, k, :], start=(k == 0), stop=(k == KD - 1))
            m.then_inc(s_ss3, 1)

        @block.scalar
        def _(sc):
            act = sc.activation

            def rms(n):
                sc.wait_ge(s_ms, n)
                act(rstd, rstd, ACT.Sqrt).then_inc(s_rms, 1)

            sc.wait_ge(s_in, 64)
            sc.wait_ge(s_cz, 1)
            act(condS[:, :, 0:NC], cT, ACT.Silu).then_inc(s_silu, 1)
            act(sq, xT, ACT.Square).then_inc(s_sq, 1)
            rms(1)
            for c in range(4 * T_TILES):
                sc.wait_ge(s_proj, c + 1)
                if c < ROT:
                    if c >= 3:
                        sc.wait_ge(s_rope, c - 2)
                    act(qs[:, c % 3, :], banks[c % 4][:, 0:N], ACT.Copy).then_inc(s_pev, 1)
                elif c == ROT:
                    act(kvc[:, 3, :], banks[c % 4][:, 0:N], ACT.Copy).then_inc(s_pev, 1)
                else:
                    act(mT[:, c - 16, :], banks[c % 4][:, 0:N], ACT.Sigmoid).then_inc(s_pev, 1)
            for t, (t0, tn) in enumerate(TOK):
                sc.wait_ge(s_row, 4 + t)
                act(vS[0:tn, t, :], banks[t][0:tn, 0:256], ACT.Copy).then_inc(s_rowA, 1)
                act(gate[0:tn, t, :], banks[t][0:tn, 256:280], ACT.Sigmoid).then_inc(s_rowA, 1)
            sc.wait_ge(s_kx, 1)
            act(kx.rearrange("p v g n -> p (v g n)"), banks[3][:, :], ACT.Copy).then_inc(s_kxe, 1)
            sc.wait_ge(s_cp, 1)
            sc.wait_ge(s_pbv, 1)
            for v in range(2):
                act(glp[:, v].rearrange("p g n -> p (g n)"), banks[7][:, 32 * (v + 1):32 * (v + 1) + 2 * NCMPP],
                    ACT.Gelu_apprx_tanh, bias=peb[:, v:v + 1]).then_inc(s_cpg, 1)
            for half in range(2):
                for v in range(2):
                    n = 2 * half + v
                    sc.wait_ge(s_cAB, 4 * half + 2 * v + 1)
                    if n:
                        sc.wait_ge(s_cS, n)
                    src = banks[2 * v][:, :].rearrange("p (b q g n) -> p b q g n", b=4, q=8, g=2)
                    for g in range(2):
                        m = act(hA[:, :, g, :].rearrange("p b (q n) -> p b q n", n=8), src[:, :, :, g, :], ACT.Copy)
                    m.then_inc(s_cA, 1)
                    sc.wait_ge(s_cS, n + 1)
                    if half:
                        sc.wait_ge(s_c2, v + 1)
                    act(gl[:, v].rearrange("p b g n -> p (b g n)"), hS.rearrange("p a n -> p (a n)"),
                        ACT.Gelu_apprx_tanh, bias=peb[:, v:v + 1]).then_inc(s_cg, 1)

            def p_exp(h):
                sc.wait_ge(s_nm, h + 1)
                sP, st = sPs[h % 2], sts[h % 2]
                for j in range(6):
                    seg = sP[j // 2][:, 0:128] if j % 2 == 0 else sP[j // 2][:, 128:384]
                    act(seg, seg, ACT.Exp, bias=st[:, 8 + j:9 + j], scale=SCALE, accum_out=st[:, 16 + j:17 + j])
                for c in range(2):
                    seg = sP[2][:, 384 + NCMPP * c:384 + NCMPP * (c + 1)]
                    m = act(seg, seg, ACT.Exp, bias=st[:, 14 + c:15 + c], scale=SCALE)
                m.then_inc(s_exp, 1)

            def p_out(h):
                g, r, hp, o = h // 4, h % 4, h // 2, DH * (h % 2)
                sc.wait_ge(s_tr, 3 * h + 1)
                if h:
                    sc.wait_ge(s_pv, 2 * h)
                act(ptC[0:NCMPP, 0:128], banks[3][0:NCMPP, 384:512], ACT.Copy)
                act(ptP[:, 0, :], banks[3][:, 0:384], ACT.Copy).then_inc(s_ptA, 1)
                sc.wait_ge(s_pv, 2 * h + 1)
                act(oTa[o:o + DH, hp, 0:NP_], banks[6][o:o + DH, 0:NP_], ACT.Copy).then_inc(s_oev, 1)
                sc.wait_ge(s_pv, 2 * h + 2)
                act(oTb[DH * g:DH * (g + 1), r, 0:NP_], banks[7][DH * g:DH * (g + 1), 0:NP_], ACT.Copy).then_inc(s_oev, 1)

            p_exp(0)
            for h in range(H):
                if h + 1 < H:
                    p_exp(h + 1)
                p_out(h)

            def smp_cmp_exp(i):
                sc.wait_ge(z_cm, i + 1)
                act(sC[:, 0:NCMP], sC[:, 0:NCMP], ACT.Exp, bias=st[:, 33:34], scale=SCALE,
                    accum_out=st[:, 34:35]).then_inc(z_ce, 1)

            def smp_exp(i, j):
                s, w = ((sM, 1088), (sW, 576), (sS, 1088))[j]
                sc.wait_ge(z_nm, 3 * i + j + 1)
                act(s[:, 0:w], s[:, 0:w], ACT.Exp, bias=st[:, 40 + j:41 + j], scale=SCALE,
                    accum_out=st[:, 44 + j:45 + j]).then_inc(z_ex, 1)

            def smp_norm(i):
                sc.wait_ge(z_rr, i + 1)
                act(sS, sS, ACT.Copy, scale=st[:, 58:59]).then_inc(z_np, 1)

            def smp_turned(i):
                for j in (0, 2, 4):
                    sc.wait_ge(z_tr, 6 * i + j + 1)
                    if i and j == 0:
                        sc.wait_ge(z_vd[1], i)
                    act(pt[:, j, :], banks[6][:, :], ACT.Copy).then_inc(z_tA, 1)

            def smp_out(i):
                sc.wait_ge(z_vd[1], i + 1)
                src = banks[7][:, 0:256].rearrange("p (b x n) -> p b x n", b=2, n=16)
                new = NP_ + 2 * NQ * i
                for u in range(2):
                    rows = slice(DH * u, DH * (u + 1))
                    act(oTa[rows, :, new:new + 16].rearrange("p h (b q) -> p b h q", b=2),
                        src[rows, :, 0:4, 8 * u:8 * u + 8], ACT.Copy)
                    m = act(oTb[rows, :, new:new + 16].rearrange("p h (b q) -> p b h q", b=2),
                            banks[7][rows, 0:256].rearrange("p (b x n) -> p b x n", b=2, n=8)[:, :, 8 + 4 * u:12 + 4 * u, :],
                            ACT.Copy)
                m.then_inc(z_oev, 1)

            smp_cmp_exp(0)
            smp_exp(0, 0)
            for i in range(4):
                smp_exp(i, 1)
                smp_exp(i, 2)
                smp_norm(i)
                smp_turned(i)
                if i + 1 < 4:
                    smp_cmp_exp(i + 1)
                    smp_exp(i + 1, 0)
                smp_out(i)

            sc.wait_ge(s_x1, KD)
            act(sq2, xT, ACT.Square).then_inc(s_sq2, 1)
            rms(2)
            sc.wait_ge(s_lc, 1)
            g4 = at(rt + 160, 4, 4)
            act(g4[0:RT], g4[0:RT], ACT.Exp).then_inc(s_le, 1)
            sc.wait_ge(s_l8, 1)
            e8 = at(rt + 400, 4, 8)
            act(e8[0:RT], e8[0:RT], ACT.Exp).then_inc(s_l8e, 1)
            for n in range(8):
                sc.wait_ge(s_ht, n + 1)
                act(hR[0:RT, n // 2, 512 * (n % 2):512 * (n % 2 + 1)], banks[2 + n % 4][0:RT, :], ACT.Copy).then_inc(s_hr, 1)

            def rows_out(p, q, first=False):
                sc.wait_ge(s_xt, p + 1)
                if not first:
                    sc.wait_ge(s_hd, p - 1)
                act(xeT[q][:, 0:4, :], banks[0][:, :].rearrange("p (k n) -> p k n", n=P), ACT.Copy).then_inc(s_xtA, 1)

            def pair_silu(p, q):
                sc.wait_ge(s_hd, p + 1)
                act(silS[:, q, :], banks[2 + q][:, 0:256], ACT.Silu).then_inc(s_sil, 1)

            def pair_store(p, q, first=False):
                sc.wait_ge(s_od, p * 2 + 1)
                if not first:
                    sc.wait_ge(s_st[q], (p - q) * 8)
                act(yeS[q][:, 0:512], banks[6][:, :], ACT.Copy).then_inc(s_yA, 1)
                sc.wait_ge(s_yA, p + 1)
                sc.wait_ge(s_yD, p + 1)
                sc.dma_start(y_rows[bass.ds(p * P, P), :], yeS[q]).then_inc(s_st[q], 16)

            rows_out(0, 0, True)
            pair_silu(0, 0)
            rows_out(1, 1, True)
            pair_silu(1, 1)
            rows_out(2, 0)
            pair_store(0, 0, True)
            pair_silu(2, 0)
            rows_out(3, 1)
            pair_store(1, 1, True)
            with sc.Fori(1, PAIRS // 2 - 1) as i:
                for q in range(2):
                    p = i * 2 + q
                    pair_silu(p + 1, 1 - q)
                    rows_out(p + 2, q)
                    pair_store(p, q)
            p = PAIRS - 2
            pair_silu(p + 1, 1)
            pair_store(p, 0)
            pair_store(p + 1, 1)

            sc.wait_ge(s_zf, 16 * (PAIRS + EXTRA + 1))
            sc.wait_ge(s_flag, 1)
            n_extra = sc.value_load(extra[0:1, 0:1], min_val=0, max_val=EXTRA)
            for x in range(EXTRA // 2):
                p, q = PAIRS + x, x % 2
                with sc.If(n_extra > 2 * x):
                    rows_out(p, q)
                    pair_silu(p, q)
                    pair_store(p, q)
                    sc.wait_ge(s_st[q], (p - q) * 8 + 16)
            for q in range(2):
                sc.wait_ge(s_st[q], PAIRS * 8)
            act(silS[:, 0, 0:1], ident[:, 0:1], ACT.Copy).then_inc(s_dn, 1)
            sc.wait_ge(s_yg, 16 * 8)
            for t in range(4):
                act(yG[0][0:RT, t, :], yG[0][0:RT, t, :], ACT.Copy, scale=at(rt + 216, 4)[0:RT, t:t + 1]).then_inc(s_g1, 1)
            sc.wait_ge(s_x2, KD)
            act(sq2, xT, ACT.Square).then_inc(s_sq3, 1)
            rms(3)

        @block.vector
        def _(ve):
            chain = [0]

            def link(ins):
                chain[0] += 1
                ins.then_inc(s_ch, 1)
                ve.wait_ge(s_ch, chain[0])

            def modulated(dst, src, s, shift):
                for k in range(KD):
                    link(ve.tensor_scalar(dst[:, k, 0:NP_], src[:, k, 0:NP_], s[:, k, 0:1], shift[:, k, 0:1], ALU.mult, ALU.add))
                a = src[:, :, NP_:N].rearrange("p k (b q) -> p k b q", q=NQ)
                o = dst[:, :, NP_:N].rearrange("p k (b q) -> p k b q", q=NQ)
                wide = [P, KD, NB, NQ]
                link(ve.tensor_tensor(o, a, s[:, :, 1:NC].unsqueeze(3).to_broadcast(wide), ALU.mult))
                return ve.tensor_tensor(o, o, shift[:, :, 1:NC].unsqueeze(3).to_broadcast(wide), ALU.add)

            def root(total, n):
                ve.tensor_scalar(rstd, total, 1.0 / D, EPS, ALU.mult, ALU.add).then_inc(s_ms, 1)
                ve.wait_ge(s_rms, n)
                link(ve.reciprocal(rstd, rstd))

            def normed(dst):
                return ve.tensor_tensor(dst, xT, rstd.unsqueeze(1).to_broadcast([P, KD, N]), ALU.mult)

            ve.memset(condS, 0.0).then_inc(s_cz, 1)
            ve.wait_ge(s_in, 64)
            ve.wait_ge(s_ss, 1)
            root(banks[7][:, 0:N], 1)
            link(normed(sq))

            def ada_rows(n):
                ve.wait_ge(s_ada, n + 1)
                if n >= 2:
                    ve.wait_ge(s_adt, n - 1)
                ve.tensor_copy(adaR[n % 2], banks[n % 2][:, :]).then_inc(s_adr, 1)

            ada_rows(0)
            for n in range(ADA_TILES):
                if n + 1 < ADA_TILES:
                    ada_rows(n + 1)
                ve.wait_ge(s_adt, n + 1)
                ve.tensor_tensor(mod[:, 4 * n:4 * n + 4, :], banks[2 + n % 2][:, 0:4 * NC].rearrange("p (c n) -> p c n", n=NC),
                                 vecs[:, 4 * n:4 * n + 4].unsqueeze(2).to_broadcast([P, 4, NC]), ALU.add).then_inc(s_mod, 1)
            ve.wait_ge(s_mod, ADA_TILES)
            for j in range(2):
                link(ve.scalar_tensor_tensor(scl[:, j], mod[:, 8 + 24 * j:16 + 24 * j, :], 1.0,
                                             gains[:, j].unsqueeze(2).to_broadcast([P, KD, NC]), ALU.add, ALU.mult))
            modulated(hT, sq, scl[:, 0], mod[:, 0:8, :]).then_inc(s_h, 1)
            dst = [qA[:, c] for c in range(4)] + [kA[:, c] for c in range(4)] + [qB[:, c] for c in range(4)] + [kvc[:, c] for c in range(3)]
            for c in range(ROT):
                ve.wait_ge(s_pev, c + 1)
                ve.wait_ge(s_rot, c + 1)
                ve.tensor_tensor(turn[:, c % 2, 0, :], qs[:, c % 3, :], cst[:, C_COS:C_COS + N], ALU.mult)
                link(ve.tensor_tensor(turn[:, c % 2, 1, :], banks[4 + c % 2][:, 0:N], cst[:, C_SIN:C_SIN + N], ALU.mult))
                ve.tensor_tensor(dst[c], turn[:, c % 2, 0, :], turn[:, c % 2, 1, :], ALU.add).then_inc(s_rope, 1)
            for t, (t0, tn) in enumerate(TOK):
                ve.wait_ge(s_row, t + 1)
                ve.tensor_copy(vA[0:tn, t, :], banks[4 + t][0:tn, :]).then_inc(s_rowV, 1)
            ve.wait_ge(s_pb, 1)
            ve.tensor_copy(peb, banks[7][:, 0:2]).then_inc(s_pbv, 1)
            ve.wait_ge(s_cp2, 1)
            ve.tensor_copy(kcmp, banks[7][:, 0:NCMPP]).then_inc(s_cpe, 1)
            ve.wait_ge(s_cp2, 2)
            ve.tensor_copy(vcmp[0:NCMPP, :], banks[6][0:NCMPP, 0:P]).then_inc(s_cpe, 1)
            for half in range(2):
                for v in range(2):
                    n = 2 * half + v
                    ve.wait_ge(s_cAB, 4 * half + 2 * v + 2)
                    if n:
                        ve.wait_ge(s_cS, n)
                    src = banks[2 * v + 1][:, :].rearrange("p (b q g n) -> p b q g n", b=4, q=8, g=2)
                    for g in range(2):
                        m = ve.tensor_copy(hB[:, :, g, :].rearrange("p b (q n) -> p b q n", n=8), src[:, :, :, g, :])
                    m.then_inc(s_cB, 1)
                    ve.wait_ge(s_cB, n + 1)
                    ve.wait_ge(s_cA, n + 1)
                    if n:
                        ve.wait_ge(s_cg, n)
                    ve.tensor_tensor(hS, hA.rearrange("p b g n -> p (b g) n")[:, :, 0:63],
                                     hB.rearrange("p b g n -> p (b g) n")[:, :, 1:64], ALU.add).then_inc(s_cS, 1)
                ve.wait_ge(s_c2, 2 * half + 1)
                ve.tensor_copy(kcm[:, 4 * half:4 * half + 4, :],
                               banks[4][:, 0:4 * NCMP].rearrange("p (b n) -> p b n", n=NCMP)).then_inc(s_kcm, 1)
                ve.wait_ge(s_c2, 2 * half + 2)
                ve.wait_ge(s_zf, 16 * (PAIRS + EXTRA + 1))
                ve.tensor_copy(vcm[0:NCMP, 4 * half:4 * half + 4, :],
                               banks[5][0:NCMP, :].rearrange("p (b n) -> p b n", n=P)).then_inc(s_kcm, 1)

            ve.wait_ge(s_rowA, 6)

            def p_max(h):
                sP, st = sPs[h % 2], sts[h % 2]
                for kind in range(3):
                    ve.wait_ge(s_sc, 3 * h + kind + 1)
                    if h >= 2:
                        ve.wait_ge(s_tr, 3 * h - 3)
                    if kind == 2:
                        ve.tensor_tensor(sP[2][:, 384:414], banks[2][:, 384:414], cst[:, C_CADD:C_CADD + 30], ALU.add)
                    ve.tensor_tensor(sP[kind][:, 0:384], banks[kind][:, 0:384], cst[:, C_TRI:C_TRI + 384], ALU.add)\
                        .then_inc(s_sev, 1)
                    ve.wait_ge(s_sev, 3 * h + kind + 1)
                    ve.tensor_reduce(st[:, 2 * kind:2 * kind + 1], sP[kind][:, 0:128], AX, ALU.max)
                    m = ve.tensor_reduce(st[:, 2 * kind + 1:2 * kind + 2], sP[kind][:, 128:384], AX, ALU.max)
                link(ve.tensor_reduce(st[:, 6:8], sP[2][:, 384:414].rearrange("p (c n) -> p c n", n=NCMPP), AX, ALU.max))
                ve.tensor_scalar(st[:, 8:16], st[:, 0:8], -SCALE, None, ALU.mult).then_inc(s_nm, 1)

            def p_norm(h):
                sP, st = sPs[h % 2], sts[h % 2]
                ve.wait_ge(s_exp, h + 1)
                link(ve.tensor_tensor(sP[2][:, 384:414], sP[2][:, 384:414], cst[:, C_C01:C_C01 + 30], ALU.mult))
                link(ve.tensor_reduce(st[:, 22:24], sP[2][:, 384:414].rearrange("p (c n) -> p c n", n=NCMPP), AX, ALU.add))
                link(ve.tensor_scalar(st[:, 16:24], st[:, 16:24], TINY, None, ALU.max))
                link(ve.reciprocal(st[:, 24:32], st[:, 16:24]))
                w = st[:, 26:32].rearrange("p (j t) -> p j t", t=2)
                link(ve.tensor_tensor(w, w, gate[:, 0:2, 3 * h:3 * h + 3].rearrange("p t j -> p j t"), ALU.mult))
                for c in range(2):
                    seg = sP[2][:, 384 + NCMPP * c:384 + NCMPP * (c + 1)]
                    ve.tensor_scalar(seg, seg, st[:, 30 + c:31 + c], None, ALU.mult)
                for kind in range(3):
                    ve.tensor_scalar(sP[kind][:, 0:128], sP[kind][:, 0:128], st[:, 24 + 2 * kind:25 + 2 * kind], None, ALU.mult)
                    ve.tensor_scalar(sP[kind][:, 128:384], sP[kind][:, 128:384], st[:, 25 + 2 * kind:26 + 2 * kind], None,
                                     ALU.mult).then_inc(s_nrm, 1)

            def p_turned(h):
                for kind in (1, 2):
                    ve.wait_ge(s_tr, 3 * h + kind + 1)
                    if h:
                        ve.wait_ge(s_pv, 2 * h)
                    if kind == 1:
                        ve.tensor_copy(ptC[0:NCMPP, 128:256], banks[4][0:NCMPP, 384:512])
                    ve.tensor_copy(ptP[:, kind, :], banks[3 + kind][:, 0:384]).then_inc(s_ptD, 1)

            p_max(0)
            for h in range(H):
                if h + 1 < H:
                    p_max(h + 1)
                p_norm(h)
                p_turned(h)

            ve.wait_ge(s_tr, 3 * H)
            ve.wait_ge(s_pv, 2 * H)
            link(ve.memset(qz, 0.0))
            link(ve.memset(qzb, 0.0))
            link(ve.memset(pcn, 0.0))
            link(ve.memset(pcg, 0.0))
            ve.wait_ge(s_gs, 16 * 16)

            def smp_blocks(i):
                if i:
                    ve.wait_ge(z_small, i)
                new = NP_ + 2 * NQ * i
                for hp in range(4):
                    for u in range(2):
                        rows = slice(DH * u, DH * (u + 1))
                        ve.tensor_copy(qz[rows, :, hp, 16 * hp + 8 * u:16 * hp + 8 * u + 8],
                                       qA[rows, hp, new:new + 16].rearrange("p (b q) -> p b q", b=2))
                for g in range(2):
                    for b in range(2):
                        rows = slice(DH * g, DH * (g + 1))
                        m = ve.tensor_copy(qzb[rows, b, 32 * g:32 * g + 32].rearrange("p (r q) -> p r q", q=NQ),
                                           qB[rows, :, new + 8 * b:new + 8 * b + 8])
                m.then_inc(z_qz, 1)

            def dropped(src, n):
                d, e, pen = st[:, 50:51], at(B + 6740, 16)[:, 0:n], at(B + 6756, 16)[:, 0:n]
                link(ve.tensor_reduce(d, src, AX, ALU.min))
                link(ve.scalar_tensor_tensor(e, src, d, idx[:, 0:n], ALU.is_equal, ALU.mult))
                link(ve.tensor_reduce(st[:, 51:52], e, AX, ALU.max))
                link(ve.tensor_scalar(pen, idx[:, 0:n], st[:, 51:52], NEG, ALU.is_equal, ALU.mult))
                return pen

            def smp_max(i):
                ve.wait_ge(z_main, i + 1)
                new = cst[:, C_NEW + NS * i:C_NEW + NS * (i + 1)]
                g4 = st[:, 52:56]
                for half in range(2):
                    m = ve.tensor_reduce(g4[:, 2 * half:2 * half + 2], banks[half][:, :].rearrange("p (j n) -> p j n", n=256),
                                         AX, ALU.add)
                link(m)
                pen = dropped(g4, 4)
                if i:
                    ve.wait_ge(z_tr, 6 * i)
                for half in range(2):
                    m = ve.tensor_tensor(sM[:, 512 * half:512 * (half + 1)].rearrange("p (j n) -> p j n", n=256),
                                         banks[half][:, :].rearrange("p (j n) -> p j n", n=256),
                                         pen[:, 2 * half:2 * half + 2].unsqueeze(2).to_broadcast([P, 2, 256]), ALU.add)
                link(m)
                ve.wait_ge(z_small, i + 1)
                link(ve.tensor_copy(sC[:, 0:NCMP], banks[5][:, 192:192 + NCMP]))
                link(ve.tensor_reduce(st[:, 32:33], sC[:, 0:NCMP], AX, ALU.max))
                ve.tensor_scalar(st[:, 33:34], st[:, 32:33], -SCALE, None, ALU.mult).then_inc(z_cm, 1)
                link(ve.tensor_tensor(sM[:, 1024:1088], banks[5][:, 0:64], new, ALU.add))
                link(ve.tensor_reduce(st[:, 36:37], sM, AX, ALU.max))
                ve.tensor_scalar(st[:, 40:41], st[:, 36:37], -SCALE, None, ALU.mult).then_inc(z_nm, 1)
                ve.tensor_tensor(sS[:, 1024:1088], banks[5][:, 64:128], new, ALU.add)
                ve.tensor_tensor(sW[:, 512:576], banks[5][:, 128:192], new, ALU.add)
                ve.wait_ge(z_ce, i + 1)
                link(ve.tensor_scalar(st[:, 34:35], st[:, 34:35], TINY, None, ALU.max))
                link(ve.reciprocal(st[:, 35:36], st[:, 34:35]))
                ve.tensor_scalar(pcn[:, 1:1 + NCMP], sC[:, 0:NCMP], st[:, 35:36], None, ALU.mult).then_inc(z_pcn, 1)
                ve.tensor_tensor(sW[:, 0:8], banks[4][:, 0:8], cst[:, C_WIN:C_WIN + 8], ALU.add)
                ve.tensor_copy(sW[:, 8:512], banks[4][:, 8:512]).then_inc(z_wev, 1)
                ve.wait_ge(z_wev, i + 1)
                link(ve.tensor_reduce(st[:, 38:39], sW, AX, ALU.max))
                ve.tensor_scalar(st[:, 41:42], st[:, 38:39], -SCALE, None, ALU.mult).then_inc(z_nm, 1)
                ve.wait_ge(z_imp, i + 1)
                imp = at(B + 6772, 16)
                grp = at(B + 6788, 66)
                link(ve.tensor_copy(grp[:, 0:65], banks[5][:, 256:321]))
                link(ve.tensor_reduce(imp, grp[:, 0:64].rearrange("p (j n) -> p j n", n=4), AX, ALU.add))
                link(ve.tensor_tensor(imp, imp, grp[:, 4:65:4], ALU.add))
                pen = dropped(imp, 16)
                for half in range(2):
                    m = ve.tensor_tensor(sS[:, 512 * half:512 * (half + 1)].rearrange("p (j n) -> p j n", n=64),
                                         banks[2 + half][:, :].rearrange("p (j n) -> p j n", n=64),
                                         pen[:, 8 * half:8 * half + 8].unsqueeze(2).to_broadcast([P, 8, 64]), ALU.add)
                m.then_inc(z_sev, 1)
                ve.wait_ge(z_sev, i + 1)
                link(ve.tensor_reduce(st[:, 37:38], sS, AX, ALU.max))
                ve.tensor_scalar(st[:, 42:43], st[:, 37:38], -SCALE, None, ALU.mult).then_inc(z_nm, 1)

            def smp_norm(i):
                for j in range(3):
                    ve.wait_ge(z_ex, 3 * i + j + 1)
                    link(ve.tensor_scalar(st[:, 44 + j:45 + j], st[:, 44 + j:45 + j], TINY, None, ALU.max))
                    link(ve.reciprocal(st[:, 56 + j:57 + j], st[:, 44 + j:45 + j]))
                    if j == 0:
                        ve.tensor_scalar(sM, sM, st[:, 56:57], None, ALU.mult).then_inc(z_nd, 1)
                    elif j == 1:
                        link(ve.tensor_tensor(st[:, 57:58], st[:, 57:58], gateS[:, i, 1:2], ALU.mult))
                        ve.tensor_scalar(pcg[:, 0:NCMP], pcn[:, 1:1 + NCMP], gateS[:, i, 2:3], None, ALU.mult)
                        ve.tensor_scalar(sW, sW, st[:, 57:58], None, ALU.mult).then_inc(z_nd, 1)
                    else:
                        ve.tensor_tensor(st[:, 58:59], st[:, 58:59], gateS[:, i, 0:1], ALU.mult).then_inc(z_rr, 1)

            def smp_turned(i):
                for j in (1, 3, 5):
                    ve.wait_ge(z_tr, 6 * i + j + 1)
                    if i and j == 1:
                        ve.wait_ge(z_vd[1], i)
                    if j < 5:
                        ve.tensor_copy(pt[:, j, :], banks[4][:, :]).then_inc(z_tD, 1)
                    else:
                        ve.tensor_copy(pt[0:64, j, :], banks[4][0:64, :]).then_inc(z_tD, 1)

            smp_blocks(0)
            for i in range(4):
                smp_max(i)
                if i + 1 < 4:
                    smp_blocks(i + 1)
                smp_norm(i)
                smp_turned(i)

            for c in range(KD):
                ve.wait_ge(s_br, c + 1)
                ve.tensor_tensor(mT[:, c, :], mT[:, c, :], banks[2 * (c % 2)][:, 0:N], ALU.mult)
                link(ve.tensor_tensor(mT[:, 8 + c, :], mT[:, 8 + c, :], banks[2 * (c % 2) + 1][:, 0:N], ALU.mult))
                ve.tensor_tensor(mT[:, c, :], mT[:, c, :], mT[:, 8 + c, :], ALU.add).then_inc(s_mg, 1)
            tmp = sample_part

            def residual(c, bank, g0, s):
                if c:
                    ve.wait_ge(s, c)
                ve.scalar_tensor_tensor(xT[:, c, 0:NP_], bank[:, 0:NP_], mod[:, g0 + c, 0:1], xT[:, c, 0:NP_], ALU.mult, ALU.add)
                link(ve.tensor_tensor(tmp.rearrange("p (b q) -> p b q", q=NQ), bank[:, NP_:N].rearrange("p (b q) -> p b q", q=NQ),
                                      mod[:, g0 + c, 1:NC].unsqueeze(2).to_broadcast([P, NB, NQ]), ALU.mult))
                ve.tensor_tensor(xT[:, c, NP_:N], xT[:, c, NP_:N], tmp, ALU.add).then_inc(s, 1)

            for c in range(KD):
                ve.wait_ge(s_op, c + 1)
                residual(c, banks[4 + c % 2], 16, s_x1)
            ve.wait_ge(s_ss2, 1)
            root(banks[7][:, 0:N], 2)
            link(normed(moe_in))
            modulated(moe_in, moe_in, scl[:, 1], mod[:, 24:32, :]).then_inc(s_h2, 1)

            ve.wait_ge(s_lg, 1)
            R = slice(0, RT)
            lg = at(rt, 4, 36)
            g4 = at(rt + 160, 4, 4)
            e8 = at(rt + 400, 4, 8)
            oh = at(rt + 180, 4, 4)
            m1 = at(rt + 200, 4)
            gw = at(rt + 204, 4)
            v2 = at(rt + 208, 4)
            big = at(rt + 240, 4, 8, 4)
            oh1, oh2, e2 = at(rt + 440, 4, 8), at(rt + 480, 4, 8), at(rt + 520, 4, 8)

            def wide(ap, n):
                return ap[R].unsqueeze(2).to_broadcast([RT, 4, n])

            def first_best(dst, src, best, n):
                down = idx[R, 0:n].unsqueeze(1).to_broadcast([RT, 4, n])
                link(ve.tensor_tensor(dst[R], src[R], wide(best, n), ALU.is_equal))
                link(ve.tensor_tensor(e2[R, :, 0:n], dst[R], down, ALU.mult))
                link(ve.scalar_tensor_tensor(dst[R], dst[R], 64.0, e2[R, :, 0:n], ALU.mult, ALU.subtract))
                link(ve.tensor_reduce(m1[R], dst[R], AX, ALU.max))
                link(ve.tensor_tensor(dst[R], dst[R], wide(m1, n), ALU.is_equal))

            link(ve.tensor_copy(lg[R], banks[0][R, 0:144].rearrange("p (t n) -> p t n", n=36)))
            link(ve.tensor_reduce(m1[R], lg[R, :, 0:4], AX, ALU.max))
            ve.tensor_tensor(g4[R], lg[R, :, 0:4], wide(m1, 4), ALU.subtract).then_inc(s_lc, 1)
            ve.wait_ge(s_le, 1)
            link(ve.tensor_reduce(gw[R], g4[R], AX, ALU.add))
            link(ve.reciprocal(gw[R], gw[R]))
            link(ve.tensor_reduce(v2[R], g4[R], AX, ALU.max))
            first_best(oh, g4, v2, 4)
            for t in range(4):
                m = ve.tensor_tensor(big[R, t], lg[R, t, 4:36].rearrange("p (g e) -> p e g", e=8),
                                     oh[R, t].unsqueeze(1).to_broadcast([RT, 8, 4]), ALU.mult)
            link(m)
            link(ve.tensor_reduce(e8[R], big[R], AX, ALU.add))
            link(ve.tensor_reduce(m1[R], e8[R], AX, ALU.max))
            ve.tensor_tensor(e8[R], e8[R], wide(m1, 8), ALU.subtract).then_inc(s_l8, 1)
            ve.wait_ge(s_l8e, 1)
            link(ve.tensor_reduce(v2[R], e8[R], AX, ALU.max))
            first_best(oh1, e8, v2, 8)
            rest = at(rt + 560, 4, 8)
            link(ve.scalar_tensor_tensor(rest[R], oh1[R], -4.0, e8[R], ALU.mult, ALU.add))
            link(ve.tensor_reduce(v2[R], rest[R], AX, ALU.max))
            first_best(oh2, rest, v2, 8)
            tot, wt1, wt2 = at(rt + 212, 4), at(rt + 216, 4), at(rt + 220, 4)
            link(ve.tensor_scalar(tot[R], v2[R], 1.0, None, ALU.add))
            link(ve.reciprocal(tot[R], tot[R]))
            link(ve.tensor_tensor(wt1[R], tot[R], gw[R], ALU.mult))
            link(ve.tensor_tensor(wt2[R], wt1[R], v2[R], ALU.mult))
            first, second, chosen = at(rt + 600, 4, E), at(rt + 730, 4, E), at(rt + 900, 4, E)
            for ch, o in ((first, oh1), (second, oh2)):
                for t in range(4):
                    m = ve.tensor_tensor(ch[R, t].rearrange("p (g e) -> p g e", e=8), o[R, t].unsqueeze(1).to_broadcast([RT, 4, 8]),
                                         oh[R, t].unsqueeze(2).to_broadcast([RT, 4, 8]), ALU.mult)
            link(m)
            ve.tensor_tensor(chosen[R], first[R], second[R], ALU.add).then_inc(s_m, 1)
            ve.wait_ge(s_pos, 1)
            pos, over, tmp4 = at(rt + 1030, 4, E), at(rt + 1160, 4, E), big[:, :, :, :].rearrange("p a b c -> p a (b c)")
            cnt, more, far = at(rt + 1300, E), at(rt + 1332, E), at(rt + 1364, E)
            ends = [at(rt + 1400 + 48 * k, 48) for k in range(2)]
            link(ve.tensor_copy(pos[R], banks[1][R, 0:4 * E].rearrange("p (t e) -> p t e", e=E)))
            link(ve.tensor_copy(cnt[R], banks[1][R, 4 * E:5 * E]))
            link(ve.tensor_scalar(more[R], cnt[R], CAP + 0.5, None, ALU.is_ge))
            for n in range(2, N // CAP):
                link(ve.scalar_tensor_tensor(more[R], cnt[R], n * CAP + 0.5, more[R], ALU.is_ge, ALU.add))
            for k in range(2):
                link(ve.memset(ends[k][R, 0:16], 0.0))
            link(ve.tensor_copy(ends[0][R, 16:48], more[R]))
            for n, step in enumerate((1, 2, 4, 8, 16)):
                a, b = ends[n % 2], ends[1 - n % 2]
                link(ve.tensor_tensor(b[R, 16:48], a[R, 16:48], a[R, 16 - step:48 - step], ALU.add))
            end = ends[1][R, 16:48]
            link(ve.tensor_tensor(far[R], end, more[R], ALU.subtract))
            link(ve.tensor_scalar(far[R], far[R], float(CAP), float(CAP * (E - 1)), ALU.mult, ALU.add))
            link(ve.tensor_tensor(far[R], far[R], cst[R, C_E:C_E + E], ALU.subtract))
            link(ve.tensor_scalar(over[R], pos[R], CAP - 0.5, None, ALU.is_ge))
            link(ve.tensor_tensor(over[R], over[R], far[R].unsqueeze(1).to_broadcast([RT, 4, E]), ALU.mult))
            link(ve.tensor_tensor(pos[R], pos[R], cst[R, C_E:C_E + E].unsqueeze(1).to_broadcast([RT, 4, E]), ALU.add))
            link(ve.tensor_tensor(pos[R], pos[R], over[R], ALU.add))
            rowf = at(rt + 224, 2, 4)
            for r, ch in enumerate((first, second)):
                link(ve.tensor_tensor(tmp4[R], ch[R], pos[R], ALU.mult))
                link(ve.tensor_reduce(rowf[R, r], tmp4[R], AX, ALU.add))
            ve.tensor_copy(index[:, :], rowf[R].rearrange("p r t -> p (r t)")).then_inc(s_idx, 1)
            which, tab = big[0:1].rearrange("p a b c -> p (a b c)"), at(rt + 1500, 16)
            for k in range(EXTRA):
                link(ve.tensor_scalar(which[:, 0:E], ends[1][0:1, 16:48], k + 0.5, None, ALU.is_le))
                link(ve.tensor_reduce(tab[0:1, 1 + k:2 + k], which[:, 0:E], AX, ALU.add))
            link(ve.tensor_scalar(tab[0:1, 1:1 + EXTRA], tab[0:1, 1:1 + EXTRA], E - 1.0, None, ALU.min))
            link(ve.tensor_copy(tab[0:1, 0:1], ends[1][0:1, 47:48]))
            ve.tensor_copy(extra[:, :], tab[0:1, 0:1 + EXTRA]).then_inc(s_flag, 1)

            def rows_out(p, q, first=False):
                ve.wait_ge(s_xt, p + 1)
                if not first:
                    ve.wait_ge(s_hd, p - 1)
                ve.tensor_copy(xeT[q][:, 4:8, :], banks[1][:, :].rearrange("p (k n) -> p k n", n=P)).then_inc(s_xtD, 1)

            def pair_act(p, q):
                ve.wait_ge(s_sil, p + 1)
                ve.tensor_tensor(actS[:, q, :], silS[:, q, :], banks[2 + q][:, 256:512], ALU.mult).then_inc(s_ac, 1)
                ve.wait_ge(s_at, p + 1)
                ve.tensor_copy(actT[:, q].rearrange("p j n -> p (j n)"), banks[4 + q][:, 0:256]).then_inc(s_atE, 1)

            def pair_out(p, q, first=False):
                ve.wait_ge(s_od, p * 2 + 2)
                if not first:
                    ve.wait_ge(s_st[q], (p - q) * 8)
                ve.tensor_copy(yeS[q][:, 512:1024], banks[7][:, :]).then_inc(s_yD, 1)

            rows_out(0, 0, True)
            rows_out(1, 1, True)
            pair_act(0, 0)
            rows_out(2, 0)
            pair_out(0, 0, True)
            pair_act(1, 1)
            rows_out(3, 1)
            pair_out(1, 1, True)
            pair_act(2, 0)
            with ve.Fori(1, PAIRS // 2 - 1) as i:
                for q in range(2):
                    p = i * 2 + q
                    rows_out(p + 2, q)
                    pair_out(p, q)
                    pair_act(p + 1, 1 - q)
            p = PAIRS - 2
            pair_out(p, 0)
            pair_act(p + 1, 1)
            pair_out(p + 1, 1)

            ve.wait_ge(s_flag, 1)
            n_extra = ve.value_load(extra[0:1, 0:1], min_val=0, max_val=EXTRA)
            for x in range(EXTRA // 2):
                p, q = PAIRS + x, x % 2
                with ve.If(n_extra > 2 * x):
                    rows_out(p, q)
                    pair_act(p, q)
                    pair_out(p, q)
            ve.wait_ge(s_yg, 16 * 8)
            for t in range(4):
                ve.wait_ge(s_g1, t + 1)
                ve.scalar_tensor_tensor(yG[0][R, t, :], yG[1][R, t, :], wt2[R, t:t + 1], yG[0][R, t, :], ALU.mult, ALU.add)\
                    .then_inc(s_yr, 1)
            for c in range(KD):
                ve.wait_ge(s_yt, c + 1)
                residual(c, banks[6 + c % 2], 40, s_x2)
            ve.wait_ge(s_ss3, 1)
            root(banks[0][:, 0:N], 3)
            link(normed(xT))
            ve.tensor_tensor(xT, xT, gains[:, 2].unsqueeze(2).to_broadcast([P, KD, N]), ALU.mult).then_inc(s_fin, 1)

        @block.gpsimd
        def _(po):
            zeros = vcm.rearrange("p b n -> p (b n)")
            po.memset(zeros, 0.0).then_inc(s_z, 1)
            po.wait_ge(s_ada, ADA_TILES - 1)
            po.dma_start(o_win[0], win_state[0]).then_inc(s_out, 16)
            po.dma_start(o_win[1], win_state[1]).then_inc(s_out, 16)
            po.wait_ge(s_z, 1)
            po.dma_start(o_zero, zeros[:, 0:256]).then_inc(s_zf, 16)
            for n in range(PAIRS + EXTRA // 2):
                po.dma_start(x_rows[P * n:P * (n + 1), :], zeros).then_inc(s_zf, 16)
            for n in range(PAIRS, PAIRS + EXTRA // 2):
                po.dma_start(y_rows[P * n:P * (n + 1), :], zeros).then_inc(s_zf, 16)
            po.wait_ge(s_rope, ROT)
            po.dma_start(o_kt, kA).then_inc(s_out, 16)
            po.wait_ge(s_pev, ROT + 1)
            po.dma_start(o_small, kvc).then_inc(s_out, 16)
            po.wait_ge(s_rowV, 3)
            po.dma_start(o_va[:, 0:2, :], vA[:, 0:2, :]).then_inc(s_out, 16)
            po.dma_start(o_va[0:64, 2, :], vA[0:64, 2, :]).then_inc(s_out, 16)
            po.wait_ge(s_rowA, 6)
            po.dma_start(o_vs[:, 0:2, :], vS[:, 0:2, :]).then_inc(s_out, 16)
            po.dma_start(o_vs[0:64, 2, :], vS[0:64, 2, :]).then_inc(s_out, 16)
            po.dma_start(scratch, gate[0:NS, 2, :]).then_inc(s_gd, 16)
            po.wait_ge(s_gd, 16)
            by_head = scratch.rearrange("(i b q) (h j) -> b h q i j", b=2, q=NQ, j=3)
            for b in range(2):
                for h in range(H):
                    row = 64 * b + 8 * h
                    po.dma_start(gateS[row:row + 8, :, :], by_head[b, h]).then_inc(s_gs, 16)

            po.wait_ge(s_zf, 16 * (PAIRS + EXTRA + 1))
            po.wait_ge(s_idx, 1)
            po.wait_ge(s_hr, 8)
            for r in range(2):
                for t in range(4):
                    po.indirect_dma_start(out=x_rows, out_offset=bass.IndirectOffsetOnAxis(index[:, 4 * r + t:4 * r + t + 1], 0),
                                          in_=hR[0:RT, t, :], in_offset=None, bounds_check=(E + EXTRA) * CAP - 1,
                                          oob_is_err=False).then_inc(s_xe, 16)
            po.wait_ge(s_dn, 1)
            for r in range(2):
                for t in range(4):
                    po.indirect_dma_start(out=yG[r][0:RT, t, :], out_offset=None, in_=y_rows,
                                          in_offset=bass.IndirectOffsetOnAxis(index[:, 4 * r + t:4 * r + t + 1], 0),
                                          bounds_check=(E + EXTRA) * CAP - 1, oob_is_err=False).then_inc(s_yg, 16)


def constants():
    import numpy as np
    c = np.zeros((P, C_ALL), np.float32)
    r = np.arange(P)
    c[:, C_ID:C_ID + P] = np.eye(P)
    tri = np.where(r[None, :] <= r[:, None], 0.0, NEG)
    c[:, C_TRI:C_TRI + P] = tri
    c[:, C_TRI + 256:C_TRI + 384] = tri
    b2, g, q = r // 64, (r % 64) // 32, r % 8
    c[:, C_R:C_R + P] = (b2[:, None] == b2) & (g[:, None] == g) & (q[:, None] == q)
    for i in range(4):
        tok = np.arange(NS)
        ok = (tok[None, :] // NQ == (2 * i + b2)[:, None]) & (tok[None, :] % NQ <= q[:, None])
        c[:, C_NEW + NS * i:C_NEW + NS * (i + 1)] = np.where(ok, 0.0, NEG)
    c[:, C_WIN:C_WIN + 8] = np.where(np.arange(8)[None, :] >= q[:, None], 0.0, NEG)
    for t in range(2):
        ok = (np.arange(NCMPP) * 16 + 31)[None, :] <= (r + P * t)[:, None]
        c[:, C_CADD + NCMPP * t:C_CADD + NCMPP * (t + 1)] = np.where(ok, 0.0, NEG)
        c[:, C_C01 + NCMPP * t:C_C01 + NCMPP * (t + 1)] = ok
    c[:, C_IDX:C_IDX + 16] = np.arange(1, 17)
    c[:, C_ONE:C_ONE + P] = 1.0
    c[(r // 64) * 64 + (r % 64 + 32) % 64, C_PERM + r] = 1.0
    pos = np.concatenate([np.arange(NP_), np.tile(1024 + np.arange(NQ), NB)]).astype(np.float32)
    inv = np.float32(10000.0) ** (-np.arange(32, dtype=np.float32) / np.float32(32))
    ang = (inv[r % 32][:, None] * pos[None, :]).astype(np.float32)
    c[:, C_COS:C_COS + N] = np.cos(ang)
    c[:, C_SIN:C_SIN + N] = np.sin(ang) * np.where(r % 64 < 32, -1.0, 1.0)[:, None]
    c[:, C_LT:C_LT + P] = r[:, None] < r[None, :]
    c[:, C_E:C_E + E] = CAP * np.arange(E)
    c[:, C_K:C_K + EXTRA] = np.arange(EXTRA)
    c[:, C_SEL:C_SEL + NC] = (r % 64)[:, None] == np.arange(NC)[None, :]
    return c


def kernel(**inputs):
    import numpy as np
    import concourse.bacc as _bacc
    from concourse.bass_utils import run_bass_kernel_spmd as _run

    a = {k: np.asarray(v) for k, v in inputs.items()}
    c_ = np.ascontiguousarray

    def kp(w):
        return w.reshape(-1, P, w.shape[-1]).transpose(1, 0, 2)

    cond = np.concatenate([a["c_prompt"], a["c_sample"]]).T
    xt = np.concatenate([a["x_prompt"].reshape(-1, D), a["x_sample"].reshape(-1, D)]).T
    w1 = [a["w_cmp_k1"][0], a["w_cmp_v1"][0]]
    vec = np.concatenate([
        a["b_ada"][0].reshape(48, P).T,
        np.stack([a["norm_mix_g"][0], a["norm_ffn_g"][0], a["norm_final_g"]]).reshape(3 * KD, P).T,
        a["w_cmp_k2"][0], a["w_cmp_v2"][0],
        a["pe_cmp_k"][0].reshape(16, P).T, a["pe_cmp_v"][0].reshape(16, P).T,
        kp(np.concatenate([a["w_router_grp"][0], a["w_router_exp"][0]], axis=1)).reshape(P, -1),
        kp(cond).reshape(P, -1)], axis=1)
    w = a["w_in"][0]
    q_b = w[:, 1536:2048].reshape(D, 2, 4, DH).transpose(0, 2, 1, 3).reshape(D, 512)
    gates = w[:, 2816:2840].reshape(D, H, 3)[:, :, [1, 2, 0]].reshape(D, GATES)
    turned = np.concatenate([w[:, 0:1024], q_b, w[:, 2048:2176], w[:, 2304:2432], w[:, 2560:2688],
                             w[:, 2176:2304], w[:, 2840:4888]], axis=1)
    rows = np.concatenate([w[:, 1024:1536], w[:, 2432:2560], w[:, 2688:2816], gates,
                           np.zeros((D, 232), w.dtype)], axis=1)
    w_in = kp(np.concatenate([turned, rows], axis=1)).reshape(P, KD, 10, 512).transpose(2, 0, 1, 3)

    def pages_t(x):
        x = x[0].reshape(NPHYS, PAGE, -1, P)
        return x.transpose(0, 3, 2, 1).reshape(NPHYS, P, -1)

    def pages_c(x):
        x = x[0].reshape(NPHYS, 8, 8, 2, 2, DH)
        return x.transpose(0, 3, 5, 2, 4, 1).reshape(NPHYS, P, P)

    ins = {
        "vec": vec, "x_t": kp(xt), "pages": a["page_table"].reshape(1, -1).astype(np.int32),
        "w_ada": kp(a["w_ada"][0]).reshape(P, KD, ADA_TILES, 512).transpose(2, 0, 1, 3),
        "w_in": w_in,
        "w1": np.stack([kp(x) for x in w1], axis=1),
        "cmp_pages": np.concatenate([pages_c(a["cache_nsa_cmp_k"]), pages_c(a["cache_nsa_cmp_v"])], axis=2),
        "k_pages": np.concatenate([pages_t(a["cache_moba_k"]), pages_t(a["cache_nsa_slc_k"])], axis=2),
        "v_pages": np.concatenate([a["cache_moba_v"][0].reshape(NPHYS, PAGE, 512),
                                   a["cache_nsa_slc_v"][0].reshape(NPHYS, PAGE, P)], axis=2),
        "win": np.stack([a["state_nsa_win_k"][0].reshape(NB, WIN, P).transpose(0, 2, 1),
                         a["state_nsa_win_v"][0].reshape(NB, 4, P, P).transpose(0, 2, 1, 3).reshape(NB, P, WIN)]),
        "w_br": kp(np.concatenate([a["w_br_a"][0],
                                   a["w_br_b"][0].reshape(2, 4, DH, D).transpose(1, 0, 2, 3).reshape(512, D)])),
        "w_out": kp(a["w_out"][0]),
        "w_ein": a["w_expert_in"][0].reshape(E, KD, P, 512).transpose(0, 2, 1, 3).reshape(E, P, -1),
        "w_eout": a["w_expert_out"][0].reshape(E, 2, P, D).transpose(0, 2, 1, 3).reshape(E, P, -1),
        "consts": constants(),
        "win_state": np.stack([a["state_nsa_win_k"][0].reshape(NB, WIN, P)[:, NQ:],
                               a["state_nsa_win_v"][0].reshape(NB, WIN, P)[:, NQ:]]).reshape(2, -1, 1008),
    }
    outs = {"y": (P, KD, N), "kt": (P, 4, N), "small": (P, 4, N), "va": (P, 3, 512), "vs": (P, 3, 256),
            "zero": (P, 256), "win_new": (2, 512, 1008)}
    nc = _bacc.Bacc("TRN2", target_bir_lowering=False, num_devices=1)
    args, arrays = [], {}
    for name, x in ins.items():
        arrays[f"in_{name}"] = c_(x)
        args.append(nc.dram_tensor(f"in_{name}", x.shape, mybir.dt.from_np(x.dtype), kind="ExternalInput").ap())
    for name, shape in outs.items():
        args.append(nc.dram_tensor(f"out_{name}", shape, F32, kind="ExternalOutput").ap())
    args.append(nc.dram_tensor("gates_scratch", (NS, GATES), F32, kind="Internal").ap())
    for name in ("x_rows", "y_rows"):
        args.append(nc.dram_tensor(name, ((E + EXTRA) * CAP, D), F32, kind="Internal").ap())
    build(nc, *args)
    got = _run(nc, [arrays], core_ids=[0]).results[0]
    y = got["out_y"].transpose(2, 1, 0).reshape(N, D)
    kt = got["out_kt"].transpose(2, 1, 0).reshape(N, 512)
    kc, ks, kw, vc = (got["out_small"][:, j, :].T for j in range(4))
    va = got["out_va"].transpose(1, 0, 2).reshape(3 * P, 512)[:N]
    vsw = got["out_vs"].transpose(1, 0, 2).reshape(3 * P, 256)[:N]
    vs, vw = vsw[:, 0:128], vsw[:, 128:256]
    zero = got["out_zero"].reshape(256, 128)
    old = got["out_win_new"].reshape(2, NB, WIN - NQ, P)

    def p_(x):
        return c_(x[:NP_].reshape(1, 1, NP_, -1, DH))

    def s_(x):
        return c_(x[NP_:].reshape(1, NB, NQ, -1, DH))

    def pw(x):
        return c_(np.concatenate([zero, x[:NP_]]).reshape(1, 1, WIN, 2, DH))

    def sw(j, x):
        return c_(np.concatenate([old[j], x[NP_:].reshape(NB, NQ, P)], axis=1).reshape(1, NB, WIN, 2, DH))

    return (c_(y[:NP_].reshape(1, NP_, D)), c_(y[NP_:].reshape(NB, NQ, D)),
            p_(kt), p_(va), p_(kc), p_(vc), p_(ks), p_(vs), pw(kw), pw(vw),
            s_(kt), s_(va), s_(kc), s_(vc), s_(ks), s_(vs), sw(0, kw), sw(1, vw))
```

```python
from contextlib import ExitStack

import concourse.bass as bass
from concourse import mybir

F32 = mybir.dt.float32
I32 = mybir.dt.int32
ALU = mybir.AluOpType
ACT = mybir.ActivationFunctionType
AX = mybir.AxisListType.X

P = 128
D = 1024
KD = D // P
NP_, NB, NQ = 256, 8, 8
NS = NB * NQ
N = NP_ + NS
NC = 1 + NB
PAGES = 8
PAGE = 128
NPHYS = 80
H = 8
DH = 64
NCMP = 63
NCMPP = 15
E = 32
EPS = 1e-6
TINY = 1e-30
NEG = -1e30
SCALE = DH ** -0.5
WIN = 512
TOK = [(0, 128), (128, 128), (256, 64)]
GATES = 3 * H
ADA_TILES = 12
T_TILES = 8
ROT = 15
SLOT = KD * 512
RT = 80
CAP = 64
EXTRA = 10
PAIRS = E // 2

C_ID, C_TRI, C_R, C_NEW = 0, 128, 512, 640
C_WIN = C_NEW + 4 * NS
C_CADD = C_WIN + 8
C_C01 = C_CADD + 2 * NCMPP
C_IDX = C_C01 + 2 * NCMPP
C_ONE = C_IDX + 16
C_PERM = C_ONE + 128
C_COS = C_PERM + 128
C_SIN = C_COS + N
C_LT = C_SIN + N
C_E = C_LT + 128
C_K = C_E + E
C_SEL = C_K + 1
C_ALL = C_SEL + NC
V_B, V_G = 0, 48
V_W2K = V_G + 3 * KD
V_W2V = V_W2K + DH
V_PE = V_W2V + DH
V_WR = V_PE + 32
V_C = V_WR + KD * 36
V_ALL = V_C + KD * NC


def build(nc, vec, x_t, pages, w_ada, w_in, w1, cmp_pages, k_pages, v_pages, win, w_br, w_out,
          w_ein, w_eout, consts, win_state,
          o_y, o_kt, o_small, o_va, o_vs, o_zero, o_win, scratch, x_rows):
    with ExitStack() as ctx:
        def sem(name):
            return ctx.enter_context(nc.semaphore(name))

        TOTAL = 53000
        arena = ctx.enter_context(nc.sbuf_tensor("arena", [P, TOTAL], F32))
        index = ctx.enter_context(nc.sbuf_tensor("expert_rows", [RT, 8], I32))
        extra = ctx.enter_context(nc.sbuf_tensor("extra_tiles", [1, 1 + EXTRA], I32))
        page_row = ctx.enter_context(nc.sbuf_tensor("page_row", [1, NB * PAGES], I32))
        banks = [ctx.enter_context(nc.psum_tensor(f"bank{i}", [P, 512], F32)) for i in range(8)]

        def at(off, *dims):
            size = 1
            for d in dims:
                size *= d
            assert off + size <= TOTAL, (off, size)
            ap = arena[:, off:off + size]
            if len(dims) == 2:
                return ap.rearrange("p (a b) -> p a b", b=dims[1])
            if len(dims) == 3:
                return ap.rearrange("p (a b c) -> p a b c", b=dims[1], c=dims[2])
            if len(dims) == 4:
                return ap.rearrange("p (a b c d) -> p a b c d", b=dims[1], c=dims[2], d=dims[3])
            return ap

        place = [0]

        def keep(*dims):
            size = 1
            for d in dims:
                size *= d
            place[0] += size
            return at(place[0] - size, *dims)

        cst = keep(C_ALL)
        vecs = keep(V_ALL)
        mod = keep(48, NC)
        scl = keep(2, KD, NC)
        xT = keep(KD, N)
        mT = keep(16, N)
        OT = place[0]
        oTa = keep(4, N)
        oTb = keep(4, N)
        rstd = keep(N)
        sample_part = keep(NS)
        slot = keep(1)
        assert place[0] <= 15000, place[0]
        PJ = place[0]
        qA, kA, qB = keep(4, N), keep(4, N), keep(4, N)
        kvc = keep(4, N)
        vA = keep(3, 512)
        vS = keep(3, 256)
        gate = keep(3, GATES)
        gateS = keep(4, 3)
        kcm = keep(NB, NCMP)
        vcm = keep(NB, P)
        kcmp, vcmp = keep(NCMPP), keep(P)
        A = place[0]
        sq = at(A, KD, N)
        hT = at(A + 2560, KD, N)
        ring = [at(A + 5120 + SLOT * k, KD, 512) for k in range(3)]
        qs = at(A + 5120 + 3 * SLOT, 3, N)
        turn = at(A + 5120 + 3 * SLOT + 3 * N, 2, 2, N)
        condS = at(A + 5120 + 3 * SLOT, KD, 64)
        adaR = [at(A + 5120 + 3 * SLOT + 3 * N + 512 * k, 512) for k in range(2)]
        kx = at(A + 5120 + 3 * SLOT + 3 * N, 2, 2, P)
        w1_sb = [at(A, 16, P), at(OT, 16, P)]
        XCO = A + 5120 + 3 * SLOT + 7 * N
        xc = [at(XCO, 32, 256), at(A + 5376, 32, 256)]
        HC = A + 2560
        hA, hB, hS = at(HC, 4, 2, 64), at(HC + 512, 4, 2, 64), at(HC + 1024, 8, 63)
        gl = at(HC + 1536, 2, 4, 2, 63)
        glp = at(HC + 2544, 2, 2, NCMPP)
        peb = at(HC + 2604, 2)
        UNIT = PAGES * 640 + WIN
        kU = [at(A + UNIT * b, UNIT) for b in range(2)]
        vU = [at(A + UNIT * (2 + b), UNIT) for b in range(2)]
        B = A + 4 * UNIT
        sM, sS, sW = at(B, 1024 + NS), at(B + 1088, 1024 + NS), at(B + 2176, WIN + NS)
        sC = at(B + 2752, 72)
        sPs = [[at(B + 3000 * d + 420 * k, 420) for k in range(3)] for d in range(2)]
        ptP = at(B + 1300, 3, 384)
        ptC = at(B + 2452, 256)
        pcn = at(B + 2824, 66)
        st = at(B + 2890, 64)
        sts = [st, at(B + 2708, 64)]
        oRa, oRb = at(B + 4264, 2, 512), at(B + 5288, 2, 4, P)
        parts = [at(B + 6312 + 384 * k, 3, 2, DH) for k in range(2)]
        pt = at(B + 2960, 6, 512)
        qz = at(B + 6032, 2, 4, 64)
        qzb = at(B + 6544, 2, 64)
        scales = at(B + 6672, 2, 4)
        osA, osB = at(B + 6864, 512), vcmp
        wbr_sb = at(A, 8, D)
        wo_sb = at(PJ, KD, D)
        assert PJ + 8192 <= A and A + 8192 <= A + 2 * UNIT
        moe_in, moe = mT[:, 0:8, :], mT[:, 8:16, :]
        sq2 = at(OT, KD, N)
        table = at(OT, 4, N)
        comb = [at(OT + 4 * N + N * k, N) for k in range(2)]
        comb1 = at(OT + 6 * N, N)
        hR = at(PJ, 4, D)
        rt = PJ + 4096
        X = rt + 1760
        xeS = [at(X + D * k, D) for k in range(2)]
        xeT = [at(X + 2048 + D * k, KD, P) for k in range(2)]
        silS, actS = at(X + 4096, 2, 256), at(X + 4608, 2, 256)
        actT = at(X + 5120, 2, 2, P)
        yeS = [at(X + 5632 + D * k, D) for k in range(2)]
        M0 = TOTAL - 24576
        assert X + 7680 <= M0
        wo2 = [at(M0 + 4096 * k, 2, 2, D) for k in range(2)]
        wi2 = [at(M0 + 8192 * (k + 1), 2, KD, 512) for k in range(2)]
        diag = at(X + 5632, 16, RT)

        ident = cst[:, C_ID:C_ID + 128]
        ones = cst[:, C_ONE:C_ONE + 128]
        cT = vecs[:, V_C:V_C + KD * NC].rearrange("p (k c) -> p k c", c=NC)
        gains = vecs[:, V_G:V_G + 3 * KD].rearrange("p (j k) -> p j k", k=KD)
        w2k, w2v = vecs[:, V_W2K:V_W2K + DH], vecs[:, V_W2V:V_W2V + DH]
        pe = vecs[:, V_PE:V_PE + 32].rearrange("p (v t) -> p v t", t=16)
        w_rt = vecs[:, V_WR:V_WR + KD * 36].rearrange("p (k n) -> p k n", n=36)
        idx = cst[:, C_IDX:C_IDX + 16]

        s_in = sem("inputs_loaded")
        s_w = [sem(f"weight_tile_loaded{k}") for k in range(3)]
        s_w1 = sem("cmp_weights_loaded")
        s_xc = sem("cmp_pages_loaded")
        s_k = [sem(f"keys_loaded{b}") for b in range(2)]
        s_v = [sem(f"values_loaded{b}") for b in range(2)]
        s_wbr, s_wo = sem("branch_weights_loaded"), sem("out_weights_loaded")
        s_wi = [sem(f"expert_in_loaded{k}") for k in range(2)]
        s_wo2 = [sem(f"expert_out_loaded{k}") for k in range(2)]
        s_xl = [sem(f"expert_rows_loaded{k}") for k in range(2)]
        s_xe, s_zf = sem("rows_scattered"), sem("rows_zeroed")
        s_gd, s_gs = sem("gates_in_dram"), sem("gates_by_row")
        s_out = sem("outputs_written")
        s_silu, s_sq, s_ss = sem("cond_silu"), sem("squares"), sem("square_sums")
        s_cz, s_adr = sem("cond_padding"), sem("ada_rows_out")
        s_adt = sem("ada_tile_turned")
        s_kx, s_kxe = sem("prompt_pairs"), sem("prompt_pairs_out")
        s_ada, s_mod, s_h = sem("ada_tile_done"), sem("mod_written"), sem("h_ready")
        s_proj, s_pev = sem("proj_chunk_done"), sem("proj_evacuated")
        s_rot, s_rope, s_t1 = sem("rotated"), sem("rope_done"), sem("rope_cos_part")
        s_row, s_rowA, s_rowV = sem("row_proj_done"), sem("row_small_evac"), sem("row_v_evac")
        s_pb, s_pbv = sem("pe_bias_sum"), sem("pe_bias_ready")
        s_cp, s_cpg, s_cp2, s_cpe = sem("cmp_prompt_hid"), sem("cmp_prompt_gelu"), sem("cmp_prompt_out"), sem("cmp_prompt_ready")
        s_cAB, s_cA, s_cB = sem("cmp_hid"), sem("cmp_first_half_out"), sem("cmp_second_half_out")
        s_cS, s_cg, s_c2, s_kcm = sem("cmp_hid_sum"), sem("cmp_gelu"), sem("cmp_out"), sem("cmp_ready")
        s_sc, s_sev, s_nm, s_exp = sem("p_scores"), sem("p_scores_out"), sem("p_max"), sem("p_exp")
        s_cmk, s_tr = sem("p_cmp_masked"), sem("p_turned")
        s_ptA, s_ptD, s_pv = sem("p_probs_moba_out"), sem("p_probs_nsa_out"), sem("p_pv")
        s_osc, s_oad, s_ot = sem("p_out_scaled"), sem("p_out_added"), sem("p_out_turned")
        s_otA, s_otD = sem("p_out_cols_act"), sem("p_out_cols_dve")
        z_main, z_wev = sem("s_page_scores"), sem("s_window_out")
        z_qz, z_kd, z_small, z_sev = sem("q_blocks"), [sem(f"keys_used{b}") for b in range(2)], sem("s_scores"), sem("s_scores_out")
        z_cm, z_ce, z_pcn, z_imp, z_gsr = sem("cmp_max"), sem("cmp_exp"), sem("cmp_probs"), sem("cmp_group_sums"), sem("cmp_group_read")
        z_nm, z_ex, z_rr = sem("s_max"), sem("s_exp"), sem("s_scales")
        z_oA, z_oB, z_ot = sem("s_moba_rows_out"), sem("s_nsa_rows_out"), sem("s_out_turned")
        z_tr, z_tA, z_tD = sem("s_turned"), sem("s_turned_out_act"), sem("s_turned_out_dve")
        z_vd, z_oev = [sem(f"values_used{b}") for b in range(2)], sem("s_o_out")
        s_br, s_mg, s_op, s_x1 = sem("branch_proj"), sem("merged"), sem("out_proj"), sem("x1_chunk")
        s_sq2, s_ss2, s_h2 = sem("squares2"), sem("square_sums2"), sem("moe_in_ready")
        s_lg, s_lc, s_le, s_l8, s_l8e = sem("logits"), sem("logit_diffs"), sem("group_exp"), sem("expert_diffs"), sem("expert_exp")
        s_m, s_pos, s_idx, s_flag = sem("chosen"), sem("positions"), sem("indices_ready"), sem("extra_tiles_ready")
        s_ht, s_hr = sem("h_rows_turned"), sem("h_rows_ready")
        s_xt, s_xtA, s_xtD = sem("pair_rows_turned"), sem("pair_rows_out_act"), sem("pair_rows_out_dve")
        s_hd, s_sil, s_ac, s_at, s_atE = (sem("pair_hidden"), sem("pair_silu"), sem("pair_act"), sem("pair_act_turned"),
                                          sem("pair_act_out"))
        s_od, s_yA, s_yD = sem("pair_out"), sem("pair_out_act"), sem("pair_out_dve")
        s_dg, s_tb, s_tbA, s_tbD = sem("choice_diagonals"), sem("choice_tables"), sem("tables_out_act"), sem("tables_out_dve")
        s_cm, s_cw, s_cs, s_slot = sem("choices_found"), sem("choices_weighed"), sem("combination_ready"), sem("slots_of_pair")
        s_cmb, s_cmc, s_acc = sem("pair_combined"), sem("chunk_combined"), sem("chunk_added")
        s_x2, s_sq3, s_ss3, s_fin = (sem("x2_chunk"), sem("squares3"), sem("square_sums3"),
                                           sem("final_ready"))
        x_w = [sem(f"extra_weights_loaded{k}") for k in range(2)]
        s_ch, s_cha, s_chp = sem("vector_chain"), sem("scalar_chain"), sem("pool_chain")
        s_z, s_y = sem("zeros_ready"), sem("y_written")
        s_ms, s_rms = sem("mean_square"), sem("root_mean_square")

        block = ctx.enter_context(nc.Block())

        @block.sync
        def _(sp):
            sp.dma_start(vecs, vec).then_inc(s_in, 16)
            sp.dma_start(cst, consts).then_inc(s_in, 16)
            sp.dma_start(xT, x_t).then_inc(s_in, 16)
            sp.dma_start(page_row[:, :], pages).then_inc(s_in, 16)

            def page_of(b, p):
                return sp.value_load(page_row[0:1, b * PAGES + p:b * PAGES + p + 1], min_val=0, max_val=NPHYS - 1)

            def cmp_half(half):
                for j in range(32):
                    pg = page_of(4 * half + j // PAGES, j % PAGES)
                    sp.dma_start(xc[half][:, j, :],
                                 cmp_pages[bass.ds(pg, 1), :, :].rearrange("o p n -> (o p) n")).then_inc(s_xc, 16)

            def unit(b, dst, src, w, s):
                for p in range(PAGES):
                    pg = page_of(b, p)
                    sp.dma_start(dst[:, p * 640:(p + 1) * 640],
                                 src[bass.ds(pg, 1), :, :].rearrange("o p n -> (o p) n")).then_inc(s, 16)
                sp.dma_start(dst[:, PAGES * 640:UNIT], win[w, b]).then_inc(s, 16)

            for n in range(ADA_TILES + 10):
                if n >= 3 and n - 3 < ADA_TILES:
                    sp.wait_ge(s_ada, n - 2)
                elif n >= 3:
                    sp.wait_ge(s_proj, 4 * (n - 2 - ADA_TILES))
                if n < ADA_TILES:
                    sp.dma_start(ring[n % 3], w_ada[n]).then_inc(s_w[n % 3], 16)
                else:
                    sp.dma_start(ring[n % 3], w_in[n - ADA_TILES]).then_inc(s_w[n % 3], 16)
                if n == ADA_TILES + 4:
                    sp.wait_ge(s_h, 1)
                    for v in range(2):
                        sp.dma_start(w1_sb[v], w1[:, v]).then_inc(s_w1, 16)
                if n == ADA_TILES + 5:
                    sp.wait_ge(s_in, 64)
                    cmp_half(0)
            sp.wait_ge(s_row, 6)
            cmp_half(1)
            sp.wait_ge(s_kcm, 4)
            sp.wait_ge(s_cpe, 2)
            def keys(i):
                for b in range(2):
                    if i:
                        sp.wait_ge(z_kd[b], i)
                    unit(2 * i + b, kU[b], k_pages, 0, s_k[b])

            def values(i):
                for b in range(2):
                    if i:
                        sp.wait_ge(z_vd[b], i)
                    unit(2 * i + b, vU[b], v_pages, 1, s_v[b])

            keys(0)
            values(0)
            keys(1)
            for i in range(1, 4):
                if i < 3:
                    keys(i + 1)
                values(i)
            for b in range(2):
                sp.wait_ge(z_kd[b], 4)
            sp.dma_start(wbr_sb, w_br).then_inc(s_wbr, 16)
            for b in range(2):
                sp.wait_ge(z_vd[b], 4)
            sp.dma_start(wo_sb, w_out).then_inc(s_wo, 16)

            def pair_in(p, q):
                sp.dma_start(wi2[q].rearrange("p e k n -> p e (k n)"),
                             w_ein[bass.ds(p * 2, 2), :, :].rearrange("e p n -> p e n")).then_inc(s_wi[q], 16)

            def pair_out(p, q):
                sp.dma_start(wo2[q].rearrange("p e k n -> p e (k n)"),
                             w_eout[bass.ds(p * 2, 2), :, :].rearrange("e p n -> p e n")).then_inc(s_wo2[q], 16)

            def pair_rows(p, q):
                sp.dma_start(xeS[q], x_rows[bass.ds(p * P, P), :]).then_inc(s_xl[q], 16)

            pair_in(0, 0)
            sp.wait_ge(z_oB, 4)
            sp.wait_ge(z_ot, 4)
            pair_in(1, 1)
            sp.wait_ge(s_br, KD)
            for q in range(2):
                pair_out(q, q)
            sp.wait_ge(s_xe, 16 * 8)
            for q in range(2):
                pair_rows(q, q)
            with sp.Fori(1, PAIRS // 2) as i:
                for q in range(2):
                    p = i * 2 + q
                    sp.wait_ge(s_xt, p - 1)
                    pair_rows(p, q)
                    sp.wait_ge(s_hd, p - 1)
                    pair_in(p, q)
                    sp.wait_ge(s_od, (p - 1) * 2)
                    pair_out(p, q)
            sp.wait_ge(s_flag, 1)
            n_extra = sp.value_load(extra[0:1, 0:1], min_val=0, max_val=EXTRA)
            for x in range(EXTRA // 2):
                p, q = PAIRS + x, x % 2
                with sp.If(n_extra > 2 * x):
                    sp.wait_ge(s_xt, p - 1)
                    pair_rows(p, q)
                    sp.wait_ge(s_od, (p - 1) * 2)
                    for u in range(2):
                        e = sp.value_load(extra[0:1, 1 + 2 * x + u:2 + 2 * x + u], min_val=0, max_val=E - 1)
                        sp.dma_start(wi2[q][:, u].rearrange("p k n -> p (k n)"),
                                     w_ein[bass.ds(e, 1), :, :].rearrange("o p n -> (o p) n")).then_inc(x_w[q], 16)
                        sp.dma_start(wo2[q][:, u].rearrange("p k n -> p (k n)"),
                                     w_eout[bass.ds(e, 1), :, :].rearrange("o p n -> (o p) n")).then_inc(x_w[q], 16)
            for k in range(0, KD, 2):
                sp.wait_ge(s_fin, k + 2)
                sp.dma_start(o_y[:, k:k + 2, :], xT[:, k:k + 2, :]).then_inc(s_y, 16)
            sp.wait_ge(s_y, 16 * KD // 2)
            sp.wait_ge(s_out, 16 * 8)

        @block.tensor
        def _(te):
            mm = te.matmul
            te.wait_ge(s_in, 64)
            te.wait_ge(s_sq, 1)
            for k in range(KD):
                m = mm(banks[7][:, 0:N], ones, sq[:, k, :], start=(k == 0), stop=(k == KD - 1))
            m.then_inc(s_ss, 1)
            te.wait_ge(s_silu, 1)

            def turn_ada(n):
                te.wait_ge(s_adr, n + 1)
                if n >= 2:
                    te.wait_ge(s_mod, n - 1)
                for c in range(4):
                    m = mm(banks[2 + n % 2][:, NC * c:NC * (c + 1)], adaR[n % 2][:, P * c:P * (c + 1)],
                           cst[:, C_SEL:C_SEL + NC], start=True, stop=True)
                m.then_inc(s_adt, 1)

            for n in range(ADA_TILES):
                te.wait_ge(s_w[n % 3], 16 * (n // 3 + 1))
                if n >= 2:
                    te.wait_ge(s_adr, n - 1)
                for k in range(0, KD, 2):
                    for j in range(2):
                        m = mm(banks[n % 2][64 * j:64 * (j + 1), :], condS[:, k + j, :], ring[n % 3][:, k + j, :],
                               start=(k == 0), stop=(k == KD - 2))
                m.then_inc(s_ada, 1)
                if n:
                    turn_ada(n - 1)
            turn_ada(ADA_TILES - 1)
            te.wait_ge(s_h, 1)
            te.wait_ge(s_mod, ADA_TILES)

            def rotate(c):
                te.wait_ge(s_pev, c + 1)
                if c >= 2:
                    te.wait_ge(s_rope, c - 1)
                mm(banks[4 + c % 2][:, 0:N], cst[:, C_PERM:C_PERM + P], qs[:, c % 3, :],
                   start=True, stop=True).then_inc(s_rot, 1)

            for c in range(4 * T_TILES):
                n = ADA_TILES + c // 4
                te.wait_ge(s_w[n % 3], 16 * (n // 3 + 1))
                if c >= 4:
                    te.wait_ge(s_pev, c - 3)
                for k in range(KD):
                    m = mm(banks[c % 4][:, 0:N], ring[n % 3][:, k, P * (c % 4):P * (c % 4 + 1)], hT[:, k, :],
                           start=(k == 0), stop=(k == KD - 1))
                m.then_inc(s_proj, 1)
                if 1 <= c <= ROT:
                    rotate(c - 1)
            te.wait_ge(s_rope, ROT)
            te.wait_ge(s_pev, 4 * T_TILES)
            for j, width in enumerate((512, 280)):
                n = ADA_TILES + T_TILES + j
                te.wait_ge(s_w[n % 3], 16 * (n // 3 + 1))
                for t, (t0, tn) in enumerate(TOK):
                    bank = banks[4 + t] if j == 0 else banks[t]
                    for k in range(KD):
                        m = mm(bank[0:tn, 0:width], hT[:, k, t0:t0 + tn], ring[n % 3][:, k, 0:width],
                               start=(k == 0), stop=(k == KD - 1))
                    m.then_inc(s_row, 1)

            for v in range(2):
                for g in range(2):
                    for t2 in range(2):
                        m = mm(banks[3][DH * t2:DH * (t2 + 1), P * (2 * v + g):P * (2 * v + g + 1)],
                               ident[:, DH * g:DH * (g + 1)], kvc[:, 3 * v, t2:NP_:2], start=True, stop=True)
            m.then_inc(s_kx, 1)
            te.wait_ge(s_w1, 32)
            for v in range(2):
                for t in range(16):
                    m = mm(banks[7][:, v:v + 1], w1_sb[v][:, t, :], pe[:, v, t:t + 1], start=(t == 0), stop=(t == 15))
            m.then_inc(s_pb, 1)
            te.wait_ge(s_kxe, 1)
            te.wait_ge(s_pbv, 1)
            for v in range(2):
                for t in range(16):
                    m = mm(banks[7][:, 32 * (v + 1):32 * (v + 1) + 2 * NCMPP].rearrange("p (g n) -> p g n", g=2),
                           w1_sb[v][:, t, :], kx[:, v, :, t:t + 8 * (NCMPP - 1) + 1:8], start=(t == 0), stop=(t == 15))
            m.then_inc(s_cp, 1)

            def cmp_hid(half):
                te.wait_ge(s_xc, 32 * 16 * (half + 1))
                if half == 0:
                    te.wait_ge(s_rowA, 6)
                for v in range(2):
                    for part in range(2):
                        if half:
                            te.wait_ge(s_cA if part == 0 else s_cB, v + 1)
                        for t in range(8):
                            c = P * v + 16 * t
                            m = mm(banks[2 * v + part][:, :].rearrange("p (j n) -> p j n", n=16),
                                   w1_sb[v][:, 8 * part + t, :], xc[half][:, :, c:c + 16],
                                   start=(t == 0), stop=(t == 7))
                        m.then_inc(s_cAB, 1)

            def cmp_out(half):
                te.wait_ge(s_cg, 2 * half + 1)
                if half:
                    te.wait_ge(s_kcm, 2)
                for g in range(2):
                    m = mm(banks[4][DH * g:DH * (g + 1), 0:4 * NCMP].rearrange("p (b n) -> p b n", n=NCMP),
                           w2k, gl[:, 0, :, g, :], start=True, stop=True)
                m.then_inc(s_c2, 1)
                te.wait_ge(s_cg, 2 * half + 2)
                for b in range(4):
                    for g in range(2):
                        m = mm(banks[5][0:NCMP, P * b + DH * g:P * b + DH * (g + 1)], gl[:, 1, b, g, :], w2v,
                               start=True, stop=True)
                m.then_inc(s_c2, 1)

            cmp_hid(0)
            te.wait_ge(s_cpg, 2)
            te.wait_ge(s_pbv, 1)
            for g in range(2):
                m = mm(banks[7][DH * g:DH * (g + 1), 0:NCMPP], w2k, glp[:, 0, g, :], start=True, stop=True)
            m.then_inc(s_cp2, 1)
            for g in range(2):
                m = mm(banks[6][0:NCMPP, DH * g:DH * (g + 1)], glp[:, 1, g, :], w2v, start=True, stop=True)
            m.then_inc(s_cp2, 1)
            cmp_out(0)
            cmp_hid(1)
            cmp_out(1)

            def p_scores(h):
                g, r, hp, o = h // 4, h % 4, h // 2, DH * (h % 2)
                for kind in range(3):
                    if h:
                        te.wait_ge(s_sev, 3 * (h - 1) + kind + 1)
                    if kind == 0:
                        q, k = qA[o:o + DH, hp, :], kA[o:o + DH, hp, :]
                    else:
                        q, k = qB[DH * g:DH * (g + 1), r, :], kvc[DH * g:DH * (g + 1), kind, :]
                    mm(banks[kind][:, 0:128], q[:, 0:128], k[:, 0:128], start=True, stop=True)
                    m = mm(banks[kind][:, 128:384], q[:, 128:256], k[:, 0:256], start=True, stop=True)
                    if kind == 2:
                        for c in range(2):
                            m = mm(banks[kind][:, 384 + NCMPP * c:384 + NCMPP * (c + 1)], q[:, 128 * c:128 * (c + 1)],
                                   kcmp[DH * g:DH * (g + 1), :], start=True, stop=True)
                    m.then_inc(s_sc, 1)

            def p_turn(h):
                sP = sPs[h % 2]
                te.wait_ge(s_exp, h + 1)
                for kind in range(3):
                    if h:
                        te.wait_ge(*((s_ptA, h) if kind == 0 else (s_ptD, 2 * (h - 1) + kind)))
                    for j in range(3):
                        m = te.transpose(banks[3 + kind][:, P * j:P * (j + 1)], sP[kind][:, P * j:P * (j + 1)], ident)
                    if kind:
                        te.wait_ge(s_cmk, h + 1)
                        c = kind - 1
                        m = te.transpose(banks[3 + kind][0:NCMPP, 384:512],
                                         sP[2][:, 384 + NCMPP * c:384 + NCMPP * (c + 1)], ident)
                    m.then_inc(s_tr, 1)

            def p_values(h):
                g = h // 4
                out = banks[6 + h % 2][:, :].rearrange("p (j t n) -> p j t n", t=2, n=DH)
                if h >= 2:
                    te.wait_ge(s_osc, h - 1)
                te.wait_ge(s_ptA, h + 1)
                te.wait_ge(s_ptD, 2 * h + 2)
                for kind in range(3):
                    if kind == 0:
                        v = [vA[:, t, DH * h:DH * (h + 1)] for t in range(2)]
                    else:
                        c = P * (kind - 1) + DH * g
                        v = [vS[:, t, c:c + DH] for t in range(2)]
                    mm(out[:, kind, 0, :], ptP[:, kind, 0:128], v[0], start=True, stop=True)
                    mm(out[:, kind, 1, :], ptP[:, kind, 128:256], v[0], start=True, stop=False)
                    mm(out[:, kind, 1, :], ptP[:, kind, 256:384], v[1], start=False, stop=True)
                for t in range(2):
                    m = mm(out[:, 3, t, :], ptC[0:NCMPP, P * t:P * (t + 1)], vcmp[0:NCMPP, DH * g:DH * (g + 1)],
                           start=True, stop=True)
                m.then_inc(s_pv, 1)

            te.wait_ge(s_cpe, 2)
            te.wait_ge(s_kcm, 4)
            p_scores(0)
            p_scores(1)
            for h in range(H):
                p_turn(h)
                if h + 2 < H:
                    p_scores(h + 2)
                p_values(h)
            for n in range(4):
                if n == 0:
                    te.wait_ge(s_osc, H)
                if n == 2:
                    te.wait_ge(s_oad, H)
                if n >= 2:
                    te.wait_ge(s_otA if n == 2 else s_otD, 1)
                for j in range(4):
                    src = oRa[:, n, P * j:P * (j + 1)] if n < 2 else oRb[:, n - 2, j, :]
                    m = te.transpose(banks[6 + n % 2][:, P * j:P * (j + 1)], src, ident)
                m.then_inc(s_ot, 1)

            def smp_scores(i):
                te.wait_ge(z_qz, i + 1)
                if i:
                    te.wait_ge(z_sev, i)
                for b in range(2):
                    te.wait_ge(s_k[b], 144 * (i + 1))
                pg = [kU[b][:, 0:PAGES * 640].rearrange("p (j n) -> p j n", n=640) for b in range(2)]
                for half in range(2):
                    for hp in range(4):
                        for b in range(2):
                            mm(banks[half][64 * b:64 * b + 64, :].rearrange("p (j n) -> p j n", n=P), qz[:, b, hp, :],
                               pg[b][:, 4 * half:4 * half + 4, P * hp:P * (hp + 1)], start=(hp == 0), stop=(hp == 3))
                    for b in range(2):
                        m = mm(banks[2 + half][64 * b:64 * b + 64, :].rearrange("p (j n) -> p j n", n=P), qzb[:, b, :],
                               pg[b][:, 4 * half:4 * half + 4, 512:640], start=True, stop=True)
                m.then_inc(z_main, 1)
                for b in range(2):
                    mm(banks[4][64 * b:64 * b + 64, :], qzb[:, b, :], kU[b][:, PAGES * 640:UNIT], start=True, stop=True)\
                        .then_inc(z_kd[b], 1)
                for b in range(2):
                    rows = slice(64 * b, 64 * b + 64)
                    for hp in range(4):
                        mm(banks[5][rows, 0:64], qz[:, b, hp, :], kA[:, hp, NP_:N], start=(hp == 0), stop=(hp == 3))
                    mm(banks[5][rows, 64:128], qzb[:, b, :], kvc[:, 1, NP_:N], start=True, stop=True)
                    mm(banks[5][rows, 128:192], qzb[:, b, :], kvc[:, 2, NP_:N], start=True, stop=True)
                    m = mm(banks[5][rows, 192:192 + NCMP], qzb[:, b, :], kcm[:, 2 * i + b, :], start=True, stop=True)
                m.then_inc(z_small, 1)

            def smp_group(i):
                te.wait_ge(z_pcn, i + 1)
                mm(banks[5][:, 256:321], cst[:, C_R:C_R + P], pcn[:, 0:65], start=True, stop=True).then_inc(z_imp, 1)

            def smp_turn(i):
                for j, n in enumerate((1, 1, 2, 3, 3, 3)):
                    te.wait_ge(z_ex, 3 * i + n)
                    bank = banks[6 + j % 2]
                    if j >= 2 or i:
                        te.wait_ge(z_tA if j % 2 == 0 else z_tD, 3 * i + j // 2)
                    for c in range(4):
                        if j < 5:
                            src = (sM, sM, sW, sS, sS)[j][:, (0, 512, 0, 0, 512)[j] + P * c:][:, 0:P]
                            m = te.transpose(bank[:, P * c:P * (c + 1)], src, ident)
                        else:
                            src = (sM[:, 1024:1088], sS[:, 1024:1088], sW[:, 512:576], pcn[:, 1:65])[c]
                            m = te.transpose(bank[0:64, P * c:P * (c + 1)], src, ident)
                    m.then_inc(z_tr, 1)

            def smp_values(i):
                te.wait_ge(z_tA, 3 * i + 3)
                te.wait_ge(z_tD, 3 * i + 3)
                for b in range(2):
                    te.wait_ge(s_v[b], 144 * (i + 1))
                both = [(b, slice(64 * b, 64 * b + 64)) for b in range(2)]
                for p in range(PAGES):
                    for b, rows in both:
                        mm(banks[7][rows, :], pt[:, p // 4, P * (p % 4) + 64 * b:P * (p % 4) + 64 * b + 64],
                           vU[b][:, 640 * p:640 * p + 512], start=(p == 0), stop=False)
                for b, rows in both:
                    mm(banks[7][rows, :], pt[0:64, 5, 64 * b:64 * b + 64], vA[0:64, 2, :], start=False, stop=True)
                for p in range(PAGES):
                    for b, rows in both:
                        mm(banks[6][rows, 0:128], pt[:, 3 + p // 4, P * (p % 4) + 64 * b:P * (p % 4) + 64 * b + 64],
                           vU[b][:, 640 * p + 512:640 * p + 640], start=(p == 0), stop=False)
                for b, rows in both:
                    mm(banks[6][rows, 0:128], pt[0:64, 5, P + 64 * b:P + 64 * b + 64], vS[0:64, 2, 0:128],
                       start=False, stop=True)
                for p in range(4):
                    for b, rows in both:
                        mm(banks[6][rows, 128:256], pt[:, 2, P * p + 64 * b:P * p + 64 * b + 64],
                           vU[b][:, PAGES * 640 + P * p:PAGES * 640 + P * (p + 1)], start=(p == 0), stop=False)
                for b, rows in both:
                    mm(banks[6][rows, 128:256], pt[0:64, 5, 2 * P + 64 * b:2 * P + 64 * b + 64], vS[0:64, 2, 128:256],
                       start=False, stop=True)
                for b, rows in both:
                    mm(banks[6][rows, 256:384], pt[0:NCMP, 5, 3 * P + 64 * b:3 * P + 64 * b + 64], vcm[0:NCMP, 2 * i + b, :],
                       start=True, stop=True).then_inc(z_vd[b], 1)

            def smp_out_turn(i):
                te.wait_ge(z_oA, i + 1)
                te.wait_ge(z_oB, i + 1)
                heads = ident.rearrange("p (b n) -> p b n", b=2)
                for hp in range(4):
                    mm(banks[7][:, 32 * hp:32 * (hp + 1)].rearrange("p (b n) -> p b n", b=2), osA[:, P * hp:P * (hp + 1)],
                       heads[:, :, 16 * hp:16 * (hp + 1)], start=True, stop=True)
                te.transpose(banks[7][:, 128:256], osB, ident).then_inc(z_ot, 1)

            smp_scores(0)
            smp_group(0)
            for i in range(4):
                if i + 1 < 4:
                    smp_scores(i + 1)
                if i:
                    smp_out_turn(i - 1)
                    te.wait_ge(z_oev, i)
                smp_turn(i)
                smp_values(i)
                if i + 1 < 4:
                    smp_group(i + 1)
            smp_out_turn(3)

            te.wait_ge(z_oev, 4)
            te.wait_ge(s_wbr, 16)
            for c in range(KD):
                for a, src in ((0, oTa), (1, oTb)):
                    if c >= 2:
                        te.wait_ge(s_mg, c - 1)
                    for k in range(4):
                        m = mm(banks[2 * (c % 2) + a][:, 0:N], wbr_sb[:, 4 * a + k, P * c:P * (c + 1)], src[:, k, :],
                               start=(k == 0), stop=(k == 3))
                m.then_inc(s_br, 1)
            te.wait_ge(s_mg, KD)
            te.wait_ge(s_wo, 16)
            for c in range(KD):
                if c >= 2:
                    te.wait_ge(s_x1, c - 1)
                for k in range(KD):
                    m = mm(banks[4 + c % 2][:, 0:N], wo_sb[:, k, P * c:P * (c + 1)], mT[:, k, :],
                           start=(k == 0), stop=(k == KD - 1))
                m.then_inc(s_op, 1)
            for k in range(KD):
                te.wait_ge(s_sq2, k + 1)
                m = mm(banks[7][:, 0:N], ones, sq2[:, k, :], start=(k == 0), stop=(k == KD - 1))
            m.then_inc(s_ss2, 1)

            te.wait_ge(s_h2, 1)
            for t in range(4):
                for k in range(KD):
                    m = mm(banks[0][0:RT, 36 * t:36 * (t + 1)], moe_in[:, k, RT * t:RT * (t + 1)], w_rt[:, k, :],
                           start=(k == 0), stop=(k == KD - 1))
            m.then_inc(s_lg, 1)
            for n in range(8):
                if n >= 4:
                    te.wait_ge(s_hr, n - 3)
                for c in range(4):
                    m = te.transpose(banks[2 + n % 4][0:RT, P * c:P * (c + 1)],
                                     moe_in[:, 4 * (n % 2) + c, RT * (n // 2):RT * (n // 2 + 1)], ident)
                m.then_inc(s_ht, 1)
            te.wait_ge(s_m, 1)
            chosen = at(rt + 900, 4, E)
            for t in range(4):
                for u in range(t + 1):
                    lhs = cst[0:RT, C_LT:C_LT + RT] if u == t else ones[0:RT, 0:RT]
                    m = mm(banks[1][0:RT, E * t:E * (t + 1)], lhs, chosen[0:RT, u, :], start=(u == 0), stop=(u == t))
            for u in range(4):
                m = mm(banks[1][0:RT, 4 * E:5 * E], ones[0:RT, 0:RT], chosen[0:RT, u, :], start=(u == 0), stop=(u == 3))
            m.then_inc(s_pos, 1)

            def turn_rows(p, q, first=False):
                te.wait_ge(s_xl[q], (p - q) * 8 + 16)
                if not first:
                    te.wait_ge(s_xtA, p)
                    te.wait_ge(s_xtD, p)
                for k in range(KD):
                    m = te.transpose(banks[k // 4][:, P * (k % 4):P * (k % 4 + 1)], xeS[q][:, P * k:P * (k + 1)], ident)
                m.then_inc(s_xt, 1)

            def hidden(p, q, loaded=None):
                te.wait_ge(*(loaded or (s_wi[q], (p - q) * 8 + 16)))
                te.wait_ge(s_xtA, p + 1)
                te.wait_ge(s_xtD, p + 1)
                for k in range(KD):
                    for e in range(2):
                        m = mm(banks[2][CAP * e:CAP * (e + 1), :], xeT[q][:, k, CAP * e:CAP * (e + 1)],
                               wi2[q][:, e, k, :], start=(k == 0), stop=(k == KD - 1))
                m.then_inc(s_hd, 1)

            def turn_act(p, q):
                te.wait_ge(s_ac, p + 1)
                for j in range(2):
                    m = te.transpose(banks[4][:, P * j:P * (j + 1)], actS[:, q, P * j:P * (j + 1)], ident)
                m.then_inc(s_at, 1)

            def pair_output(p, q, first=False, loaded=None):
                te.wait_ge(*(loaded or (s_wo2[q], (p - q) * 8 + 16)))
                te.wait_ge(s_atE, p + 1)
                for half in range(2):
                    if not first:
                        te.wait_ge(s_yA if half == 0 else s_yD, p)
                    for j in range(2):
                        for e in range(2):
                            m = mm(banks[6 + half][CAP * e:CAP * (e + 1), :], actT[:, q, j, CAP * e:CAP * (e + 1)],
                                   wo2[q][:, e, j, 512 * half:512 * (half + 1)], start=(j == 0), stop=(j == 1))
                    m.then_inc(s_od, 1)

            def combine(p, q, first=False):
                te.wait_ge(s_cs, p + 1)
                te.wait_ge(s_yA, p + 1)
                te.wait_ge(s_yD, p + 1)
                for c in range(KD):
                    if not first or c >= 2:
                        te.wait_ge(s_acc, p * KD + (c - 1))
                    m = mm(banks[3 + 2 * (c % 2)][:, 0:N], yeS[q][:, P * c:P * (c + 1)], comb[q], start=True, stop=True)
                    if c < KD - 1:
                        m.then_inc(s_cmc, 1)
                m.then_inc(s_cmb, 1)

            te.wait_ge(s_dg, 1)
            te.wait_ge(s_hr, 8)
            for k, bank in enumerate((3, 6, 5, 7)):
                mm(banks[bank][:, 0:N], ones[0:RT, :], diag[0:RT, 4 * k:4 * k + 4, :], start=True, stop=True).then_inc(s_tb, 1)
            te.wait_ge(s_flag, 1)
            te.wait_ge(s_tbA, 2)
            te.wait_ge(s_tbD, 2)
            turn_rows(0, 0, True)
            hidden(0, 0)
            turn_rows(1, 1)
            turn_act(0, 0)
            hidden(1, 1)
            turn_rows(2, 0)
            pair_output(0, 0, True)
            turn_act(1, 1)

            def step(p, q, first=False):
                hidden(p, q)
                turn_rows(p + 1, 1 - q)
                pair_output(p - 1, 1 - q)
                combine(p - 2, q, first)
                turn_act(p, q)

            step(2, 0, True)
            step(3, 1)
            with te.Fori(2, PAIRS // 2 - 1) as i:
                for q in range(2):
                    step(i * 2 + q, q)
            p = PAIRS - 2
            step(p, 0)
            hidden(p + 1, 1)
            pair_output(p, 0)
            combine(p - 1, 1)
            turn_act(p + 1, 1)
            pair_output(p + 1, 1)
            combine(p, 0)
            combine(p + 1, 1)

            n_extra = te.value_load(extra[0:1, 0:1], min_val=0, max_val=EXTRA)
            for x in range(EXTRA // 2):
                p, q = PAIRS + x, x % 2
                with te.If(n_extra > 2 * x):
                    loaded = (x_w[q], 64 * (x // 2 + 1))
                    turn_rows(p, q)
                    hidden(p, q, loaded)
                    turn_act(p, q)
                    pair_output(p, q, False, loaded)
                    combine(p, q)
            for k in range(KD):
                te.wait_ge(s_sq3, k + 1)
                m = mm(banks[0][:, 0:N], ones, sq2[:, k, :], start=(k == 0), stop=(k == KD - 1))
            m.then_inc(s_ss3, 1)

        @block.scalar
        def _(sc):
            act = sc.activation

            def rms(n):
                sc.wait_ge(s_ms, n)
                act(rstd, rstd, ACT.Sqrt).then_inc(s_rms, 1)

            sc.wait_ge(s_in, 64)
            sc.wait_ge(s_cz, 1)
            act(condS[:, :, 0:NC], cT, ACT.Silu).then_inc(s_silu, 1)
            act(sq, xT, ACT.Square).then_inc(s_sq, 1)
            rms(1)
            for c in range(4 * T_TILES):
                sc.wait_ge(s_proj, c + 1)
                if c < ROT:
                    if c >= 3:
                        sc.wait_ge(s_rope, c - 2)
                    act(qs[:, c % 3, :], banks[c % 4][:, 0:N], ACT.Copy).then_inc(s_pev, 1)
                elif c == ROT:
                    act(kvc[:, 3, :], banks[c % 4][:, 0:N], ACT.Copy).then_inc(s_pev, 1)
                else:
                    act(mT[:, c - 16, :], banks[c % 4][:, 0:N], ACT.Sigmoid).then_inc(s_pev, 1)
            for t, (t0, tn) in enumerate(TOK):
                sc.wait_ge(s_row, 4 + t)
                act(vS[0:tn, t, :], banks[t][0:tn, 0:256], ACT.Copy).then_inc(s_rowA, 1)
                act(gate[0:tn, t, :], banks[t][0:tn, 256:280], ACT.Sigmoid).then_inc(s_rowA, 1)
            sc.wait_ge(s_kx, 1)
            act(kx.rearrange("p v g n -> p (v g n)"), banks[3][:, :], ACT.Copy).then_inc(s_kxe, 1)
            sc.wait_ge(s_cp, 1)
            sc.wait_ge(s_pbv, 1)
            for v in range(2):
                act(glp[:, v].rearrange("p g n -> p (g n)"), banks[7][:, 32 * (v + 1):32 * (v + 1) + 2 * NCMPP],
                    ACT.Gelu_apprx_tanh, bias=peb[:, v:v + 1]).then_inc(s_cpg, 1)
            for half in range(2):
                for v in range(2):
                    n = 2 * half + v
                    sc.wait_ge(s_cAB, 4 * half + 2 * v + 1)
                    if n:
                        sc.wait_ge(s_cS, n)
                    src = banks[2 * v][:, :].rearrange("p (b q g n) -> p b q g n", b=4, q=8, g=2)
                    for g in range(2):
                        m = act(hA[:, :, g, :].rearrange("p b (q n) -> p b q n", n=8), src[:, :, :, g, :], ACT.Copy)
                    m.then_inc(s_cA, 1)
                    sc.wait_ge(s_cS, n + 1)
                    if half:
                        sc.wait_ge(s_c2, v + 1)
                    act(gl[:, v].rearrange("p b g n -> p (b g n)"), hS.rearrange("p a n -> p (a n)"),
                        ACT.Gelu_apprx_tanh, bias=peb[:, v:v + 1]).then_inc(s_cg, 1)

            def p_exp(h):
                sc.wait_ge(s_nm, h + 1)
                sP, st = sPs[h % 2], sts[h % 2]
                for j in range(6):
                    seg = sP[j // 2][:, 0:128] if j % 2 == 0 else sP[j // 2][:, 128:384]
                    act(seg, seg, ACT.Exp, bias=st[:, 8 + j:9 + j], scale=SCALE, accum_out=st[:, 16 + j:17 + j])
                for c in range(2):
                    seg = sP[2][:, 384 + NCMPP * c:384 + NCMPP * (c + 1)]
                    m = act(seg, seg, ACT.Exp, bias=st[:, 14 + c:15 + c], scale=SCALE)
                m.then_inc(s_exp, 1)

            def p_turned(h):
                sc.wait_ge(s_tr, 3 * h + 1)
                if h:
                    sc.wait_ge(s_pv, h)
                act(ptP[:, 0, :], banks[3][:, 0:384], ACT.Copy).then_inc(s_ptA, 1)

            p_exp(0)
            for h in range(H):
                if h + 1 < H:
                    p_exp(h + 1)
                p_turned(h)
            for n in (0, 2):
                sc.wait_ge(s_ot, n + 1)
                act((oTa if n == 0 else oTb)[:, :, 0:P], banks[6][:, :].rearrange("p (j n) -> p j n", n=P), ACT.Copy)\
                    .then_inc(s_otA, 1)

            def smp_cmp_exp(i):
                sc.wait_ge(z_cm, i + 1)
                act(sC[:, 0:NCMP], sC[:, 0:NCMP], ACT.Exp, bias=st[:, 33:34], scale=SCALE,
                    accum_out=st[:, 34:35]).then_inc(z_ce, 1)

            def smp_exp(i, j):
                s, w = ((sM, 1088), (sW, 576), (sS, 1088))[j]
                sc.wait_ge(z_nm, 3 * i + j + 1)
                act(s[:, 0:w], s[:, 0:w], ACT.Exp, bias=st[:, 40 + j:41 + j], scale=SCALE,
                    accum_out=st[:, 44 + j:45 + j]).then_inc(z_ex, 1)

            def smp_turned(i):
                for j in (0, 2, 4):
                    sc.wait_ge(z_tr, 6 * i + j + 1)
                    if i and j == 0:
                        sc.wait_ge(z_vd[1], i)
                    act(pt[:, j, :], banks[6][:, :], ACT.Copy).then_inc(z_tA, 1)

            def smp_rows_out(i):
                sc.wait_ge(z_vd[1], i + 1)
                sc.wait_ge(z_rr, i + 1)
                act(osA, banks[7][:, :], ACT.Copy, scale=scales[:, i % 2, 0:1]).then_inc(z_oA, 1)

            def smp_out(i):
                sc.wait_ge(z_ot, i + 1)
                new = NP_ + 2 * NQ * i
                for u in range(2):
                    rows = slice(DH * u, DH * (u + 1))
                    act(oTa[rows, :, new:new + 16].rearrange("p h (b q) -> p h b q", b=2),
                        banks[7][rows, 0:128].rearrange("p (h b x q) -> p h b x q", h=4, b=2, x=2)[:, :, :, u, :], ACT.Copy)
                    m = act(oTb[rows, :, new:new + 16].rearrange("p h (b q) -> p b h q", b=2),
                            banks[7][rows, 128:256].rearrange("p (b x n) -> p b x n", b=2, n=8)[:, :, 4 * u:4 * u + 4, :],
                            ACT.Copy)
                m.then_inc(z_oev, 1)

            smp_cmp_exp(0)
            smp_exp(0, 0)
            for i in range(4):
                smp_exp(i, 1)
                smp_exp(i, 2)
                if i:
                    smp_out(i - 1)
                smp_turned(i)
                if i + 1 < 4:
                    smp_cmp_exp(i + 1)
                    smp_exp(i + 1, 0)
                smp_rows_out(i)
            smp_out(3)

            for k in range(KD):
                sc.wait_ge(s_x1, k + 1)
                act(sq2[:, k], xT[:, k], ACT.Square).then_inc(s_sq2, 1)
            rms(2)
            sc.wait_ge(s_lc, 1)
            g4 = at(rt + 160, 4, 4)
            act(g4[0:RT], g4[0:RT], ACT.Exp).then_inc(s_le, 1)
            sc.wait_ge(s_l8, 1)
            e8 = at(rt + 400, 4, 8)
            act(e8[0:RT], e8[0:RT], ACT.Exp).then_inc(s_l8e, 1)
            for n in range(8):
                sc.wait_ge(s_ht, n + 1)
                act(hR[0:RT, n // 2, 512 * (n % 2):512 * (n % 2 + 1)], banks[2 + n % 4][0:RT, :], ACT.Copy).then_inc(s_hr, 1)

            def rows_out(p, q, first=False):
                sc.wait_ge(s_xt, p + 1)
                if not first:
                    sc.wait_ge(s_hd, p - 1)
                act(xeT[q][:, 0:4, :], banks[0][:, :].rearrange("p (k n) -> p k n", n=P), ACT.Copy).then_inc(s_xtA, 1)

            def pair_silu(p, q):
                sc.wait_ge(s_hd, p + 1)
                act(silS[:, q, :], banks[2][:, 0:256], ACT.Silu).then_inc(s_sil, 1)

            def pair_out(p, q, first=False):
                sc.wait_ge(s_od, p * 2 + 1)
                if not first:
                    sc.wait_ge(s_cmb, p - 1)
                act(yeS[q][:, 0:512], banks[6][:, :], ACT.Copy).then_inc(s_yA, 1)

            for k, bank in ((0, 3), (1, 6)):
                sc.wait_ge(s_tb, k + 1)
                act(table[:, k], banks[bank][:, 0:N], ACT.Copy).then_inc(s_tbA, 1)
            rows_out(0, 0, True)
            pair_silu(0, 0)
            rows_out(1, 1, True)

            def step(p, q, first=False):
                pair_silu(p, q)
                rows_out(p + 1, 1 - q)
                pair_out(p - 1, 1 - q, first)

            step(1, 1, True)
            step(2, 0, True)
            step(3, 1)
            with sc.Fori(2, PAIRS // 2 - 1) as i:
                for q in range(2):
                    step(i * 2 + q, q)
            p = PAIRS - 2
            step(p, 0)
            pair_silu(p + 1, 1)
            pair_out(p, 0)
            pair_out(p + 1, 1)

            n_extra = sc.value_load(extra[0:1, 0:1], min_val=0, max_val=EXTRA)
            for x in range(EXTRA // 2):
                p, q = PAIRS + x, x % 2
                with sc.If(n_extra > 2 * x):
                    rows_out(p, q)
                    pair_silu(p, q)
                    pair_out(p, q)
            for k in range(KD):
                sc.wait_ge(s_x2, k + 1)
                act(sq2[:, k], xT[:, k], ACT.Square).then_inc(s_sq3, 1)
            rms(3)

        @block.vector
        def _(ve):
            chain = [0]

            def link(ins):
                chain[0] += 1
                ins.then_inc(s_ch, 1)
                ve.wait_ge(s_ch, chain[0])

            def modulated(dst, src, s, shift):
                for k in range(KD):
                    ve.tensor_scalar(dst[:, k, 0:NP_], src[:, k, 0:NP_], s[:, k, 0:1], shift[:, k, 0:1], ALU.mult, ALU.add)
                a = src[:, :, NP_:N].rearrange("p k (b q) -> p k b q", q=NQ)
                o = dst[:, :, NP_:N].rearrange("p k (b q) -> p k b q", q=NQ)
                wide = [P, KD, NB, NQ]
                link(ve.tensor_tensor(o, a, s[:, :, 1:NC].unsqueeze(3).to_broadcast(wide), ALU.mult))
                return ve.tensor_tensor(o, o, shift[:, :, 1:NC].unsqueeze(3).to_broadcast(wide), ALU.add)

            def root(total, n):
                ve.tensor_scalar(rstd, total, 1.0 / D, EPS, ALU.mult, ALU.add).then_inc(s_ms, 1)
                ve.wait_ge(s_rms, n)
                link(ve.reciprocal(rstd, rstd))

            def normed(dst):
                return ve.tensor_tensor(dst, xT, rstd.unsqueeze(1).to_broadcast([P, KD, N]), ALU.mult)

            ve.memset(condS, 0.0).then_inc(s_cz, 1)
            ve.wait_ge(s_in, 64)
            ve.wait_ge(s_ss, 1)
            root(banks[7][:, 0:N], 1)
            link(normed(sq))

            def ada_rows(n):
                ve.wait_ge(s_ada, n + 1)
                if n >= 2:
                    ve.wait_ge(s_adt, n - 1)
                ve.tensor_copy(adaR[n % 2], banks[n % 2][:, :]).then_inc(s_adr, 1)

            ada_rows(0)
            for n in range(ADA_TILES):
                if n + 1 < ADA_TILES:
                    ada_rows(n + 1)
                ve.wait_ge(s_adt, n + 1)
                ve.tensor_tensor(mod[:, 4 * n:4 * n + 4, :], banks[2 + n % 2][:, 0:4 * NC].rearrange("p (c n) -> p c n", n=NC),
                                 vecs[:, 4 * n:4 * n + 4].unsqueeze(2).to_broadcast([P, 4, NC]), ALU.add).then_inc(s_mod, 1)
            ve.wait_ge(s_mod, ADA_TILES)
            for j in range(2):
                link(ve.scalar_tensor_tensor(scl[:, j], mod[:, 8 + 24 * j:16 + 24 * j, :], 1.0,
                                             gains[:, j].unsqueeze(2).to_broadcast([P, KD, NC]), ALU.add, ALU.mult))
            modulated(hT, sq, scl[:, 0], mod[:, 0:8, :]).then_inc(s_h, 1)
            dst = [qA[:, c] for c in range(4)] + [kA[:, c] for c in range(4)] + [qB[:, c] for c in range(4)] + [kvc[:, c] for c in range(3)]
            for c in range(ROT):
                ve.wait_ge(s_pev, c + 1)
                ve.wait_ge(s_rot, c + 1)
                ve.tensor_tensor(turn[:, c % 2, 0, :], qs[:, c % 3, :], cst[:, C_COS:C_COS + N], ALU.mult)
                link(ve.tensor_tensor(turn[:, c % 2, 1, :], banks[4 + c % 2][:, 0:N], cst[:, C_SIN:C_SIN + N], ALU.mult))
                ve.tensor_tensor(dst[c], turn[:, c % 2, 0, :], turn[:, c % 2, 1, :], ALU.add).then_inc(s_rope, 1)
            for t, (t0, tn) in enumerate(TOK):
                ve.wait_ge(s_row, t + 1)
                ve.tensor_copy(vA[0:tn, t, :], banks[4 + t][0:tn, :]).then_inc(s_rowV, 1)
            ve.wait_ge(s_pb, 1)
            ve.tensor_copy(peb, banks[7][:, 0:2]).then_inc(s_pbv, 1)
            ve.wait_ge(s_cp2, 1)
            ve.tensor_copy(kcmp, banks[7][:, 0:NCMPP]).then_inc(s_cpe, 1)
            ve.wait_ge(s_cp2, 2)
            ve.tensor_copy(vcmp[0:NCMPP, :], banks[6][0:NCMPP, 0:P]).then_inc(s_cpe, 1)
            for half in range(2):
                for v in range(2):
                    n = 2 * half + v
                    ve.wait_ge(s_cAB, 4 * half + 2 * v + 2)
                    if n:
                        ve.wait_ge(s_cS, n)
                    src = banks[2 * v + 1][:, :].rearrange("p (b q g n) -> p b q g n", b=4, q=8, g=2)
                    for g in range(2):
                        m = ve.tensor_copy(hB[:, :, g, :].rearrange("p b (q n) -> p b q n", n=8), src[:, :, :, g, :])
                    m.then_inc(s_cB, 1)
                    ve.wait_ge(s_cB, n + 1)
                    ve.wait_ge(s_cA, n + 1)
                    if n:
                        ve.wait_ge(s_cg, n)
                    ve.tensor_tensor(hS, hA.rearrange("p b g n -> p (b g) n")[:, :, 0:63],
                                     hB.rearrange("p b g n -> p (b g) n")[:, :, 1:64], ALU.add).then_inc(s_cS, 1)
                ve.wait_ge(s_c2, 2 * half + 1)
                ve.tensor_copy(kcm[:, 4 * half:4 * half + 4, :],
                               banks[4][:, 0:4 * NCMP].rearrange("p (b n) -> p b n", n=NCMP)).then_inc(s_kcm, 1)
                ve.wait_ge(s_c2, 2 * half + 2)
                ve.wait_ge(s_zf, 16 * (PAIRS + EXTRA // 2 + 1))
                ve.tensor_copy(vcm[0:NCMP, 4 * half:4 * half + 4, :],
                               banks[5][0:NCMP, :].rearrange("p (b n) -> p b n", n=P)).then_inc(s_kcm, 1)

            ve.wait_ge(s_rowA, 6)

            def p_max(h):
                sP, st = sPs[h % 2], sts[h % 2]
                for kind in range(3):
                    ve.wait_ge(s_sc, 3 * h + kind + 1)
                    if h >= 2:
                        ve.wait_ge(s_tr, 3 * h - 3)
                    if kind == 2:
                        ve.tensor_tensor(sP[2][:, 384:414], banks[2][:, 384:414], cst[:, C_CADD:C_CADD + 30], ALU.add)
                    ve.tensor_tensor(sP[kind][:, 0:384], banks[kind][:, 0:384], cst[:, C_TRI:C_TRI + 384], ALU.add)\
                        .then_inc(s_sev, 1)
                    ve.wait_ge(s_sev, 3 * h + kind + 1)
                    ve.tensor_reduce(st[:, 2 * kind:2 * kind + 1], sP[kind][:, 0:128], AX, ALU.max)
                    m = ve.tensor_reduce(st[:, 2 * kind + 1:2 * kind + 2], sP[kind][:, 128:384], AX, ALU.max)
                link(ve.tensor_reduce(st[:, 6:8], sP[2][:, 384:414].rearrange("p (c n) -> p c n", n=NCMPP), AX, ALU.max))
                ve.tensor_scalar(st[:, 8:16], st[:, 0:8], -SCALE, None, ALU.mult).then_inc(s_nm, 1)

            def p_sums(h):
                sP, st = sPs[h % 2], sts[h % 2]
                ve.wait_ge(s_exp, h + 1)
                ve.tensor_tensor(sP[2][:, 384:414], sP[2][:, 384:414], cst[:, C_C01:C_C01 + 30], ALU.mult).then_inc(s_cmk, 1)
                ve.wait_ge(s_cmk, h + 1)
                link(ve.tensor_reduce(st[:, 22:24], sP[2][:, 384:414].rearrange("p (c n) -> p c n", n=NCMPP), AX, ALU.add))
                link(ve.tensor_scalar(st[:, 16:24], st[:, 16:24], TINY, None, ALU.max))
                link(ve.reciprocal(st[:, 24:32], st[:, 16:24]))
                w = st[:, 26:32].rearrange("p (j t) -> p j t", t=2)
                link(ve.tensor_tensor(w, w, gate[:, 0:2, 3 * h:3 * h + 3].rearrange("p t j -> p j t"), ALU.mult))

            def p_turned(h):
                for kind in (1, 2):
                    ve.wait_ge(s_tr, 3 * h + kind + 1)
                    if h:
                        ve.wait_ge(s_pv, h)
                    ve.tensor_copy(ptC[0:NCMPP, P * (kind - 1):P * kind], banks[3 + kind][0:NCMPP, 384:512])
                    ve.tensor_copy(ptP[:, kind, :], banks[3 + kind][:, 0:384]).then_inc(s_ptD, 1)

            def p_scale(h):
                st = sts[h % 2]
                ve.wait_ge(s_pv, h + 1)
                if h >= 2:
                    ve.wait_ge(s_oad, h - 1)
                out = banks[6 + h % 2][:, :].rearrange("p (j n) -> p j n", n=DH)
                ve.tensor_tensor(parts[h % 2].rearrange("p j t n -> p (j t) n"), out[:, 2:8, :],
                                 st[:, 26:32].unsqueeze(2).to_broadcast([P, 6, DH]), ALU.mult)
                ve.tensor_tensor(oRa[:, :, DH * h:DH * (h + 1)], out[:, 0:2, :],
                                 st[:, 24:26].unsqueeze(2).to_broadcast([P, 2, DH]), ALU.mult).then_inc(s_osc, 1)

            p_max(0)
            for h in range(H):
                if h + 1 < H:
                    p_max(h + 1)
                p_sums(h)
                if h:
                    p_scale(h - 1)
                p_turned(h)
            p_scale(H - 1)
            for n in (1, 3):
                ve.wait_ge(s_ot, n + 1)
                ve.tensor_copy((oTa if n == 1 else oTb)[:, :, P:2 * P], banks[7][:, :].rearrange("p (j n) -> p j n", n=P))\
                    .then_inc(s_otD, 1)

            ve.wait_ge(s_ot, 4)
            link(ve.memset(qz, 0.0))
            link(ve.memset(qzb, 0.0))
            link(ve.memset(pcn, 0.0))
            ve.wait_ge(s_gs, 16 * 16)

            def smp_blocks(i):
                if i:
                    ve.wait_ge(z_small, i)
                new = NP_ + 2 * NQ * i
                for hp in range(4):
                    for u in range(2):
                        rows = slice(DH * u, DH * (u + 1))
                        ve.tensor_copy(qz[rows, :, hp, 16 * hp + 8 * u:16 * hp + 8 * u + 8],
                                       qA[rows, hp, new:new + 16].rearrange("p (b q) -> p b q", b=2))
                for g in range(2):
                    for b in range(2):
                        rows = slice(DH * g, DH * (g + 1))
                        m = ve.tensor_copy(qzb[rows, b, 32 * g:32 * g + 32].rearrange("p (r q) -> p r q", q=NQ),
                                           qB[rows, :, new + 8 * b:new + 8 * b + 8])
                m.then_inc(z_qz, 1)

            def dropped(src, n):
                d, e, pen = st[:, 50:51], at(B + 6740, 16)[:, 0:n], at(B + 6756, 16)[:, 0:n]
                link(ve.tensor_reduce(d, src, AX, ALU.min))
                link(ve.scalar_tensor_tensor(e, src, d, idx[:, 0:n], ALU.is_equal, ALU.mult))
                link(ve.tensor_reduce(st[:, 51:52], e, AX, ALU.max))
                link(ve.tensor_scalar(pen, idx[:, 0:n], st[:, 51:52], NEG, ALU.is_equal, ALU.mult))
                return pen

            def smp_max(i):
                ve.wait_ge(z_main, i + 1)
                new = cst[:, C_NEW + NS * i:C_NEW + NS * (i + 1)]
                g4 = st[:, 52:56]
                for half in range(2):
                    m = ve.tensor_reduce(g4[:, 2 * half:2 * half + 2], banks[half][:, :].rearrange("p (j n) -> p j n", n=256),
                                         AX, ALU.add)
                link(m)
                pen = dropped(g4, 4)
                if i:
                    ve.wait_ge(z_tr, 6 * i)
                for half in range(2):
                    m = ve.tensor_tensor(sM[:, 512 * half:512 * (half + 1)].rearrange("p (j n) -> p j n", n=256),
                                         banks[half][:, :].rearrange("p (j n) -> p j n", n=256),
                                         pen[:, 2 * half:2 * half + 2].unsqueeze(2).to_broadcast([P, 2, 256]), ALU.add)
                link(m)
                ve.wait_ge(z_small, i + 1)
                link(ve.tensor_copy(sC[:, 0:NCMP], banks[5][:, 192:192 + NCMP]))
                link(ve.tensor_reduce(st[:, 32:33], sC[:, 0:NCMP], AX, ALU.max))
                ve.tensor_scalar(st[:, 33:34], st[:, 32:33], -SCALE, None, ALU.mult).then_inc(z_cm, 1)
                link(ve.tensor_tensor(sM[:, 1024:1088], banks[5][:, 0:64], new, ALU.add))
                link(ve.tensor_reduce(st[:, 36:37], sM, AX, ALU.max))
                ve.tensor_scalar(st[:, 40:41], st[:, 36:37], -SCALE, None, ALU.mult).then_inc(z_nm, 1)
                ve.tensor_tensor(sS[:, 1024:1088], banks[5][:, 64:128], new, ALU.add)
                ve.tensor_tensor(sW[:, 512:576], banks[5][:, 128:192], new, ALU.add)
                ve.wait_ge(z_ce, i + 1)
                link(ve.tensor_scalar(st[:, 34:35], st[:, 34:35], TINY, None, ALU.max))
                link(ve.reciprocal(st[:, 35:36], st[:, 34:35]))
                ve.tensor_scalar(pcn[:, 1:1 + NCMP], sC[:, 0:NCMP], st[:, 35:36], None, ALU.mult).then_inc(z_pcn, 1)
                ve.tensor_tensor(sW[:, 0:8], banks[4][:, 0:8], cst[:, C_WIN:C_WIN + 8], ALU.add)
                ve.tensor_copy(sW[:, 8:512], banks[4][:, 8:512]).then_inc(z_wev, 1)
                ve.wait_ge(z_wev, i + 1)
                link(ve.tensor_reduce(st[:, 38:39], sW, AX, ALU.max))
                ve.tensor_scalar(st[:, 41:42], st[:, 38:39], -SCALE, None, ALU.mult).then_inc(z_nm, 1)
                ve.wait_ge(z_imp, i + 1)
                imp = at(B + 6772, 16)
                grp = at(B + 6788, 66)
                link(ve.tensor_copy(grp[:, 0:65], banks[5][:, 256:321]))
                link(ve.tensor_reduce(imp, grp[:, 0:64].rearrange("p (j n) -> p j n", n=4), AX, ALU.add))
                link(ve.tensor_tensor(imp, imp, grp[:, 4:65:4], ALU.add))
                pen = dropped(imp, 16)
                for half in range(2):
                    m = ve.tensor_tensor(sS[:, 512 * half:512 * (half + 1)].rearrange("p (j n) -> p j n", n=64),
                                         banks[2 + half][:, :].rearrange("p (j n) -> p j n", n=64),
                                         pen[:, 8 * half:8 * half + 8].unsqueeze(2).to_broadcast([P, 8, 64]), ALU.add)
                m.then_inc(z_sev, 1)
                ve.wait_ge(z_sev, i + 1)
                link(ve.tensor_reduce(st[:, 37:38], sS, AX, ALU.max))
                ve.tensor_scalar(st[:, 42:43], st[:, 37:38], -SCALE, None, ALU.mult).then_inc(z_nm, 1)

            def smp_scales(i):
                ve.wait_ge(z_ex, 3 * i + 3)
                if i >= 2:
                    ve.wait_ge(z_oA, i - 1)
                link(ve.tensor_scalar(st[:, 44:47], st[:, 44:47], TINY, None, ALU.max))
                link(ve.reciprocal(scales[:, i % 2, 0:3], st[:, 44:47]))
                ve.tensor_tensor(scales[:, i % 2, 1:2], scales[:, i % 2, 1:2], gateS[:, i, 1:2], ALU.mult)
                ve.tensor_tensor(scales[:, i % 2, 2:3], scales[:, i % 2, 2:3], gateS[:, i, 0:1], ALU.mult)
                ve.tensor_copy(scales[:, i % 2, 3:4], gateS[:, i, 2:3]).then_inc(z_rr, 1)

            def smp_turned(i):
                for j in (1, 3, 5):
                    ve.wait_ge(z_tr, 6 * i + j + 1)
                    if i and j == 1:
                        ve.wait_ge(z_vd[1], i)
                    rows = slice(0, P if j < 5 else 64)
                    ve.tensor_copy(pt[rows, j, :], banks[7][rows, :]).then_inc(z_tD, 1)

            def smp_rows_out(i):
                ve.wait_ge(z_vd[1], i + 1)
                if i:
                    ve.wait_ge(z_ot, i)
                else:
                    ve.wait_ge(z_rr, 1)
                sc3 = scales[:, i % 2]
                link(ve.tensor_scalar(osB, banks[6][:, 0:128], sc3[:, 2:3], None, ALU.mult))
                link(ve.scalar_tensor_tensor(osB, banks[6][:, 128:256], sc3[:, 1:2], osB, ALU.mult, ALU.add))
                ve.scalar_tensor_tensor(osB, banks[6][:, 256:384], sc3[:, 3:4], osB, ALU.mult, ALU.add).then_inc(z_oB, 1)

            smp_blocks(0)
            for i in range(4):
                smp_max(i)
                if i:
                    smp_rows_out(i - 1)
                if i + 1 < 4:
                    smp_blocks(i + 1)
                smp_scales(i)
                smp_turned(i)
            smp_rows_out(3)

            for c in range(KD):
                ve.wait_ge(s_br, c + 1)
                ve.tensor_tensor(mT[:, c, :], mT[:, c, :], banks[2 * (c % 2)][:, 0:N], ALU.mult)
                link(ve.tensor_tensor(mT[:, 8 + c, :], mT[:, 8 + c, :], banks[2 * (c % 2) + 1][:, 0:N], ALU.mult))
                ve.tensor_tensor(mT[:, c, :], mT[:, c, :], mT[:, 8 + c, :], ALU.add).then_inc(s_mg, 1)
            tmp = sample_part

            def residual(c, bank, g0, s):
                if c:
                    ve.wait_ge(s, c)
                ve.scalar_tensor_tensor(xT[:, c, 0:NP_], bank[:, 0:NP_], mod[:, g0 + c, 0:1], xT[:, c, 0:NP_], ALU.mult, ALU.add)
                link(ve.tensor_tensor(tmp.rearrange("p (b q) -> p b q", q=NQ), bank[:, NP_:N].rearrange("p (b q) -> p b q", q=NQ),
                                      mod[:, g0 + c, 1:NC].unsqueeze(2).to_broadcast([P, NB, NQ]), ALU.mult))
                ve.tensor_tensor(xT[:, c, NP_:N], xT[:, c, NP_:N], tmp, ALU.add).then_inc(s, 1)

            for c in range(KD):
                ve.wait_ge(s_op, c + 1)
                residual(c, banks[4 + c % 2], 16, s_x1)
            ve.wait_ge(s_ss2, 1)
            root(banks[7][:, 0:N], 2)
            link(normed(moe_in))
            modulated(moe_in, moe_in, scl[:, 1], mod[:, 24:32, :]).then_inc(s_h2, 1)

            ve.wait_ge(s_lg, 1)
            R = slice(0, RT)
            lg = at(rt, 4, 36)
            g4 = at(rt + 160, 4, 4)
            e8 = at(rt + 400, 4, 8)
            oh = at(rt + 180, 4, 4)
            m1 = at(rt + 200, 4)
            gw = at(rt + 204, 4)
            v2 = at(rt + 208, 4)
            big = at(rt + 240, 4, 8, 4)
            oh1, oh2, e2 = at(rt + 440, 4, 8), at(rt + 480, 4, 8), at(rt + 520, 4, 8)

            def wide(ap, n):
                return ap[R].unsqueeze(2).to_broadcast([RT, 4, n])

            def first_best(dst, src, best, n):
                down = idx[R, 0:n].unsqueeze(1).to_broadcast([RT, 4, n])
                link(ve.tensor_tensor(dst[R], src[R], wide(best, n), ALU.is_equal))
                link(ve.tensor_tensor(e2[R, :, 0:n], dst[R], down, ALU.mult))
                link(ve.scalar_tensor_tensor(dst[R], dst[R], 64.0, e2[R, :, 0:n], ALU.mult, ALU.subtract))
                link(ve.tensor_reduce(m1[R], dst[R], AX, ALU.max))
                link(ve.tensor_tensor(dst[R], dst[R], wide(m1, n), ALU.is_equal))

            link(ve.tensor_copy(lg[R], banks[0][R, 0:144].rearrange("p (t n) -> p t n", n=36)))
            link(ve.tensor_reduce(m1[R], lg[R, :, 0:4], AX, ALU.max))
            ve.tensor_tensor(g4[R], lg[R, :, 0:4], wide(m1, 4), ALU.subtract).then_inc(s_lc, 1)
            ve.wait_ge(s_le, 1)
            link(ve.tensor_reduce(gw[R], g4[R], AX, ALU.add))
            link(ve.reciprocal(gw[R], gw[R]))
            link(ve.tensor_reduce(v2[R], g4[R], AX, ALU.max))
            first_best(oh, g4, v2, 4)
            for t in range(4):
                m = ve.tensor_tensor(big[R, t], lg[R, t, 4:36].rearrange("p (g e) -> p e g", e=8),
                                     oh[R, t].unsqueeze(1).to_broadcast([RT, 8, 4]), ALU.mult)
            link(m)
            link(ve.tensor_reduce(e8[R], big[R], AX, ALU.add))
            link(ve.tensor_reduce(m1[R], e8[R], AX, ALU.max))
            ve.tensor_tensor(e8[R], e8[R], wide(m1, 8), ALU.subtract).then_inc(s_l8, 1)
            ve.wait_ge(s_l8e, 1)
            link(ve.tensor_reduce(v2[R], e8[R], AX, ALU.max))
            first_best(oh1, e8, v2, 8)
            rest = at(rt + 560, 4, 8)
            link(ve.scalar_tensor_tensor(rest[R], oh1[R], -4.0, e8[R], ALU.mult, ALU.add))
            link(ve.tensor_reduce(v2[R], rest[R], AX, ALU.max))
            first_best(oh2, rest, v2, 8)
            tot, wt1, wt2 = at(rt + 212, 4), at(rt + 216, 4), at(rt + 220, 4)
            link(ve.tensor_scalar(tot[R], v2[R], 1.0, None, ALU.add))
            link(ve.reciprocal(tot[R], tot[R]))
            link(ve.tensor_tensor(wt1[R], tot[R], gw[R], ALU.mult))
            link(ve.tensor_tensor(wt2[R], wt1[R], v2[R], ALU.mult))
            first, second, chosen = at(rt + 600, 4, E), at(rt + 730, 4, E), at(rt + 900, 4, E)
            for ch, o in ((first, oh1), (second, oh2)):
                for t in range(4):
                    m = ve.tensor_tensor(ch[R, t].rearrange("p (g e) -> p g e", e=8), o[R, t].unsqueeze(1).to_broadcast([RT, 4, 8]),
                                         oh[R, t].unsqueeze(2).to_broadcast([RT, 4, 8]), ALU.mult)
            link(m)
            ve.tensor_tensor(chosen[R], first[R], second[R], ALU.add).then_inc(s_m, 1)
            ve.wait_ge(s_pos, 1)
            pos, over, tmp4 = at(rt + 1030, 4, E), at(rt + 1160, 4, E), big[:, :, :, :].rearrange("p a b c -> p a (b c)")
            cnt, more, far = at(rt + 1300, E), at(rt + 1332, E), at(rt + 1364, E)
            ends = [at(rt + 1400 + 48 * k, 48) for k in range(2)]
            link(ve.tensor_copy(pos[R], banks[1][R, 0:4 * E].rearrange("p (t e) -> p t e", e=E)))
            link(ve.tensor_copy(cnt[R], banks[1][R, 4 * E:5 * E]))
            link(ve.tensor_scalar(more[R], cnt[R], CAP + 0.5, None, ALU.is_ge))
            for n in range(2, N // CAP):
                link(ve.scalar_tensor_tensor(more[R], cnt[R], n * CAP + 0.5, more[R], ALU.is_ge, ALU.add))
            for k in range(2):
                link(ve.memset(ends[k][R, 0:16], 0.0))
            link(ve.tensor_copy(ends[0][R, 16:48], more[R]))
            for n, step in enumerate((1, 2, 4, 8, 16)):
                a, b = ends[n % 2], ends[1 - n % 2]
                link(ve.tensor_tensor(b[R, 16:48], a[R, 16:48], a[R, 16 - step:48 - step], ALU.add))
            end = ends[1][R, 16:48]
            link(ve.tensor_tensor(far[R], end, more[R], ALU.subtract))
            link(ve.tensor_scalar(far[R], far[R], float(CAP), float(CAP * (E - 1)), ALU.mult, ALU.add))
            link(ve.tensor_tensor(far[R], far[R], cst[R, C_E:C_E + E], ALU.subtract))
            link(ve.tensor_scalar(over[R], pos[R], CAP - 0.5, None, ALU.is_ge))
            link(ve.tensor_tensor(over[R], over[R], far[R].unsqueeze(1).to_broadcast([RT, 4, E]), ALU.mult))
            link(ve.tensor_tensor(pos[R], pos[R], cst[R, C_E:C_E + E].unsqueeze(1).to_broadcast([RT, 4, E]), ALU.add))
            link(ve.tensor_tensor(pos[R], pos[R], over[R], ALU.add))
            rowf = at(rt + 224, 2, 4)
            for r, ch in enumerate((first, second)):
                link(ve.tensor_tensor(tmp4[R], ch[R], pos[R], ALU.mult))
                link(ve.tensor_reduce(rowf[R, r], tmp4[R], AX, ALU.add))
            ve.tensor_copy(index[:, :], rowf[R].rearrange("p r t -> p (r t)")).then_inc(s_idx, 1)
            ve.tensor_tensor(diag[R], ident[R, 0:RT].unsqueeze(1).to_broadcast([RT, 16, RT]),
                             at(rt + 216, 16)[R].unsqueeze(2).to_broadcast([RT, 16, RT]), ALU.mult).then_inc(s_dg, 1)
            which, tab = big[0:1].rearrange("p a b c -> p (a b c)"), at(rt + 1500, 16)
            for k in range(EXTRA):
                link(ve.tensor_scalar(which[:, 0:E], ends[1][0:1, 16:48], k + 0.5, None, ALU.is_le))
                link(ve.tensor_reduce(tab[0:1, 1 + k:2 + k], which[:, 0:E], AX, ALU.add))
            link(ve.tensor_scalar(tab[0:1, 1:1 + EXTRA], tab[0:1, 1:1 + EXTRA], E - 1.0, None, ALU.min))
            link(ve.tensor_copy(tab[0:1, 0:1], ends[1][0:1, 47:48]))
            ve.tensor_copy(extra[:, :], tab[0:1, 0:1 + EXTRA]).then_inc(s_flag, 1)

            def rows_out(p, q, first=False):
                ve.wait_ge(s_xt, p + 1)
                if not first:
                    ve.wait_ge(s_hd, p - 1)
                ve.tensor_copy(xeT[q][:, 4:8, :], banks[1][:, :].rearrange("p (k n) -> p k n", n=P)).then_inc(s_xtD, 1)

            def pair_act(p, q):
                ve.wait_ge(s_sil, p + 1)
                ve.tensor_tensor(actS[:, q, :], silS[:, q, :], banks[2][:, 256:512], ALU.mult).then_inc(s_ac, 1)

            def act_out(p, q):
                ve.wait_ge(s_at, p + 1)
                ve.tensor_copy(actT[:, q].rearrange("p j n -> p (j n)"), banks[4][:, 0:256]).then_inc(s_atE, 1)

            def pair_out(p, q, first=False):
                ve.wait_ge(s_od, p * 2 + 2)
                if not first:
                    ve.wait_ge(s_cmb, p - 1)
                ve.tensor_copy(yeS[q][:, 512:1024], banks[7][:, :]).then_inc(s_yD, 1)

            def add(p, first=False):
                for c in range(KD):
                    bank = banks[3 + 2 * (c % 2)][:, 0:N]
                    if c < KD - 1:
                        ve.wait_ge(s_cmc, p * (KD - 1) + (c + 1))
                    else:
                        ve.wait_ge(s_cmb, p + 1)
                    if first:
                        ve.tensor_copy(moe[:, c, :], bank).then_inc(s_acc, 1)
                    else:
                        ve.wait_ge(s_acc, p * KD + (c + 1 - KD))
                        ve.tensor_tensor(moe[:, c, :], moe[:, c, :], bank, ALU.add).then_inc(s_acc, 1)

            for k, bank in ((2, 5), (3, 7)):
                ve.wait_ge(s_tb, k + 1)
                ve.tensor_copy(table[:, k], banks[bank][:, 0:N]).then_inc(s_tbD, 1)
            rows_out(0, 0, True)
            rows_out(1, 1, True)
            pair_act(0, 0)
            act_out(0, 0)
            rows_out(2, 0)
            pair_act(1, 1)
            pair_out(0, 0, True)
            act_out(1, 1)

            def step(p, q, out_first=False, add_first=False):
                rows_out(p + 1, 1 - q)
                pair_act(p, q)
                pair_out(p - 1, 1 - q, out_first)
                add(p - 2, add_first)
                act_out(p, q)

            step(2, 0, True, True)
            step(3, 1)
            with ve.Fori(2, PAIRS // 2 - 1) as i:
                for q in range(2):
                    step(i * 2 + q, q)
            p = PAIRS - 2
            step(p, 0)
            pair_act(p + 1, 1)
            pair_out(p, 0)
            add(p - 1)
            act_out(p + 1, 1)
            pair_out(p + 1, 1)
            add(p)
            add(p + 1)

            ve.wait_ge(s_flag, 1)
            n_extra = ve.value_load(extra[0:1, 0:1], min_val=0, max_val=EXTRA)
            for x in range(EXTRA // 2):
                p, q = PAIRS + x, x % 2
                with ve.If(n_extra > 2 * x):
                    rows_out(p, q)
                    pair_act(p, q)
                    act_out(p, q)
                    pair_out(p, q)
                    add(p)
                    ve.wait_ge(s_acc, KD * (p + 1))
            ve.wait_ge(s_acc, KD * PAIRS)
            wide4 = [P, KD, NB, NQ]
            smp = moe[:, :, NP_:N].rearrange("p k (b q) -> p k b q", q=NQ)
            link(ve.tensor_tensor(smp, smp, mod[:, 40:48, 1:NC].unsqueeze(3).to_broadcast(wide4), ALU.mult))
            ve.tensor_tensor(xT[:, :, NP_:N], xT[:, :, NP_:N], moe[:, :, NP_:N], ALU.add)
            for k in range(KD):
                ve.scalar_tensor_tensor(xT[:, k, 0:NP_], moe[:, k, 0:NP_], mod[:, 40 + k, 0:1], xT[:, k, 0:NP_],
                                        ALU.mult, ALU.add).then_inc(s_x2, 1)
            ve.wait_ge(s_ss3, 1)
            root(banks[0][:, 0:N], 3)
            for k in range(KD):
                ve.scalar_tensor_tensor(xT[:, k, :], xT[:, k, :], gains[:, 2, k:k + 1], rstd, ALU.mult, ALU.mult)\
                    .then_inc(s_fin, 1)

        @block.gpsimd
        def _(po):
            zeros = vcm.rearrange("p b n -> p (b n)")
            po.memset(zeros, 0.0).then_inc(s_z, 1)
            po.wait_ge(s_ada, ADA_TILES - 1)
            po.dma_start(o_win[0], win_state[0]).then_inc(s_out, 16)
            po.dma_start(o_win[1], win_state[1]).then_inc(s_out, 16)
            po.wait_ge(s_z, 1)
            po.dma_start(o_zero, zeros[:, 0:256]).then_inc(s_zf, 16)
            for n in range(PAIRS + EXTRA // 2):
                po.dma_start(x_rows[P * n:P * (n + 1), :], zeros).then_inc(s_zf, 16)
            po.wait_ge(s_rope, ROT)
            po.dma_start(o_kt, kA).then_inc(s_out, 16)
            po.wait_ge(s_pev, ROT + 1)
            po.dma_start(o_small, kvc).then_inc(s_out, 16)
            po.wait_ge(s_rowV, 3)
            po.dma_start(o_va[:, 0:2, :], vA[:, 0:2, :]).then_inc(s_out, 16)
            po.dma_start(o_va[0:64, 2, :], vA[0:64, 2, :]).then_inc(s_out, 16)
            po.wait_ge(s_rowA, 6)
            po.dma_start(o_vs[:, 0:2, :], vS[:, 0:2, :]).then_inc(s_out, 16)
            po.dma_start(o_vs[0:64, 2, :], vS[0:64, 2, :]).then_inc(s_out, 16)
            po.dma_start(scratch, gate[0:NS, 2, :]).then_inc(s_gd, 16)
            po.wait_ge(s_gd, 16)
            by_head = scratch.rearrange("(i b q) (h j) -> b h q i j", b=2, q=NQ, j=3)
            for b in range(2):
                for h in range(H):
                    row = 64 * b + 8 * h
                    po.dma_start(gateS[row:row + 8, :, :], by_head[b, h]).then_inc(s_gs, 16)

            for h in range(H):
                po.wait_ge(s_osc, h + 1)
                dst = oRb[:, :, h % 4, DH * (h // 4):DH * (h // 4 + 1)]
                part = parts[h % 2]
                po.tensor_tensor(part[:, 0], part[:, 0], part[:, 1], ALU.add).then_inc(s_chp, 1)
                po.wait_ge(s_chp, h + 1)
                po.tensor_tensor(dst, part[:, 0], part[:, 2], ALU.add).then_inc(s_oad, 1)
            po.wait_ge(s_zf, 16 * (PAIRS + EXTRA // 2 + 1))
            po.wait_ge(s_idx, 1)
            po.wait_ge(s_hr, 8)
            for r in range(2):
                for t in range(4):
                    po.indirect_dma_start(out=x_rows, out_offset=bass.IndirectOffsetOnAxis(index[:, 4 * r + t:4 * r + t + 1], 0),
                                          in_=hR[0:RT, t, :], in_offset=None, bounds_check=(E + EXTRA) * CAP - 1,
                                          oob_is_err=False).then_inc(s_xe, 16)

            def combination(p, q, first=False):
                if not first:
                    po.wait_ge(s_cs, p)
                    po.wait_ge(s_cmb, p - 1)
                po.wait_ge(s_slot, p + 1)
                po.tensor_scalar(comb1, table[:, 2], slot, None, ALU.is_equal).then_inc(s_cm, 1)
                po.tensor_scalar(comb[q], table[:, 3], slot, None, ALU.is_equal).then_inc(s_cm, 1)
                po.wait_ge(s_cm, p * 2 + 2)
                po.tensor_scalar(slot, slot, float(P), None, ALU.add).then_inc(s_slot, 1)
                po.tensor_tensor(comb1, comb1, table[:, 0], ALU.mult).then_inc(s_cw, 1)
                po.tensor_tensor(comb[q], comb[q], table[:, 1], ALU.mult).then_inc(s_cw, 1)
                po.wait_ge(s_cw, p * 2 + 2)
                po.tensor_tensor(comb[q], comb[q], comb1, ALU.add).then_inc(s_cs, 1)

            po.tensor_copy(slot, cst[:, C_K:C_K + 1]).then_inc(s_slot, 1)
            po.wait_ge(s_tbA, 2)
            po.wait_ge(s_tbD, 2)
            combination(0, 0, True)
            po.wait_ge(s_cs, 1)
            combination(1, 1, True)
            for p in range(2, PAIRS):
                combination(p, p % 2)
            po.wait_ge(s_flag, 1)
            n_extra = po.value_load(extra[0:1, 0:1], min_val=0, max_val=EXTRA)
            for x in range(EXTRA // 2):
                with po.If(n_extra > 2 * x):
                    combination(PAIRS + x, x % 2)


def constants():
    import numpy as np
    c = np.zeros((P, C_ALL), np.float32)
    r = np.arange(P)
    c[:, C_ID:C_ID + P] = np.eye(P)
    tri = np.where(r[None, :] <= r[:, None], 0.0, NEG)
    c[:, C_TRI:C_TRI + P] = tri
    c[:, C_TRI + 256:C_TRI + 384] = tri
    b2, g, q = r // 64, (r % 64) // 32, r % 8
    c[:, C_R:C_R + P] = (b2[:, None] == b2) & (g[:, None] == g) & (q[:, None] == q)
    for i in range(4):
        tok = np.arange(NS)
        ok = (tok[None, :] // NQ == (2 * i + b2)[:, None]) & (tok[None, :] % NQ <= q[:, None])
        c[:, C_NEW + NS * i:C_NEW + NS * (i + 1)] = np.where(ok, 0.0, NEG)
    c[:, C_WIN:C_WIN + 8] = np.where(np.arange(8)[None, :] >= q[:, None], 0.0, NEG)
    for t in range(2):
        ok = (np.arange(NCMPP) * 16 + 31)[None, :] <= (r + P * t)[:, None]
        c[:, C_CADD + NCMPP * t:C_CADD + NCMPP * (t + 1)] = np.where(ok, 0.0, NEG)
        c[:, C_C01 + NCMPP * t:C_C01 + NCMPP * (t + 1)] = ok
    c[:, C_IDX:C_IDX + 16] = np.arange(1, 17)
    c[:, C_ONE:C_ONE + P] = 1.0
    c[(r // 64) * 64 + (r % 64 + 32) % 64, C_PERM + r] = 1.0
    pos = np.concatenate([np.arange(NP_), np.tile(1024 + np.arange(NQ), NB)]).astype(np.float32)
    inv = np.float32(10000.0) ** (-np.arange(32, dtype=np.float32) / np.float32(32))
    ang = (inv[r % 32][:, None] * pos[None, :]).astype(np.float32)
    c[:, C_COS:C_COS + N] = np.cos(ang)
    c[:, C_SIN:C_SIN + N] = np.sin(ang) * np.where(r % 64 < 32, -1.0, 1.0)[:, None]
    c[:, C_LT:C_LT + P] = r[:, None] < r[None, :]
    c[:, C_E:C_E + E] = CAP * np.arange(E)
    c[:, C_K] = r
    c[:, C_SEL:C_SEL + NC] = (r % 64)[:, None] == np.arange(NC)[None, :]
    return c


def kernel(**inputs):
    import numpy as np
    import concourse.bacc as _bacc
    from concourse.bass_utils import run_bass_kernel_spmd as _run

    a = {k: np.asarray(v) for k, v in inputs.items()}
    c_ = np.ascontiguousarray

    def kp(w):
        return w.reshape(-1, P, w.shape[-1]).transpose(1, 0, 2)

    cond = np.concatenate([a["c_prompt"], a["c_sample"]]).T
    xt = np.concatenate([a["x_prompt"].reshape(-1, D), a["x_sample"].reshape(-1, D)]).T
    w1 = [a["w_cmp_k1"][0], a["w_cmp_v1"][0]]
    vec = np.concatenate([
        a["b_ada"][0].reshape(48, P).T,
        np.stack([a["norm_mix_g"][0], a["norm_ffn_g"][0], a["norm_final_g"]]).reshape(3 * KD, P).T,
        a["w_cmp_k2"][0], a["w_cmp_v2"][0],
        a["pe_cmp_k"][0].reshape(16, P).T, a["pe_cmp_v"][0].reshape(16, P).T,
        kp(np.concatenate([a["w_router_grp"][0], a["w_router_exp"][0]], axis=1)).reshape(P, -1),
        kp(cond).reshape(P, -1)], axis=1)
    w = a["w_in"][0]
    q_b = w[:, 1536:2048].reshape(D, 2, 4, DH).transpose(0, 2, 1, 3).reshape(D, 512)
    gates = w[:, 2816:2840].reshape(D, H, 3)[:, :, [1, 2, 0]].reshape(D, GATES)
    turned = np.concatenate([w[:, 0:1024], q_b, w[:, 2048:2176], w[:, 2304:2432], w[:, 2560:2688],
                             w[:, 2176:2304], w[:, 2840:4888]], axis=1)
    rows = np.concatenate([w[:, 1024:1536], w[:, 2432:2560], w[:, 2688:2816], gates,
                           np.zeros((D, 232), w.dtype)], axis=1)
    w_in = kp(np.concatenate([turned, rows], axis=1)).reshape(P, KD, 10, 512).transpose(2, 0, 1, 3)

    def pages_t(x):
        x = x[0].reshape(NPHYS, PAGE, -1, P)
        return x.transpose(0, 3, 2, 1).reshape(NPHYS, P, -1)

    def pages_c(x):
        x = x[0].reshape(NPHYS, 8, 8, 2, 2, DH)
        return x.transpose(0, 3, 5, 2, 4, 1).reshape(NPHYS, P, P)

    ins = {
        "vec": vec, "x_t": kp(xt), "pages": a["page_table"].reshape(1, -1).astype(np.int32),
        "w_ada": kp(a["w_ada"][0]).reshape(P, KD, ADA_TILES, 512).transpose(2, 0, 1, 3),
        "w_in": w_in,
        "w1": np.stack([kp(x) for x in w1], axis=1),
        "cmp_pages": np.concatenate([pages_c(a["cache_nsa_cmp_k"]), pages_c(a["cache_nsa_cmp_v"])], axis=2),
        "k_pages": np.concatenate([pages_t(a["cache_moba_k"]), pages_t(a["cache_nsa_slc_k"])], axis=2),
        "v_pages": np.concatenate([a["cache_moba_v"][0].reshape(NPHYS, PAGE, 512),
                                   a["cache_nsa_slc_v"][0].reshape(NPHYS, PAGE, P)], axis=2),
        "win": np.stack([a["state_nsa_win_k"][0].reshape(NB, WIN, P).transpose(0, 2, 1),
                         a["state_nsa_win_v"][0].reshape(NB, 4, P, P).transpose(0, 2, 1, 3).reshape(NB, P, WIN)]),
        "w_br": kp(np.concatenate([a["w_br_a"][0],
                                   a["w_br_b"][0].reshape(2, 4, DH, D).transpose(1, 0, 2, 3).reshape(512, D)])),
        "w_out": kp(a["w_out"][0]),
        "w_ein": a["w_expert_in"][0].reshape(E, KD, P, 512).transpose(0, 2, 1, 3).reshape(E, P, -1),
        "w_eout": a["w_expert_out"][0].reshape(E, 2, P, D).transpose(0, 2, 1, 3).reshape(E, P, -1),
        "consts": constants(),
        "win_state": np.stack([a["state_nsa_win_k"][0].reshape(NB, WIN, P)[:, NQ:],
                               a["state_nsa_win_v"][0].reshape(NB, WIN, P)[:, NQ:]]).reshape(2, -1, 1008),
    }
    outs = {"y": (P, KD, N), "kt": (P, 4, N), "small": (P, 4, N), "va": (P, 3, 512), "vs": (P, 3, 256),
            "zero": (P, 256), "win_new": (2, 512, 1008)}
    nc = _bacc.Bacc("TRN2", target_bir_lowering=False, num_devices=1)
    args, arrays = [], {}
    for name, x in ins.items():
        arrays[f"in_{name}"] = c_(x)
        args.append(nc.dram_tensor(f"in_{name}", x.shape, mybir.dt.from_np(x.dtype), kind="ExternalInput").ap())
    for name, shape in outs.items():
        args.append(nc.dram_tensor(f"out_{name}", shape, F32, kind="ExternalOutput").ap())
    args.append(nc.dram_tensor("gates_scratch", (NS, GATES), F32, kind="Internal").ap())
    args.append(nc.dram_tensor("x_rows", ((E + EXTRA) * CAP, D), F32, kind="Internal").ap())
    build(nc, *args)
    got = _run(nc, [arrays], core_ids=[0]).results[0]
    y = got["out_y"].transpose(2, 1, 0).reshape(N, D)
    kt = got["out_kt"].transpose(2, 1, 0).reshape(N, 512)
    kc, ks, kw, vc = (got["out_small"][:, j, :].T for j in range(4))
    va = got["out_va"].transpose(1, 0, 2).reshape(3 * P, 512)[:N]
    vsw = got["out_vs"].transpose(1, 0, 2).reshape(3 * P, 256)[:N]
    vs, vw = vsw[:, 0:128], vsw[:, 128:256]
    zero = got["out_zero"].reshape(256, 128)
    old = got["out_win_new"].reshape(2, NB, WIN - NQ, P)

    def p_(x):
        return c_(x[:NP_].reshape(1, 1, NP_, -1, DH))

    def s_(x):
        return c_(x[NP_:].reshape(1, NB, NQ, -1, DH))

    def pw(x):
        return c_(np.concatenate([zero, x[:NP_]]).reshape(1, 1, WIN, 2, DH))

    def sw(j, x):
        return c_(np.concatenate([old[j], x[NP_:].reshape(NB, NQ, P)], axis=1).reshape(1, NB, WIN, 2, DH))

    return (c_(y[:NP_].reshape(1, NP_, D)), c_(y[NP_:].reshape(NB, NQ, D)),
            p_(kt), p_(va), p_(kc), p_(vc), p_(ks), p_(vs), pw(kw), pw(vw),
            s_(kt), s_(va), s_(kc), s_(vc), s_(ks), s_(vs), sw(0, kw), sw(1, vw))
```
